# Optimizing a Trainium2 kernel written in Bass

```python
import math
import jax, jax.numpy as jnp
from jax import lax
import numpy as np
import jax
import jax.numpy as jnp

D_MODEL = 1024
BATCH = 1
SEQ = 512
DEPTH = 2

HGRN_HEADS = 4
HGRN_DK = D_MODEL // (2 * HGRN_HEADS)
HGRN_DV = D_MODEL // (2 * HGRN_HEADS)
RET_HEADS = 4
RET_DK = D_MODEL // (2 * RET_HEADS)
RET_DV = D_MODEL // (2 * RET_HEADS)
LIN_CHUNK = 64
EVEN_COLS = [HGRN_HEADS * HGRN_DK, HGRN_HEADS * HGRN_DK, HGRN_HEADS * HGRN_DV, HGRN_HEADS * HGRN_DV,
             RET_HEADS * RET_DK, RET_HEADS * RET_DK, RET_HEADS * RET_DV, RET_HEADS * RET_DV]
EVEN_MIX_OUT = HGRN_HEADS * HGRN_DV + RET_HEADS * RET_DV

NSA_HD = 64
NSA_HEADS = D_MODEL // NSA_HD
NSA_KV_GROUPS = 2
CMP_BLOCK = 32
CMP_STRIDE = 16
SLC_BLOCK = 64
SLC_TOPN = 16
WINDOW = 512
Q_BLOCK = 128
KVW = NSA_KV_GROUPS * NSA_HD
ODD_COLS = [NSA_HEADS * NSA_HD, KVW, KVW, KVW, KVW, KVW, KVW, 3 * NSA_HEADS]

FFN_HIDDEN = ((8 * D_MODEL // 3 + 255) // 256) * 256
N_EVEN = (DEPTH + 1) // 2
N_ODD = DEPTH // 2
RMS_EPS = 1e-6
NEG_INF = -1e30
FORCE_SCORE = 1e9


def rmsnorm(x, g):
    xf = x.astype(jnp.float32)
    y = xf * lax.rsqrt(jnp.mean(xf * xf, axis=-1, keepdims=True) + RMS_EPS)
    return (y * g.astype(jnp.float32)).astype(x.dtype)

def split_cols(a, sizes):
    return jnp.split(a, np.cumsum(sizes)[:-1].tolist(), axis=-1)

def to_chunks(a, c):
    b, t, h, d = a.shape
    return a.reshape(b, t // c, c, h, d).transpose(1, 0, 3, 2, 4)

def from_chunks(a):
    n, b, h, c, d = a.shape
    return a.transpose(1, 0, 3, 2, 4).reshape(b, n * c, h, d)

def hgrn2_chunked(q, k, v, log_f):
    b_, t_, h_, dk = q.shape
    dv = v.shape[-1]
    c = LIN_CHUNK
    causal = jnp.tril(jnp.ones((c, c), dtype=bool))[:, :, None]

    def step(state, inp):
        qi, ki, vi, gi = inp
        cum = jnp.cumsum(gi, axis=2)
        diff = cum[:, :, :, None, :] - cum[:, :, None, :, :]
        decay = jnp.exp(jnp.where(causal, diff, NEG_INF))
        attn = jnp.einsum('bhid,bhjd,bhijd->bhij', qi, ki, decay)
        out = jnp.einsum('bhij,bhjv->bhiv', attn, vi) + jnp.einsum('bhid,bhdv->bhiv', qi * jnp.exp(cum), state)
        last = cum[:, :, -1:, :]
        state = jnp.exp(last[:, :, 0, :])[..., None] * state + jnp.einsum('bhjd,bhjv->bhdv', ki * jnp.exp(last - cum), vi)
        return state, out

    s0 = jnp.zeros((b_, h_, dk, dv), jnp.float32)
    xs = tuple(to_chunks(a.astype(jnp.float32), c) for a in (q, k, v, log_f))
    _, o = lax.scan(step, s0, xs)
    return from_chunks(o)

def retention_chunked(q, k, v, log_gamma):
    b_, t_, h_, dk = q.shape
    dv = v.shape[-1]
    c = LIN_CHUNK
    pos = jnp.arange(c, dtype=jnp.float32)
    rel = pos[:, None] - pos[None, :]
    decay = jnp.where(rel[None] >= 0, jnp.exp(jnp.maximum(rel, 0.0)[None] * log_gamma[:, None, None]), 0.0)
    q_decay = jnp.exp((pos + 1.0)[None, :] * log_gamma[:, None])[..., None]
    k_decay = jnp.exp((c - 1.0 - pos)[None, :] * log_gamma[:, None])[..., None]
    chunk_decay = jnp.exp(c * log_gamma)[:, None, None]

    def step(state, inp):
        qi, ki, vi = inp
        attn = jnp.einsum('bhid,bhjd->bhij', qi, ki) * decay
        out = jnp.einsum('bhij,bhjv->bhiv', attn, vi) + jnp.einsum('bhid,bhdv->bhiv', qi * q_decay, state)
        state = chunk_decay * state + jnp.einsum('bhjd,bhjv->bhdv', ki * k_decay, vi)
        return state, out

    s0 = jnp.zeros((b_, h_, dk, dv), jnp.float32)
    xs = tuple(to_chunks(a.astype(jnp.float32), c) for a in (q, k, v))
    _, o = lax.scan(step, s0, xs)
    return from_chunks(o)

def even_mixer(h, w_in, lower_bound, hgrn_norm, ret_norm, w_out):
    b_, t_, _ = h.shape
    hq, hf, hi, hg, rq, rk, rv, rg = split_cols(h @ w_in, EVEN_COLS)
    heads = lambda a, n: a.reshape(b_, t_, n, -1)
    f = lower_bound + (1.0 - lower_bound) * jax.nn.sigmoid(hf.astype(jnp.float32))
    o_h = hgrn2_chunked(heads(jax.nn.silu(hq), HGRN_HEADS), heads(1.0 - f, HGRN_HEADS),
                        heads(hi, HGRN_HEADS), heads(jnp.log(f), HGRN_HEADS))
    o_h = rmsnorm(o_h, hgrn_norm) * jax.nn.silu(heads(hg, HGRN_HEADS).astype(jnp.float32))
    log_gamma = jnp.log(1.0 - jnp.exp2(-5.0 - jnp.arange(RET_HEADS, dtype=jnp.float32)))
    o_r = retention_chunked(heads(rq, RET_HEADS), heads(rk, RET_HEADS) * (RET_DK ** -0.5),
                            heads(rv, RET_HEADS), log_gamma)
    o_r = rmsnorm(o_r, ret_norm) * jax.nn.silu(heads(rg, RET_HEADS).astype(jnp.float32))
    o = jnp.concatenate([o_h.reshape(b_, t_, -1), o_r.reshape(b_, t_, -1)], axis=-1)
    return o.astype(h.dtype) @ w_out

def alibi_slopes(n):
    return jnp.exp2(-8.0 * jnp.arange(1, n + 1, dtype=jnp.float32) / n)

def compress_blocks(k, pos_emb, w1, w2):
    b_, t_, g_, d = k.shape
    r = CMP_BLOCK // CMP_STRIDE
    ch = k.reshape(b_, t_ // CMP_STRIDE, CMP_STRIDE, g_, d)
    nc = t_ // CMP_STRIDE - r + 1
    blocks = jnp.concatenate([ch[:, j:j + nc] for j in range(r)], axis=2)
    blocks = blocks + pos_emb[None, None, :, None, :]
    flat = blocks.transpose(0, 1, 3, 2, 4).reshape(b_, nc, g_, CMP_BLOCK * d)
    return jax.nn.silu(flat @ w1) @ w2

def cmp_to_slc_overlap(nc, ns):
    c0 = jnp.arange(nc) * CMP_STRIDE
    s0 = jnp.arange(ns) * SLC_BLOCK
    lo = jnp.maximum(c0[:, None], s0[None, :])
    hi = jnp.minimum(c0[:, None] + CMP_BLOCK, s0[None, :] + SLC_BLOCK)
    return (jnp.maximum(hi - lo, 0) / CMP_BLOCK).astype(jnp.float32)

def odd_mixer(h, w_in, cmp_pos_k, cmp_pos_v, cmp_w1_k, cmp_w2_k, cmp_w1_v, cmp_w2_v, w_out):
    b_, t_, _ = h.shape
    H, G, d = NSA_HEADS, NSA_KV_GROUPS, NSA_HD
    R = H // G
    q, kc, vc, ks, vs, kw, vw, gl = split_cols(h @ w_in, ODD_COLS)
    q = q.reshape(b_, t_, H, d) * (d ** -0.5)
    kvh = lambda a: a.reshape(b_, t_, G, d)
    k_cmp = compress_blocks(kvh(kc), cmp_pos_k, cmp_w1_k, cmp_w2_k)
    v_cmp = compress_blocks(kvh(vc), cmp_pos_v, cmp_w1_v, cmp_w2_v)
    nc = k_cmp.shape[1]
    ns = t_ // SLC_BLOCK
    n_sel = min(SLC_TOPN, ns)
    overlap = cmp_to_slc_overlap(nc, ns)
    c_end = jnp.arange(nc) * CMP_STRIDE + CMP_BLOCK - 1
    k_sb = kvh(ks).reshape(b_, ns, SLC_BLOCK, G, d).transpose(0, 3, 1, 2, 4)
    v_sb = kvh(vs).reshape(b_, ns, SLC_BLOCK, G, d).transpose(0, 3, 1, 2, 4)
    kw_pad = jnp.pad(kvh(kw), ((0, 0), (WINDOW, 0), (0, 0), (0, 0)))
    vw_pad = jnp.pad(kvh(vw), ((0, 0), (WINDOW, 0), (0, 0), (0, 0)))
    slopes = alibi_slopes(H).reshape(G, R)
    gates = jax.nn.sigmoid(gl.astype(jnp.float32)).reshape(b_, t_, H, 3)
    gather = jax.vmap(jax.vmap(lambda tbl, ix: tbl[ix]))
    nq = t_ // Q_BLOCK
    f32 = jnp.float32

    def block(args):
        n, qb, gb = args
        qg = qb.reshape(b_, Q_BLOCK, G, R, d)
        t = n * Q_BLOCK + jnp.arange(Q_BLOCK)
        s_c = jnp.einsum('bqgrd,bcgd->bgrqc', qg, k_cmp, preferred_element_type=f32)
        dist_c = (t[:, None] - c_end[None, :]).astype(f32)
        valid_c = dist_c >= 0
        s_c = jnp.where(valid_c, s_c - slopes[None, :, :, None, None] * dist_c, NEG_INF)
        p_c = jax.nn.softmax(s_c, axis=-1) * valid_c
        o_c = jnp.einsum('bgrqc,bcgd->bqgrd', p_c, v_cmp.astype(f32))
        p_slc = jnp.einsum('bgrqc,cj->bgqj', p_c, overlap)
        qblk = t // SLC_BLOCK
        js = jnp.arange(ns)
        forced = (js[None, :] == 0) | (js[None, :] == qblk[:, None]) | (js[None, :] == qblk[:, None] - 1)
        allowed = js[None, :] <= qblk[:, None]
        score = jnp.where(forced, FORCE_SCORE, jnp.where(allowed, p_slc, NEG_INF))
        _, idx = lax.top_k(score, n_sel)
        kg = gather(k_sb, idx)
        vg = gather(v_sb, idx)
        s_s = jnp.einsum('bqgrd,bgqnld->bgrqnl', qg, kg, preferred_element_type=f32)
        spos = idx[..., None] * SLC_BLOCK + jnp.arange(SLC_BLOCK)
        dist_s = (t[None, None, :, None, None] - spos).astype(f32)[:, :, None]
        s_s = jnp.where(dist_s >= 0, s_s - slopes[None, :, :, None, None, None] * dist_s, NEG_INF)
        p_s = jax.nn.softmax(s_s.reshape(b_, G, R, Q_BLOCK, -1), axis=-1).reshape(s_s.shape)
        o_s = jnp.einsum('bgrqnl,bgqnld->bqgrd', p_s, vg.astype(f32))
        kwb = lax.dynamic_slice_in_dim(kw_pad, n * Q_BLOCK, WINDOW + Q_BLOCK, axis=1)
        vwb = lax.dynamic_slice_in_dim(vw_pad, n * Q_BLOCK, WINDOW + Q_BLOCK, axis=1)
        wpos = n * Q_BLOCK - WINDOW + jnp.arange(WINDOW + Q_BLOCK)
        dist_w = t[:, None] - wpos[None, :]
        valid_w = (dist_w >= 0) & (dist_w < WINDOW) & (wpos[None, :] >= 0)
        s_w = jnp.einsum('bqgrd,bkgd->bgrqk', qg, kwb, preferred_element_type=f32)
        s_w = jnp.where(valid_w, s_w - slopes[None, :, :, None, None] * dist_w.astype(f32), NEG_INF)
        p_w = jax.nn.softmax(s_w, axis=-1)
        o_w = jnp.einsum('bgrqk,bkgd->bqgrd', p_w, vwb.astype(f32))
        g5 = gb.reshape(b_, Q_BLOCK, G, R, 3)
        o = g5[..., 0:1] * o_c + g5[..., 1:2] * o_s + g5[..., 2:3] * o_w
        return o.reshape(b_, Q_BLOCK, H * d)

    qblocks = q.reshape(b_, nq, Q_BLOCK, H, d).transpose(1, 0, 2, 3, 4)
    gblocks = gates.reshape(b_, nq, Q_BLOCK, H, 3).transpose(1, 0, 2, 3, 4)
    out = lax.map(block, (jnp.arange(nq), qblocks, gblocks))
    out = out.transpose(1, 0, 2, 3).reshape(b_, t_, H * d)
    return out.astype(h.dtype) @ w_out

def swiglu(h, w_gate_up, w_down):
    g, u = jnp.split(h @ w_gate_up, 2, axis=-1)
    return (jax.nn.silu(g) * u) @ w_down

def first_inputs(seed: int = 0) -> dict:
    key = jax.random.key(seed)
    ks = jax.random.split(key, 20)
    f32 = jnp.float32
    w = lambda k, shape, fan_in: jax.random.normal(k, shape, f32) * (fan_in ** -0.5)
    gain = lambda k, shape: 1.0 + 0.02 * jax.random.normal(k, shape, f32)
    even_in = sum(EVEN_COLS)
    odd_in = sum(ODD_COLS)
    return {
        'x': jax.random.normal(ks[0], (BATCH, SEQ, D_MODEL), f32),
        'mix_norm': gain(ks[1], (DEPTH, D_MODEL)),
        'ffn_norm': gain(ks[2], (DEPTH, D_MODEL)),
        'final_norm': gain(ks[3], (D_MODEL,)),
        'even_w_in': w(ks[4], (N_EVEN, D_MODEL, even_in), D_MODEL),
        'hgrn_lower_bounds': 0.1 * jax.random.normal(ks[5], (N_EVEN + 1, HGRN_HEADS * HGRN_DK), f32),
        'hgrn_out_norm': gain(ks[6], (N_EVEN, HGRN_DV)),
        'ret_out_norm': gain(ks[7], (N_EVEN, RET_DV)),
        'even_w_out': w(ks[8], (N_EVEN, EVEN_MIX_OUT, D_MODEL), EVEN_MIX_OUT),
        'odd_w_in': w(ks[9], (N_ODD, D_MODEL, odd_in), D_MODEL),
        'cmp_pos_k': 0.1 * jax.random.normal(ks[10], (N_ODD, CMP_BLOCK, NSA_HD), f32),
        'cmp_pos_v': 0.1 * jax.random.normal(ks[11], (N_ODD, CMP_BLOCK, NSA_HD), f32),
        'cmp_w1_k': w(ks[12], (N_ODD, CMP_BLOCK * NSA_HD, NSA_HD), CMP_BLOCK * NSA_HD),
        'cmp_w2_k': w(ks[13], (N_ODD, NSA_HD, NSA_HD), NSA_HD),
        'cmp_w1_v': w(ks[14], (N_ODD, CMP_BLOCK * NSA_HD, NSA_HD), CMP_BLOCK * NSA_HD),
        'cmp_w2_v': w(ks[15], (N_ODD, NSA_HD, NSA_HD), NSA_HD),
        'odd_w_out': w(ks[16], (N_ODD, NSA_HEADS * NSA_HD, D_MODEL), NSA_HEADS * NSA_HD),
        'ffn_w_gate_up': w(ks[17], (DEPTH, D_MODEL, 2 * FFN_HIDDEN), D_MODEL),
        'ffn_w_down': w(ks[18], (DEPTH, FFN_HIDDEN, D_MODEL), FFN_HIDDEN),
    }

def first_block(x, mix_norm, ffn_norm, final_norm, even_w_in, hgrn_lower_bounds, hgrn_out_norm,
              ret_out_norm, even_w_out, odd_w_in, cmp_pos_k, cmp_pos_v, cmp_w1_k, cmp_w2_k,
              cmp_w1_v, cmp_w2_v, odd_w_out, ffn_w_gate_up, ffn_w_down):
    lb_all = jnp.cumsum(jax.nn.softmax(hgrn_lower_bounds.astype(jnp.float32), axis=0), axis=0)
    h = x
    for layer in range(DEPTH):
        hn = rmsnorm(h, mix_norm[layer])
        if layer % 2 == 0:
            e = layer // 2
            h = h + even_mixer(hn, even_w_in[e], lb_all[e], hgrn_out_norm[e], ret_out_norm[e], even_w_out[e])
        else:
            o = layer // 2
            h = h + odd_mixer(hn, odd_w_in[o], cmp_pos_k[o], cmp_pos_v[o], cmp_w1_k[o], cmp_w2_k[o],
                              cmp_w1_v[o], cmp_w2_v[o], odd_w_out[o])
        h = h + swiglu(rmsnorm(h, ffn_norm[layer]), ffn_w_gate_up[layer], ffn_w_down[layer])
    return rmsnorm(h, final_norm)


N_MIXERS = 4
NORM_EPS = 1e-6
ROPE_THETA = 10000.0
HEAD_DIM = 64
NEG_INF_2 = -1e30

POOL_WINDOWS = (2, 4, 8, 16)
POOL_GROUP = D_MODEL // len(POOL_WINDOWS)

DIFF_HEADS = D_MODEL // (2 * HEAD_DIM)
DIFF_SUBLN_EPS = 1e-5

LRU_WIDTH = D_MODEL
LRU_BLOCKS = D_MODEL // HEAD_DIM
LRU_BLOCK_DIM = LRU_WIDTH // LRU_BLOCKS
LRU_CONV = 4
LRU_C = 8.0

DIL_GROUPS = ((128, 1), (512, 4), (2048, 16))
DIL_HEADS = D_MODEL // HEAD_DIM
DIL_WIDTH = DIL_HEADS * HEAD_DIM

D_FF = 2816
FFN_CONV = 3


def _n_layers_of(mixer):
    return len(range(mixer, DEPTH, N_MIXERS))

def _rms_norm(x, gain, eps=NORM_EPS):
    xf = x.astype(jnp.float32)
    y = xf * lax.rsqrt(jnp.mean(xf * xf, axis=-1, keepdims=True) + eps)
    return (y * gain.astype(jnp.float32)).astype(x.dtype)

def _rope_tables(positions, head_dim):
    inv = ROPE_THETA ** (-jnp.arange(0, head_dim, 2, dtype=jnp.float32) / head_dim)
    ang = positions.astype(jnp.float32)[:, None] * inv[None, :]
    return jnp.cos(ang), jnp.sin(ang)

def _rope(x, cos, sin):
    shape = (cos.shape[0],) + (1,) * (x.ndim - 3) + (cos.shape[1],)
    c, s = cos.reshape(shape), sin.reshape(shape)
    xf = x.astype(jnp.float32)
    x1, x2 = jnp.split(xf, 2, axis=-1)
    return jnp.concatenate([x1 * c - x2 * s, x2 * c + x1 * s], axis=-1).astype(x.dtype)

def _pool_mixer(x, w, scale):
    b, s, d = x.shape
    xf = x.astype(jnp.float32)
    cs = jnp.concatenate([jnp.zeros((b, 1, d), jnp.float32), lax.cumsum(xf, axis=1)], axis=1)
    t = jnp.arange(s)
    parts = []
    for g, win in enumerate(POOL_WINDOWS):
        lo = jnp.clip(t - win // 2, 0, s)
        hi = jnp.clip(t + win - win // 2, 0, s)
        sl = slice(g * POOL_GROUP, (g + 1) * POOL_GROUP)
        csg = cs[:, :, sl]
        mean = (csg[:, hi] - csg[:, lo]) / (hi - lo).astype(jnp.float32)[:, None]
        parts.append(mean - xf[:, :, sl])
    pooled = jnp.stack(parts, axis=2).astype(x.dtype)
    y = jnp.einsum('bsgc,gce->bsge', pooled, w).reshape(b, s, d)
    return y * scale

def _diff_attention(x, w_qkv, lq1, lk1, lq2, lk2, subln, w_o, cos, sin, layer_idx):
    b, s, _ = x.shape
    h, dh = DIFF_HEADS, HEAD_DIM
    q, k, v = jnp.split(x @ w_qkv, 3, axis=-1)
    q = _rope(q.reshape(b, s, 2 * h, dh), cos, sin).reshape(b, s, h, 2, dh) * (dh ** -0.5)
    k = _rope(k.reshape(b, s, 2 * h, dh), cos, sin).reshape(b, s, h, 2, dh)
    v = v.reshape(b, s, h, 2 * dh)
    lam_init = 0.8 - 0.6 * math.exp(-0.3 * layer_idx)
    lam = (jnp.exp(jnp.sum(lq1.astype(jnp.float32) * lk1.astype(jnp.float32)))
           - jnp.exp(jnp.sum(lq2.astype(jnp.float32) * lk2.astype(jnp.float32))) + lam_init)
    nb = s // Q_BLOCK
    q_blocks = q.reshape(b, nb, Q_BLOCK, h, 2, dh).swapaxes(0, 1)

    def one_block(qb):
        sc = jnp.einsum('bqhce,bkhce->bhcqk', qb, k).astype(jnp.float32)
        p = jax.nn.softmax(sc, axis=-1)
        a = p[:, :, 0] - lam * p[:, :, 1]
        return jnp.einsum('bhqk,bkhe->bqhe', a.astype(v.dtype), v)

    o = lax.map(one_block, q_blocks).swapaxes(0, 1).reshape(b, s, h, 2 * dh)
    o = _rms_norm(o, subln, DIFF_SUBLN_EPS) * (1.0 - lam_init)
    return o.reshape(b, s, h * 2 * dh) @ w_o

def _causal_conv(x, w, bias):
    kw = w.shape[0]
    s = x.shape[1]
    xp = jnp.pad(x, ((0, 0), (kw - 1, 0), (0, 0)))
    y = bias
    for j in range(kw):
        y = y + w[j] * xp[:, j:j + s]
    return y

def _rg_lru_direction(u, conv_w, conv_b, w_a, b_a, w_x, b_x, lam):
    b, s, c = u.shape
    xc = _causal_conv(u, conv_w, conv_b)
    xb = xc.reshape(b, s, LRU_BLOCKS, LRU_BLOCK_DIM)
    r = jax.nn.sigmoid((jnp.einsum('bsni,nij->bsnj', xb, w_a).reshape(b, s, c) + b_a).astype(jnp.float32))
    i = jax.nn.sigmoid((jnp.einsum('bsni,nij->bsnj', xb, w_x).reshape(b, s, c) + b_x).astype(jnp.float32))
    log_a = LRU_C * r * jax.nn.log_sigmoid(lam.astype(jnp.float32))
    a = jnp.exp(log_a)
    inp = jnp.sqrt(-jnp.expm1(2.0 * log_a)) * (i * xc.astype(jnp.float32))

    def combine(left, right):
        a_l, b_l = left
        a_r, b_r = right
        return a_l * a_r, a_r * b_l + b_r

    _, h = lax.associative_scan(combine, (a, inp), axis=1)
    return h

def _rglru_mixer(x, w_in, conv_w, conv_b, w_a, b_a, w_x, b_x, lam, w_out):
    gate, u = jnp.split(x @ w_in, 2, axis=-1)
    h_fwd = _rg_lru_direction(u, conv_w[0], conv_b[0], w_a[0], b_a[0], w_x[0], b_x[0], lam[0])
    h_bwd = jnp.flip(_rg_lru_direction(jnp.flip(u, axis=1), conv_w[1], conv_b[1], w_a[1], b_a[1],
                                       w_x[1], b_x[1], lam[1]), axis=1)
    y = jax.nn.gelu(gate.astype(jnp.float32), approximate=True) * (h_fwd + h_bwd)
    return y.astype(x.dtype) @ w_out

def _dilated_chain_attention(q, k, v, dilation, half):
    b, s, h, dh = q.shape
    n = s // dilation
    blk = half
    nb = -(-n // blk)
    pad = nb * blk - n

    def chains(t):
        return t.reshape(b, n, dilation, h, dh).transpose(0, 2, 3, 1, 4)

    qc = jnp.pad(chains(q), ((0, 0), (0, 0), (0, 0), (0, pad), (0, 0))).reshape(b, dilation, h, nb, blk, dh)

    def windows(t):
        tp = jnp.pad(chains(t), ((0, 0), (0, 0), (0, 0), (blk, blk + pad), (0, 0)))
        tp = tp.reshape(b, dilation, h, nb + 2, blk, dh)
        return jnp.concatenate([tp[:, :, :, :-2], tp[:, :, :, 1:-1], tp[:, :, :, 2:]], axis=4)

    kw, vw = windows(k), windows(v)
    qpos = jnp.arange(nb * blk).reshape(nb, blk)
    kpos = jnp.arange(nb)[:, None] * blk + jnp.arange(-blk, 2 * blk)[None, :]
    rel = kpos[:, None, :] - qpos[:, :, None]
    valid = (jnp.abs(rel) <= half) & (kpos[:, None, :] >= 0) & (kpos[:, None, :] < n)
    sc = jnp.einsum('bdhnqe,bdhnke->bdhnqk', qc, kw).astype(jnp.float32)
    sc = jnp.where(valid, sc, NEG_INF_2)
    lse = jax.nn.logsumexp(sc, axis=-1)
    p = jnp.exp(sc - lse[..., None])
    o = jnp.einsum('bdhnqk,bdhnke->bdhnqe', p.astype(v.dtype), vw)

    def unchain(t):
        t = t.reshape((b, dilation, h, nb * blk) + t.shape[5:])[:, :, :, :n]
        t = jnp.moveaxis(t, 3, 1)
        return t.reshape((b, s, h) + t.shape[4:])

    return unchain(o), unchain(lse)

def _dilated_mixer(x, w_qkv, w_o, cos, sin):
    b, s, _ = x.shape
    n_groups = len(DIL_GROUPS)
    qkv = (x @ w_qkv).reshape(b, s, n_groups, 3, DIL_HEADS, HEAD_DIM)
    q = _rope(qkv[:, :, :, 0], cos, sin) * (HEAD_DIM ** -0.5)
    k = _rope(qkv[:, :, :, 1], cos, sin)
    v = qkv[:, :, :, 2]
    outs, lses = [], []
    for g, (window, dilation) in enumerate(DIL_GROUPS):
        o, l = _dilated_chain_attention(q[:, :, g], k[:, :, g], v[:, :, g], dilation, window // (2 * dilation))
        outs.append(o.astype(jnp.float32))
        lses.append(l)
    wts = jax.nn.softmax(jnp.stack(lses, axis=0), axis=0)
    o = jnp.sum(wts[..., None] * jnp.stack(outs, axis=0), axis=0)
    return o.astype(x.dtype).reshape(b, s, DIL_WIDTH) @ w_o

def _conv_ffn(x, w_up, conv_w, conv_b, w_down):
    s = x.shape[1]
    g, u = jnp.split(x @ w_up, 2, axis=-1)
    half = FFN_CONV // 2
    gp = jnp.pad(g, ((0, 0), (half, half), (0, 0)))
    gc = conv_b
    for j in range(FFN_CONV):
        gc = gc + conv_w[j] * gp[:, j:j + s]
    act = jax.nn.gelu(gc.astype(jnp.float32), approximate=False).astype(x.dtype)
    return (act * u) @ w_down

def second_inputs(seed: int = 0) -> dict:
    key = jax.random.key(seed)
    keys = iter(jax.random.split(key, 48))
    f32 = jnp.float32
    n_a, n_b, n_c, n_d = (_n_layers_of(m) for m in range(N_MIXERS))

    def dense(shape, fan_in):
        return jax.random.normal(next(keys), shape, f32) * fan_in ** -0.5

    def gain(shape):
        return 1.0 + 0.05 * jax.random.normal(next(keys), shape, f32)

    def small(shape, scale=0.02):
        return scale * jax.random.normal(next(keys), shape, f32)

    x = jax.random.normal(next(keys), (BATCH, SEQ, D_MODEL), f32)
    a_c = jax.random.uniform(next(keys), (n_c, 2, LRU_WIDTH), f32, 0.9, 0.999)
    base = a_c ** (1.0 / LRU_C)
    lru_lambda = jnp.log(base) - jnp.log1p(-base)
    return {
        "x": x,
        "positions": jnp.arange(SEQ, dtype=jnp.int32),
        "mix_norm": gain((DEPTH, D_MODEL)),
        "pool_w": dense((n_a, len(POOL_WINDOWS), POOL_GROUP, POOL_GROUP), POOL_GROUP),
        "pool_scale": gain((n_a, D_MODEL)),
        "diff_w_qkv": dense((n_b, D_MODEL, 3 * D_MODEL), D_MODEL),
        "diff_lam_q1": small((n_b, HEAD_DIM), 0.1),
        "diff_lam_k1": small((n_b, HEAD_DIM), 0.1),
        "diff_lam_q2": small((n_b, HEAD_DIM), 0.1),
        "diff_lam_k2": small((n_b, HEAD_DIM), 0.1),
        "diff_subln": gain((n_b, 2 * HEAD_DIM)),
        "diff_w_o": dense((n_b, D_MODEL, D_MODEL), D_MODEL),
        "lru_w_in": dense((n_c, D_MODEL, 2 * LRU_WIDTH), D_MODEL),
        "lru_conv_w": dense((n_c, 2, LRU_CONV, LRU_WIDTH), LRU_CONV),
        "lru_conv_b": small((n_c, 2, LRU_WIDTH)),
        "lru_w_a": dense((n_c, 2, LRU_BLOCKS, LRU_BLOCK_DIM, LRU_BLOCK_DIM), LRU_BLOCK_DIM),
        "lru_b_a": small((n_c, 2, LRU_WIDTH)),
        "lru_w_x": dense((n_c, 2, LRU_BLOCKS, LRU_BLOCK_DIM, LRU_BLOCK_DIM), LRU_BLOCK_DIM),
        "lru_b_x": small((n_c, 2, LRU_WIDTH)),
        "lru_lambda": lru_lambda,
        "lru_w_out": dense((n_c, LRU_WIDTH, D_MODEL), LRU_WIDTH),
        "dil_w_qkv": dense((n_d, D_MODEL, len(DIL_GROUPS) * 3 * DIL_WIDTH), D_MODEL),
        "dil_w_o": dense((n_d, DIL_WIDTH, D_MODEL), DIL_WIDTH),
        "ffn_norm": gain((DEPTH, D_MODEL)),
        "ffn_w_up": dense((DEPTH, D_MODEL, 2 * D_FF), D_MODEL),
        "ffn_conv_w": dense((DEPTH, FFN_CONV, D_FF), FFN_CONV),
        "ffn_conv_b": small((DEPTH, D_FF)),
        "ffn_w_down": dense((DEPTH, D_FF, D_MODEL), D_FF),
        "final_norm": gain((D_MODEL,)),
    }

def second_block(x, positions, mix_norm, pool_w, pool_scale, diff_w_qkv, diff_lam_q1, diff_lam_k1,
              diff_lam_q2, diff_lam_k2, diff_subln, diff_w_o, lru_w_in, lru_conv_w, lru_conv_b,
              lru_w_a, lru_b_a, lru_w_x, lru_b_x, lru_lambda, lru_w_out, dil_w_qkv, dil_w_o,
              ffn_norm, ffn_w_up, ffn_conv_w, ffn_conv_b, ffn_w_down, final_norm):
    cos, sin = _rope_tables(positions, HEAD_DIM)
    h = x
    for i in range(DEPTH):
        m, j = i % N_MIXERS, i // N_MIXERS
        hn = _rms_norm(h, mix_norm[i])
        if m == 0:
            y = _pool_mixer(hn, pool_w[j], pool_scale[j])
        elif m == 1:
            y = _diff_attention(hn, diff_w_qkv[j], diff_lam_q1[j], diff_lam_k1[j], diff_lam_q2[j],
                                diff_lam_k2[j], diff_subln[j], diff_w_o[j], cos, sin, i)
        elif m == 2:
            y = _rglru_mixer(hn, lru_w_in[j], lru_conv_w[j], lru_conv_b[j], lru_w_a[j], lru_b_a[j],
                             lru_w_x[j], lru_b_x[j], lru_lambda[j], lru_w_out[j])
        else:
            y = _dilated_mixer(hn, dil_w_qkv[j], dil_w_o[j], cos, sin)
        h = h + y
        h = h + _conv_ffn(_rms_norm(h, ffn_norm[i]), ffn_w_up[i], ffn_conv_w[i], ffn_conv_b[i], ffn_w_down[i])
    return _rms_norm(h, final_norm)


def setup_inputs(seed=0):
    out = dict(first_inputs(seed))
    for name, value in second_inputs(seed + 1).items():
        if name != "x":
            out[name + "_2"] = value
    return out


def reference(
    x, mix_norm, ffn_norm, final_norm, even_w_in, hgrn_lower_bounds, hgrn_out_norm,
    ret_out_norm, even_w_out, odd_w_in, cmp_pos_k, cmp_pos_v, cmp_w1_k, cmp_w2_k, cmp_w1_v,
    cmp_w2_v, odd_w_out, ffn_w_gate_up, ffn_w_down, positions_2, mix_norm_2, pool_w_2,
    pool_scale_2, diff_w_qkv_2, diff_lam_q1_2, diff_lam_k1_2, diff_lam_q2_2, diff_lam_k2_2,
    diff_subln_2, diff_w_o_2, lru_w_in_2, lru_conv_w_2, lru_conv_b_2, lru_w_a_2, lru_b_a_2,
    lru_w_x_2, lru_b_x_2, lru_lambda_2, lru_w_out_2, dil_w_qkv_2, dil_w_o_2, ffn_norm_2,
    ffn_w_up_2, ffn_conv_w_2, ffn_conv_b_2, ffn_w_down_2, final_norm_2,
):
    x = first_block(
        x, mix_norm, ffn_norm, final_norm, even_w_in, hgrn_lower_bounds, hgrn_out_norm,
        ret_out_norm, even_w_out, odd_w_in, cmp_pos_k, cmp_pos_v, cmp_w1_k, cmp_w2_k, cmp_w1_v,
        cmp_w2_v, odd_w_out, ffn_w_gate_up, ffn_w_down,
    )
    return second_block(
        x, positions_2, mix_norm_2, pool_w_2, pool_scale_2, diff_w_qkv_2, diff_lam_q1_2,
        diff_lam_k1_2, diff_lam_q2_2, diff_lam_k2_2, diff_subln_2, diff_w_o_2, lru_w_in_2,
        lru_conv_w_2, lru_conv_b_2, lru_w_a_2, lru_b_a_2, lru_w_x_2, lru_b_x_2, lru_lambda_2,
        lru_w_out_2, dil_w_qkv_2, dil_w_o_2, ffn_norm_2, ffn_w_up_2, ffn_conv_w_2, ffn_conv_b_2,
        ffn_w_down_2, final_norm_2,
    )


_drawn_inputs = setup_inputs


def setup_inputs(seed=0):
    import zlib

    import numpy as np

    out = dict(_drawn_inputs(seed))
    spreads = {}
    factors = {'hgrn_lower_bounds': 7.261,
     'hgrn_out_norm': 13.168,
     'ret_out_norm': 13.128,
     'cmp_pos_k': 200.0,
     'diff_lam_q1_2': 2.668,
     'ffn_conv_b_2': 4.298,
     'ffn_norm': 4.937,
     'cmp_w2_k': 14.661,
     'cmp_pos_v': 8.0,
     'cmp_w1_k': 5.088,
     'cmp_w1_v': 2.783}
    for name, (base, spread) in spreads.items():
        noise = np.random.default_rng([zlib.crc32(name.encode()), seed]).standard_normal(out[name].shape)
        drawn = base * np.exp(spread * noise) if base else spread * noise
        out[name] = jnp.asarray(drawn.astype(out[name].dtype))
    for name, factor in factors.items():
        out[name] = (out[name] * factor).astype(out[name].dtype)
    return out
```

```python
from contextlib import ExitStack
import math

import numpy as np
import concourse.bass as bass
from concourse import mybir

F32 = mybir.dt.float32
F32R = mybir.dt.float32r
I32 = mybir.dt.int32
ACT = mybir.ActivationFunctionType
ALU = mybir.AluOpType
AX = mybir.AxisListType

P = 128
T = 512
D = 1024
KT = D // P
TT = T // P
UNIT = 1024
RAW_SLOTS = 3
SPLIT_SLOTS = 3
RING_BANKS = 6

EPS = 1e-6
SUBLN_EPS = 1e-5
HG_HEADS = 4
CHUNK = 128
NSA_HEADS, NSA_HD, GROUPS = 16, 64, 2
KVW = GROUPS * NSA_HD
CMP_BLOCK, CMP_STRIDE = 32, 16
NC = T // CMP_STRIDE - CMP_BLOCK // CMP_STRIDE + 1
NCP = 32
MASKED = 1e30
ODD_KC, ODD_VC, ODD_KS, ODD_VS, ODD_KW, ODD_VW, ODD_GATES = (D + KVW * i for i in range(7))
ODD_VALUES = ((ODD_VS, KVW), (ODD_VW, KVW + 3 * NSA_HEADS))
ODD_VALUE_COLUMNS = 2 * KVW + 3 * NSA_HEADS
FFN1, FFN2 = 2816, 2816
HT = FFN1 // P
POOL_WINDOWS = (2, 4, 8, 16)
DIFF_HEADS = 8
LAM_INIT = 0.8 - 0.6 * math.exp(-0.3 * 1)
ROPE_THETA = 10000.0

STAGES = ("even", "ffn_a", "odd", "ffn_b", "between", "pool", "ffn_c", "diff", "ffn_d")
NORM_OF = {"even": 0, "ffn_a": 1, "odd": 2, "ffn_b": 3, "pool": 4, "ffn_c": 5, "diff": 6, "ffn_d": 7, "between": 8, "final": 9}


def feature_units(matrix, layer, column, k_tiles):
    return [(matrix, layer, k, min(UNIT // P, k_tiles - k), column, P) for k in range(0, k_tiles, UNIT // P)]


def token_units(matrix, layer, column, columns, k_tiles):
    return [(matrix, layer, k, 2, column, columns) for k in range(0, k_tiles, 2)]


def stage_units(stage):
    units = []
    if stage == "even":
        hq, hf, hi, hg, rq, rk, rv, rg = (512 * i for i in range(8))
        for base in (hf, hq, hg, rg, rq, rk):
            for h in range(HG_HEADS):
                units += feature_units("even_w_in", 0, base + P * h, KT)
        units += token_units("even_w_in", 0, hi, 512, KT) + token_units("even_w_in", 0, rv, 512, KT)
        for n in range(KT):
            units += feature_units("even_w_out", 0, P * n, KT)
    if stage == "odd":
        for col in (ODD_KC, ODD_VC, ODD_KS, ODD_KW):
            units += feature_units("odd_w_in", 0, col, KT)
        units += token_units("odd_w_in", 0, ODD_VALUES, ODD_VALUE_COLUMNS, KT)
        for n in range(KT):
            units += feature_units("odd_w_in", 0, P * n, KT)
        for n in range(KT):
            units += feature_units("odd_w_out", 0, P * n, KT)
    if stage in ("ffn_a", "ffn_b", "ffn_c", "ffn_d"):
        up, down = ("ffn_w_gate_up", "ffn_w_down") if stage in ("ffn_a", "ffn_b") else ("ffn_w_up_2", "ffn_w_down_2")
        layer = 0 if stage in ("ffn_a", "ffn_c") else 1
        for j in range(HT):
            units += feature_units(up, layer, P * j, KT) + feature_units(up, layer, FFN1 + P * j, KT)
        for n in range(KT):
            units += feature_units(down, layer, P * n, HT)
    if stage == "pool":
        for g in range(len(POOL_WINDOWS)):
            units += [("pool_w_2", g, 0, 2, 0, 256)]
    if stage == "diff":
        for col in range(0, 2 * D, P):
            units += feature_units("diff_w_qkv_2", 0, col, KT)
        for half in range(2):
            units += token_units("diff_w_qkv_2", 0, 2 * D + 512 * half, 512, KT)
        for n in range(KT):
            units += feature_units("diff_w_o_2", 0, P * n, KT)
    return units


class Lane:
    def __init__(self, sem):
        self.sem, self.count, self.queue, self.reached = sem, 0, [], {}

    def wait(self, *marks):
        for mark in marks:
            if mark is None:
                continue
            if isinstance(mark, list):
                self.wait(*mark)
                continue
            sem, value = mark
            if value > self.reached.get(sem.name, 0):
                self.reached[sem.name] = value
                self.queue.append(lambda e, s=sem, v=value: e.wait_ge(s, v))

    def put(self, emit):
        self.queue.append(emit)

    def do(self, emit, *after):
        self.wait(*after)
        self.count += 1
        self.queue.append(lambda e: emit(e).then_inc(self.sem, 1))
        return self.mark()

    def do_all(self, emits, *after):
        self.wait(*after)
        for emit in emits[:-1]:
            self.put(emit)
        return self.do(emits[-1])

    def mark(self):
        return (self.sem, self.count) if self.count else None

    def run(self, engine):
        for emit in self.queue:
            emit(engine)


class Transfers:
    def __init__(self, sem):
        self.sem, self.count = sem, 0

    def start(self, lane, dst, src, *after):
        lane.wait(*after)
        self.count += 16
        lane.put(lambda e: e.dma_start(dst, src).then_inc(self.sem, 16))
        return (self.sem, self.count)


class Program:

    def __init__(self, nc, ctx, dram, units):
        self.nc, self.ctx, self.dram, self.units = nc, ctx, dram, units
        self.pe, self.dve, self.act, self.pool, self.sp = (
            Lane(self.sem(f"{n}_done")) for n in ("pe", "dve", "act", "pool", "sp"))
        self.bank = [ctx.enter_context(nc.psum_tensor(f"bank{i}", [P, 512], F32)) for i in range(8)]
        self.bank_free = [None] * 8
        self.ring_at = 0
        self.residual = self.tile("residual", [P, KT, T], F32)
        self.residual_ready = [None] * KT
        self.norm_gain = self.tile("norm_gain", [P, 10, KT], F32)
        self.ident = self.tile("ident", [P, P], F32)
        self.ones = self.tile("ones", [P, 1], F32)
        self.square = self.tile("square", [P, 2, T], F32)
        self.square_free = [None, None]
        self.normed = self.tile("normed", [P, 2, T], F32)
        self.normed_free = [None, None]
        self.rms = self.tile("rms", [P, 3, TT], F32)
        self.constants = Transfers(self.sem("constants_loaded"))
        self.raw = self.tile("weight_raw", [P, RAW_SLOTS, UNIT], F32)
        self.w_hi = [self.tile(f"weight_hi{i}", [P, UNIT], F32R) for i in range(SPLIT_SLOTS)]
        self.w_lo = [self.tile(f"weight_lo{i}", [P, UNIT], F32R) for i in range(SPLIT_SLOTS)]
        self.raw_loads = [Transfers(self.sem(f"weights_loaded{i}")) for i in range(RAW_SLOTS)]
        self.loaded, self.is_split, self.used = {}, {}, {}
        self.unit_at = 0

    def sem(self, name):
        return self.ctx.enter_context(self.nc.semaphore(name))

    def tile(self, name, shape, dtype, scope=None):
        return (scope or self.ctx).enter_context(self.nc.sbuf_tensor(name, shape, dtype))

    def load(self, name, lane, moves, *after):
        transfers = Transfers(self.sem(name + "_loaded"))
        for dst, src in moves:
            mark = transfers.start(lane, dst, src, *after)
        return mark

    def fence(self):
        return [lane.mark() for lane in (self.pe, self.dve, self.act, self.pool)]

    def take_bank(self):
        i = self.ring_at
        self.ring_at = (i + 1) % RING_BANKS
        return i

    def load_unit(self, u):
        if u >= len(self.units):
            return
        _, _, _, k, _, c = self.units[u]
        slot = u % RAW_SLOTS
        self.loaded[u] = self.raw_loads[slot].start(
            self.sp, self.raw[:, slot, 0:k * c], self.dram["weights"][u, :, 0:k * c], self.is_split.get(u - RAW_SLOTS))

    def split_unit(self, u):
        if u >= len(self.units):
            return
        _, _, _, k, _, c = self.units[u]
        raw, hi, lo = self.raw[:, u % RAW_SLOTS, 0:k * c], self.w_hi[u % SPLIT_SLOTS], self.w_lo[u % SPLIT_SLOTS]
        high = self.act.do(lambda e: e.activation(hi[:, 0:k * c], raw, ACT.Copy), self.loaded[u], self.used.get(u - SPLIT_SLOTS))
        self.is_split[u] = self.dve.do(
            lambda e: e.tensor_tensor(lo[:, 0:k * c], raw, hi[:, 0:k * c].bitcast(F32), ALU.subtract), high)
        self.load_unit(u + RAW_SLOTS)

    def take_unit(self, matrix, column):
        u = self.unit_at
        self.unit_at += 1
        assert self.units[u][0] == matrix and self.units[u][4] == column, (self.units[u], matrix, column)
        if u + SPLIT_SLOTS - 1 not in self.is_split:
            self.split_unit(u + SPLIT_SLOTS - 1)
        _, _, _, k, _, c = self.units[u]
        view = lambda t: t[:, 0:k * c].rearrange("p (k c) -> p k c", k=k)
        return u, view(self.w_hi[u % SPLIT_SLOTS]), view(self.w_lo[u % SPLIT_SLOTS])

    def start_weights(self):
        for u in range(RAW_SLOTS):
            self.load_unit(u)
        for u in range(SPLIT_SLOTS - 1):
            self.split_unit(u)

    def project_features(self, matrix, column, k_tiles, x_hi, x_lo, x_ready):
        b = self.take_bank()
        out = self.bank[b]
        self.pe.wait(self.bank_free[b])
        k0 = 0
        while k0 < k_tiles:
            u, w_hi, w_lo = self.take_unit(matrix, column)
            self.pe.wait(self.is_split[u])
            n = self.units[u][3]
            for k in range(n):
                self.pe.wait(x_ready[k0 + k])
                for i, (w, x) in enumerate(((w_hi, x_hi), (w_hi, x_lo), (w_lo, x_hi))):
                    emit = lambda e, w=w, x=x, k=k, kk=k0 + k, i=i: e.matmul(
                        out[:, :], w[:, k, :], x[:, kk, :], start=(kk == 0 and i == 0), stop=(kk == k_tiles - 1 and i == 2))
                    if k == n - 1 and i == 2:
                        self.used[u] = self.pe.do(emit)
                    else:
                        self.pe.put(emit)
            k0 += n
        return b, self.used[u]

    def project_tokens(self, matrix, column, columns, x_hi, x_lo, x_ready):
        banks = [self.take_bank() for _ in range(TT)]
        self.pe.wait(*[self.bank_free[b] for b in banks])
        for k0 in range(0, KT, 2):
            u, w_hi, w_lo = self.take_unit(matrix, column)
            self.pe.wait(self.is_split[u], x_ready[k0], x_ready[k0 + 1])
            for t in range(TT):
                for k in range(2):
                    for i, (w, x) in enumerate(((w_hi, x_hi), (w_lo, x_hi), (w_hi, x_lo))):
                        emit = lambda e, w=w, x=x, k=k, kk=k0 + k, i=i, t=t: e.matmul(
                            self.bank[banks[t]][:, 0:columns], x[:, kk, P * t:P * (t + 1)], w[:, k, :],
                            start=(kk == 0 and i == 0), stop=(kk == KT - 1 and i == 2))
                        last = k == 1 and i == 2 and t == TT - 1
                        if last:
                            self.used[u] = self.pe.do(emit)
                        else:
                            self.pe.put(emit)
        return banks, self.used[u]

    def add_square(self, k):
        s = k % 2
        squared = self.act.do(lambda e: e.activation(self.square[:, s, :], self.residual[:, k, :], ACT.Square),
                              self.residual_ready[k], self.square_free[s])
        if k == 0:
            self.pe.wait(self.bank_free[7], self.const_ready)
        self.pe.wait(squared)
        for t in range(TT):
            emit = lambda e, t=t: e.matmul(self.bank[7][:, t:t + 1], self.square[:, s, P * t:P * (t + 1)], self.ones[:, :],
                                           start=(k == 0 and t == 0), stop=(k == KT - 1), skip_group_check=True)
            if t < TT - 1:
                self.pe.put(emit)
            else:
                self.square_free[s] = self.pe.do(emit)
        return self.square_free[s]

    def token_scales(self, sums, n, count, eps, done, out, tmp, tmp2, free=None):
        mean = self.dve.do(lambda e: e.tensor_scalar(tmp, sums, 1.0 / count, eps, ALU.mult, ALU.add), done, free)
        root = self.act.do(lambda e: e.activation(tmp2, tmp, ACT.Sqrt), mean)
        return mean, self.dve.do(lambda e: e.reciprocal(out, tmp2), root)

    def spread_scales(self, column, bank, ready):
        self.pe.wait(self.bank_free[bank], ready, self.const_ready)
        for t in range(TT):
            emit = lambda e, t=t: e.matmul(self.bank[bank][:, P * t:P * (t + 1)], column(t).broadcast_to([P, P]),
                                           self.ident[:, :], start=True, stop=True)
            if t < TT - 1:
                self.pe.put(emit)
            else:
                return self.pe.do(emit)

    def norm_scales(self):
        sums = self.square_free[(KT - 1) % 2]
        read, ready = self.token_scales(self.bank[7][:, 0:TT], TT, D, EPS, sums, self.rms[:, 2, :], self.rms[:, 0, :], self.rms[:, 1, :])
        self.bank_free[7] = read
        return self.spread_scales(lambda t: self.rms[:, 2, t:t + 1], 6, ready)

    def split_into(self, x, hi, lo, ready, *free):
        high = self.act.do(lambda e: e.activation(hi, x, ACT.Copy), ready, *free)
        return self.dve.do(lambda e: e.tensor_tensor(lo, x, hi.bitcast(F32), ALU.subtract), high)

    def normalise(self, stage, x_hi, x_lo, free):
        scales = self.norm_scales()
        row, ready = NORM_OF[stage], []
        for k in range(KT):
            s = k % 2
            x = self.normed[:, s, :]
            full = self.dve.do(lambda e, x=x, k=k: e.scalar_tensor_tensor(
                x, self.residual[:, k, :], self.norm_gain[:, row, k:k + 1], self.bank[6][:, :], ALU.mult, ALU.mult),
                scales, self.const_ready, self.normed_free[s])
            low = self.split_into(x, x_hi[:, k, :], x_lo[:, k, :], full, free)
            self.normed_free[s] = low
            ready.append(low)
        self.bank_free[6] = full
        return ready

    def add_to_residual(self, matrix, k_tiles, x_hi, x_lo, x_ready):
        for n in range(KT):
            b, done = self.project_features(matrix, P * n, k_tiles, x_hi, x_lo, x_ready)
            self.residual_ready[n] = self.dve.do(
                lambda e, n=n, b=b: e.tensor_tensor(self.residual[:, n, :], self.residual[:, n, :], self.bank[b][:, :], ALU.add), done)
            self.bank_free[b] = self.residual_ready[n]
            if n:
                self.add_square(n - 1)
        self.add_square(KT - 1)


def feed_forward(g, stage):
    swiglu = stage in ("ffn_a", "ffn_b")
    layer = 0 if stage in ("ffn_a", "ffn_c") else 1
    up, down = ("ffn_w_gate_up", "ffn_w_down") if swiglu else ("ffn_w_up_2", "ffn_w_down_2")
    with ExitStack() as scope:
        free = g.fence()
        h_hi = g.tile(f"{stage}_h_hi", [P, HT, T], F32R, scope)
        h_lo = g.tile(f"{stage}_h_lo", [P, HT, T], F32R, scope)
        gate = g.tile(f"{stage}_gate", [P, 2, T], F32, scope)
        hidden = g.tile(f"{stage}_hidden", [P, 2, T], F32, scope)
        x_hi = g.tile(f"{stage}_x_hi", [P, KT, T], F32R, scope)
        x_lo = g.tile(f"{stage}_x_lo", [P, KT, T], F32R, scope)
        x_ready = g.normalise(stage, x_hi, x_lo, free)
        gate_free, hidden_free, h_ready = [None, None], [None, None], []
        for j in range(HT):
            s = j % 2
            bg, gate_done = g.project_features(up, P * j, KT, x_hi, x_lo, x_ready)
            bu, up_done = g.project_features(up, FFN1 + P * j, KT, x_hi, x_lo, x_ready)
            acc, u, gt, hd = g.bank[bg], g.bank[bu], gate[:, s, :], hidden[:, s, :]
            if swiglu:
                opened = g.act.do(lambda e, gt=gt, acc=acc: e.activation(gt, acc[:, :], ACT.Silu), gate_done, gate_free[s], free)
                g.bank_free[bg] = opened
            else:
                w = lambda tap, j=j: g.conv_w[:, 3 * layer + tap, j:j + 1]
                mid = g.dve.do(lambda e, gt=gt, acc=acc, w=w, j=j: e.tensor_scalar(
                    gt, acc[:, :], w(1), g.conv_b[:, layer, j:j + 1], ALU.mult, ALU.add), gate_done, gate_free[s], g.const_ready, free)
                left = g.dve.do(lambda e, gt=gt, acc=acc, w=w: e.scalar_tensor_tensor(
                    gt[:, 1:T], acc[:, 0:T - 1], w(0), gt[:, 1:T], ALU.mult, ALU.add), mid)
                right = g.dve.do(lambda e, gt=gt, acc=acc, w=w: e.scalar_tensor_tensor(
                    gt[:, 0:T - 1], acc[:, 1:T], w(2), gt[:, 0:T - 1], ALU.mult, ALU.add), left)
                g.bank_free[bg] = right
                opened = g.act.do(lambda e, gt=gt: e.activation(gt, gt, ACT.Gelu), right)
            product = g.dve.do(lambda e, gt=gt, hd=hd, u=u: e.tensor_tensor(hd, gt, u[:, :], ALU.mult),
                               opened, up_done, hidden_free[s], free)
            gate_free[s] = g.bank_free[bu] = product
            hidden_free[s] = g.split_into(hd, h_hi[:, j, :], h_lo[:, j, :], product)
            h_ready.append(hidden_free[s])
        g.add_to_residual(down, HT, h_hi, h_lo, h_ready)


def hgrn_levels(g, q, k, cum, diff, k_dec, q_dec, scores, level_mask, mask_loaded, ready):
    blocks = HG_HEADS * TT
    pairs = lambda t, s: t.rearrange("p (n z s) -> p n z s", z=2, s=s)
    half = blocks // 2
    for part in range(2):
        emits = []
        for m in range(half):
            c = slice(P * (half * part + m), P * (half * part + m + 1))
            out = g.bank[6 + m // 4][:, P * (m % 4):P * (m % 4 + 1)]
            emits.append(lambda e, out=out, c=c: e.matmul(out, k[:, c], q[:, c], start=True, stop=True))
        mm = g.pe.do_all(emits, g.bank_free[6], g.bank_free[7], ready)
        for b in range(2):
            c = slice(P * (half * part + 4 * b), P * (half * part + 4 * b + 4))
            at_level = g.dve.do(lambda e, b=b, c=c: e.tensor_tensor(
                scores[:, c].rearrange("p (m i) -> p m i", m=4), g.bank[6 + b][:, :].rearrange("p (m i) -> p m i", m=4),
                g.ident[:, :].unsqueeze(1).broadcast_to([P, 4, P]), ALU.mult), mm, g.const_ready)
            g.bank_free[6 + b] = at_level
        yield
    k_free = q_free = diff_free = None
    chosen = at_level

    def one_level(level, s):
        nonlocal k_free, q_free, diff_free, chosen
        n = blocks * P // (2 * s)
        c4, d4, kd4, q4, k4 = (pairs(t[:, :], s) for t in (cum, diff, k_dec, q, k))
        mid = c4[:, :, 0, s - 1:s]
        rel = g.dve.do(lambda e: e.tensor_tensor(
            diff[:, :].rearrange("p (n t) -> p n t", n=n), cum[:, :].rearrange("p (n t) -> p n t", n=n),
            mid.broadcast_to([P, n, 2 * s]), ALU.subtract), ready, diff_free)
        first = g.act.do(lambda e: e.activation(d4[:, :, 0, :], d4[:, :, 0, :], ACT.Exp, scale=-1.0), rel)
        second = g.act.do(lambda e: e.activation(d4[:, :, 1, :], d4[:, :, 1, :], ACT.Exp), rel)
        k_ready = g.pool.do(lambda e: e.tensor_tensor(kd4[:, :, 0, :], k4[:, :, 0, :], d4[:, :, 0, :], ALU.mult), first, k_free, ready)
        q_ready = g.dve.do(lambda e: e.tensor_tensor(
            q_dec[:, :].rearrange("p (n s) -> p n s", s=s), q4[:, :, 1, :], d4[:, :, 1, :], ALU.mult), second, q_free)
        diff_free = [k_ready, q_ready]
        emits = []
        for m in range(blocks):
            out = g.bank[6 + m // 8][:, 64 * (m % 8):64 * (m % 8 + 1)]
            emits.append(lambda e, out=out, m=m: e.matmul(
                out, k_dec[:, P * m:P * (m + 1)], q_dec[:, 64 * m:64 * (m + 1)], start=True, stop=True))
        k_free = q_free = mm = g.pe.do_all(emits, k_ready, q_ready, g.bank_free[6], g.bank_free[7])
        mask = level_mask[:, level, :].rearrange("p (n s) -> p n s", s=s).unsqueeze(1).broadcast_to([P, 8, 64 // s, s])
        for b in range(2):
            rows = slice(P * 8 * b, P * 8 * (b + 1))
            chosen = g.dve.do(lambda e, b=b, rows=rows: e.copy_predicated(
                scores[:, rows].rearrange("p (m n z s) -> p m n z s", m=8, z=2, s=s)[:, :, :, 1, :], mask,
                g.bank[6 + b][:, :].rearrange("p (m n s) -> p m n s", m=8, s=s)), mm, mask_loaded, chosen)
            g.bank_free[6 + b] = chosen
        g.scores_ready = chosen

    for level, s in enumerate((64, 32, 16, 8, 4, 2, 1)):
        one_level(level, s)
        yield


def even_mixer(g):
    mul, add, sub = ALU.mult, ALU.add, ALU.subtract
    width = HG_HEADS * T
    outer = ExitStack()
    free = g.fence()
    hg_gate = g.tile("hgrn_gate", [P, HG_HEADS, T], F32, outer)
    ret_gate = g.tile("ret_gate", [P, HG_HEADS, T], F32, outer)
    inner = ExitStack()
    names = ("hgrn_q", "hgrn_k", "hgrn_cum", "ret_q", "ret_k", "hgrn_v", "ret_v", "hgrn_scores", "hgrn_diff", "hgrn_k_dec")
    hq, hk, cum, rq, rk, hv, rv, scores, diff, k_dec = (g.tile(n, [P, width], F32, inner) for n in names)
    q_dec = g.tile("hgrn_q_dec", [P, width // 2], F32, inner)
    bound = g.tile("hgrn_bound", [P, 6, HG_HEADS], F32, inner)
    xs = ExitStack()
    x_hi = g.tile("even_x_hi", [P, KT, T], F32R, xs)
    x_lo = g.tile("even_x_lo", [P, KT, T], F32R, xs)
    level_mask = g.tile("hgrn_level_mask", [P, 7, 64], I32, xs)
    mask_loaded = g.load("hgrn_level_mask", g.pool, [(level_mask[:, :, :], g.dram["level_mask"])], free)

    b0, b1 = g.lower_bounds[:, 0, :], g.lower_bounds[:, 1, :]
    top, e0, e1, total, low, rest = (bound[:, i, :] for i in range(6))
    m = g.dve.do(lambda e: e.tensor_tensor(top, b0, b1, ALU.max), g.const_ready, free)
    m = g.dve.do(lambda e: e.tensor_tensor(e0, b0, top, sub), m)
    m = g.dve.do(lambda e: e.tensor_tensor(e1, b1, top, sub), m)
    m = g.act.do(lambda e: e.activation(bound[:, 1:3, :], bound[:, 1:3, :], ACT.Exp), m)
    m = g.dve.do(lambda e: e.tensor_tensor(total, e0, e1, add), m)
    m = g.dve.do(lambda e: e.reciprocal(total, total), m)
    m = g.dve.do(lambda e: e.tensor_tensor(low, e0, total, mul), m)
    bound_ready = g.dve.do(lambda e: e.tensor_scalar(rest, low, -1.0, 1.0, mul, add), m)

    x_ready = g.normalise("even", x_hi, x_lo, free)
    project = lambda base, h: g.project_features("even_w_in", 512 * base + P * h, KT, x_hi, x_lo, x_ready)
    part = lambda t, h: t[:, T * h:T * (h + 1)]

    for h in range(HG_HEADS):
        b, done = project(1, h)
        g.bank_free[b] = m = g.act.do(lambda e, h=h, b=b: e.activation(part(cum, h), g.bank[b][:, :], ACT.Sigmoid), done, free)
        m = g.dve.do(lambda e, h=h: e.tensor_scalar(part(cum, h), part(cum, h), rest[:, h:h + 1], low[:, h:h + 1], mul, add), m, bound_ready)
        f_ready = g.dve.do(lambda e, h=h: e.tensor_scalar(part(hk, h), part(cum, h), -1.0, 1.0, mul, add), m, free)
    for base, dst in ((0, hq), (3, hg_gate), (7, ret_gate)):
        for h in range(HG_HEADS):
            b, done = project(base, h)
            out = part(dst, h) if base == 0 else dst[:, h, :]
            g.bank_free[b] = m = g.act.do(lambda e, out=out, b=b: e.activation(out, g.bank[b][:, :], ACT.Silu), done, free)
            if base == 0:
                q_ready = m
    gates_ready = m
    logged = g.act.do(lambda e: e.activation(cum[:, :], cum[:, :], ACT.Ln), f_ready)
    m = g.pool.do(lambda e: e.memset(k_dec[:, :], 1.0), free)
    m = g.pool.do(lambda e: e.memset(k_dec[:, :].rearrange("p (m t) -> p m t", t=CHUNK)[:, :, 0:1], 0.0), m)
    summed = g.dve.do(lambda e: e.tensor_tensor_scan(diff[:, :], k_dec[:, :], cum[:, :], 0.0, mul, add), m, logged, free)
    summed = g.dve.do(lambda e: e.tensor_copy(cum[:, :], diff[:, :]), summed)
    cleared = g.pool.do(lambda e: e.memset(k_dec[:, :], 0.0), summed)

    levels = hgrn_levels(g, hq, hk, cum, diff, k_dec, q_dec, scores, level_mask, mask_loaded, [summed, cleared, q_ready, f_ready])
    for base, dst in ((4, rq), (5, rk)):
        for h in range(HG_HEADS):
            b, done = project(base, h)
            g.bank_free[b] = ret_qk_ready = g.act.do(lambda e, dst=dst, h=h, b=b: e.activation(part(dst, h), g.bank[b][:, :], ACT.Copy), done, free)
            next(levels, None)
    for base, dst in ((2, hv), (6, rv)):
        banks, done = g.project_tokens("even_w_in", 512 * base, 512, x_hi, x_lo, x_ready)
        for t in range(TT):
            g.bank_free[banks[t]] = v_ready = g.act.do(
                lambda e, dst=dst, t=t, b=banks[t]: e.activation(part(dst, t), g.bank[b][:, :], ACT.Copy), done, free)
    for _ in levels:
        pass
    xs.close()

    late = ExitStack()
    free = g.fence()
    cross = g.tile("hgrn_cross", [P, HG_HEADS, 6, P], F32, late)
    k_end = g.tile("hgrn_k_end", [P, width], F32, late)
    k_far = g.tile("hgrn_k_far", [P, HG_HEADS, 3, P], F32, late)
    across = g.tile("hgrn_across", [P, HG_HEADS, TT], F32, late)
    decay = g.tile("ret_decay", [P, HG_HEADS, T], F32, late)
    ret_scores = g.tile("ret_scores", [P, 2, 1280], F32, late)
    decay_loaded = g.load("ret_decay", g.pool, [(decay[:, :, :], g.dram["ret_decay"])], free)
    tiles = lambda t: t.rearrange("p (m t) -> p m t", t=P)
    heads = lambda t: t.rearrange("p (h m t) -> p h m t", h=HG_HEADS, t=P)
    ends = tiles(cum[:, :])[:, :, P - 1:P]
    m = g.act.do(lambda e: e.activation(diff[:, :], cum[:, :], ACT.Exp), free)
    q_start = g.dve.do(lambda e: e.tensor_tensor(k_dec[:, :], hq[:, :], diff[:, :], mul), m, free)
    m = g.dve.do(lambda e: e.tensor_tensor(tiles(diff[:, :]), tiles(cum[:, :]), ends.broadcast_to([P, HG_HEADS * TT, P]), sub), q_start)
    m = g.act.do(lambda e: e.activation(diff[:, :], diff[:, :], ACT.Exp, scale=-1.0), m)
    kend = g.dve.do(lambda e: e.tensor_tensor(k_end[:, :], hk[:, :], diff[:, :], mul), m)
    whole = g.act.do(lambda e: e.activation(across[:, :, :].rearrange("p h m -> p (h m)"), ends.rearrange("p m o -> p (m o)"), ACT.Exp), free)
    far = lambda i: k_far[:, :, i, :]
    one = lambda m: across[:, :, m:m + 1].broadcast_to([P, HG_HEADS, P])
    m = g.dve.do(lambda e: e.tensor_tensor(far(0), heads(k_end[:, :])[:, :, 0, :], one(1), mul), kend, whole)
    g.dve.do(lambda e: e.tensor_tensor(far(1), heads(k_end[:, :])[:, :, 1, :], one(2), mul), kend)
    kfar = g.dve.do(lambda e: e.tensor_tensor(far(2), far(0), one(2), mul), m)
    PAIRS = ((0, 1), (1, 2), (2, 3), (0, 2), (1, 3), (0, 3))
    for h in range(HG_HEADS):
        banks = [g.take_bank(), g.take_bank()]
        emits = []
        for i, (kj, qi) in enumerate(PAIRS):
            lhs = k_end[:, T * h + P * kj:T * h + P * (kj + 1)] if i < 3 else k_far[:, h, i - 3, :]
            emits.append(lambda e, i=i, lhs=lhs, qi=qi, h=h, banks=banks: e.matmul(
                g.bank[banks[i // 3]][:, P * (i % 3):P * (i % 3 + 1)], lhs, k_dec[:, T * h + P * qi:T * h + P * (qi + 1)], start=True, stop=True))
        mm = g.pe.do_all(emits, q_start, kend, kfar, *[g.bank_free[b] for b in banks])
        for i in range(2):
            g.bank_free[banks[i]] = cross_ready = g.act.do(lambda e, i=i, h=h, b=banks[i]: e.activation(
                cross[:, h, 3 * i:3 * i + 3, :].rearrange("p m t -> p (m t)"), g.bank[b][:, 0:3 * P], ACT.Copy), mm, free)

    def finish_head(bank, done, gate, h, gain, head):
        s = head % 2
        sq = g.act.do(lambda e: e.activation(g.square[:, s, :], g.bank[bank][:, :], ACT.Square), done, g.square_free[s])
        out = g.dve.do(lambda e: e.scalar_tensor_tensor(gate[:, h, :], g.bank[bank][:, :], gain, gate[:, h, :], mul, mul), sq, gates_ready, g.const_ready)
        g.bank_free[bank] = [sq, out]
        return sq, out

    def sum_squares(sq, head):
        s = head % 2
        if head == 0:
            g.pe.wait(g.bank_free[7])
        emits = []
        for t in range(TT):
            col = TT * head + t
            emits.append(lambda e, t=t, col=col: e.matmul(g.bank[7][:, col:col + 1], g.square[:, s, P * t:P * (t + 1)], g.ones[:, :],
                                                          start=(col == 0), stop=True, skip_group_check=True))
        g.square_free[s] = g.pe.do_all(emits, sq)
        return g.square_free[s]

    outs = []
    pending = None
    for h in range(HG_HEADS):
        b = g.take_bank()
        emits = []
        for i in range(TT):
            out = g.bank[b][:, P * i:P * (i + 1)]
            for j in range(i + 1):
                rhs = scores[:, T * h + P * i:T * h + P * (i + 1)] if j == i else cross[:, h, PAIRS.index((j, i)), :]
                emits.append(lambda e, out=out, j=j, rhs=rhs, i=i, h=h: e.matmul(
                    out, hv[:, T * j + P * h:T * j + P * (h + 1)], rhs, start=(j == 0), stop=(j == i)))
        mm = g.pe.do_all(emits, g.bank_free[b], v_ready, cross_ready, g.scores_ready)
        if pending:
            sum_squares(*pending)
        sq, out = finish_head(b, mm, hg_gate, h, g.hgrn_gain[:, :], h)
        outs.append(out)
        pending = (sq, h)
    spans = [(j, T - P * j) for j in range(TT)]
    offset = [0, 512, 896, 1152]
    ret_free = [None, None]

    def ret_score(h):
        s = h % 2
        for j, n in spans:
            b = g.take_bank()
            g.pe.wait(g.bank_free[b], ret_qk_ready)
            mm = g.pe.do(lambda e, b=b, j=j, n=n: e.matmul(
                g.bank[b][:, 0:n], rk[:, T * h + P * j:T * h + P * (j + 1)], rq[:, T * h + P * j:T * (h + 1)], start=True, stop=True))
            g.bank_free[b] = m = g.dve.do(lambda e, b=b, j=j, n=n, s=s: e.tensor_tensor(
                ret_scores[:, s, offset[j]:offset[j] + n], g.bank[b][:, 0:n], decay[:, h, 0:n], mul), mm, decay_loaded, ret_free[s], free)
        return m

    made = ret_score(0)
    for h in range(HG_HEADS):
        ready, s = made, h % 2
        if h + 1 < HG_HEADS:
            made = ret_score(h + 1)
        b = g.take_bank()
        emits = []
        for j, n in spans:
            emits.append(lambda e, b=b, j=j, n=n, s=s, h=h: e.matmul(
                g.bank[b][:, P * j:T], rv[:, T * j + P * h:T * j + P * (h + 1)], ret_scores[:, s, offset[j]:offset[j] + n],
                start=(j == 0), stop=(j == TT - 1)))
        mm = g.pe.do_all(emits, g.bank_free[b], v_ready, ready)
        ret_free[s] = mm
        sum_squares(*pending)
        sq, out = finish_head(b, mm, ret_gate, h, g.ret_gain[:, :], HG_HEADS + h)
        outs.append(out)
        pending = (sq, HG_HEADS + h)
    sums = sum_squares(*pending)
    n = 2 * HG_HEADS * TT
    head_rms = g.head_rms
    g.bank_free[7], ready = g.token_scales(g.bank[7][:, 0:n], n, P, EPS, sums, head_rms[:, 2, :], head_rms[:, 0, :], head_rms[:, 1, :])
    late.close()
    inner.close()
    free = g.fence()
    o_hi = g.tile("even_o_hi", [P, KT, T], F32R, outer)
    o_lo = g.tile("even_o_lo", [P, KT, T], F32R, outer)
    o_ready = []
    for head in range(KT):
        gate, h = (hg_gate, head) if head < HG_HEADS else (ret_gate, head - HG_HEADS)
        b = g.take_bank()
        spread = g.spread_scales(lambda t, head=head: head_rms[:, 2, TT * head + t:TT * head + t + 1], b, ready)
        x = gate[:, h, :]
        g.bank_free[b] = full = g.dve.do(lambda e, x=x, b=b: e.tensor_tensor(x, x, g.bank[b][:, :], mul), spread, outs[head])
        o_ready.append(g.split_into(x, o_hi[:, head, :], o_lo[:, head, :], full, free))
    g.add_to_residual("even_w_out", KT, o_hi, o_lo, o_ready)
    outer.close()


def pool_mixer(g):
    with ExitStack() as scope:
        free = g.fence()
        PAD = max(POOL_WINDOWS)
        W = T + 2 * PAD
        x_hi = g.tile("pool_x_hi", [P, KT, T], F32R, scope)
        x_lo = g.tile("pool_x_lo", [P, KT, T], F32R, scope)
        padded = g.tile("pool_padded", [P, KT, W], F32, scope)
        sums = g.tile("pool_sums", [P, 2, W], F32, scope)
        pooled = g.tile("pool_pooled", [P, 2, T], F32, scope)
        share = g.tile("pool_share", [P, len(POOL_WINDOWS), T], F32, scope)
        share_loaded = g.load("pool_share", g.pool, [(share[:, :, :], g.dram["pool_share"])], free)
        zeroed = g.pool.do(lambda e: e.memset(padded[:, :, :], 0.0), free)
        scales = g.norm_scales()
        x_ready, sums_free, pooled_free = [], [None, None], [None, None]
        for k in range(KT):
            s, window = k % 2, POOL_WINDOWS[k // 2]
            x = padded[:, k, PAD:PAD + T]
            full = g.dve.do(lambda e, x=x, k=k: e.scalar_tensor_tensor(
                x, g.residual[:, k, :], g.norm_gain[:, NORM_OF["pool"], k:k + 1], g.bank[6][:, :], ALU.mult, ALU.mult),
                scales, g.const_ready, zeroed)
            g.bank_free[6] = full
            src, done = padded[:, k, :], full
            lo, hi = 1, W
            span, which = 2, 0
            back, ahead = 1, 0
            m = full
            while True:
                dst = sums[:, which, :]
                m = g.pool.do(lambda e, dst=dst, src=src, lo=lo, hi=hi, back=back, ahead=ahead: e.tensor_tensor(
                    dst[:, lo:hi], src[:, lo - back:hi - back], src[:, lo + ahead:hi + ahead], ALU.add), m, sums_free[0], free)
                if span == window:
                    break
                src = dst
                back = ahead = span // 2
                lo, hi = lo + back, hi - ahead
                span *= 2
                which = 1 - which
            out = pooled[:, s, :]
            m = g.dve.do(lambda e, out=out, dst=dst, k=k: e.tensor_tensor(out, dst[:, PAD:PAD + T], share[:, k // 2, :], ALU.mult),
                         m, share_loaded, pooled_free[s])
            sums_free = [m]
            m = g.dve.do(lambda e, out=out, x=x: e.tensor_tensor(out, out, x, ALU.subtract), m)
            pooled_free[s] = g.split_into(out, x_hi[:, k, :], x_lo[:, k, :], m, free)
            x_ready.append(pooled_free[s])
        for group in range(len(POOL_WINDOWS)):
            u, w_hi, w_lo = g.take_unit("pool_w_2", 0)
            for half in range(2):
                b, n = g.take_bank(), 2 * group + half
                c = slice(P * half, P * (half + 1))
                emits = []
                for k in range(2):
                    for i, (w, x) in enumerate(((w_hi, x_hi), (w_hi, x_lo), (w_lo, x_hi))):
                        emits.append(lambda e, b=b, w=w, x=x, k=k, i=i, c=c, group=group: e.matmul(
                            g.bank[b][:, :], w[:, k, c], x[:, 2 * group + k, :], start=(k == 0 and i == 0), stop=(k == 1 and i == 2)))
                mm = g.pe.do_all(emits, g.is_split[u], g.bank_free[b], x_ready[2 * group], x_ready[2 * group + 1])
                g.residual_ready[n] = g.bank_free[b] = g.dve.do(lambda e, n=n, b=b: e.scalar_tensor_tensor(
                    g.residual[:, n, :], g.bank[b][:, :], g.pool_scale[:, n:n + 1], g.residual[:, n, :], ALU.mult, ALU.add), mm)
                if n:
                    g.add_square(n - 1)
            g.used[u] = mm
        g.add_square(KT - 1)


def transpose_tiles(g, src, n_tiles, bank, ready):
    emits = [lambda e, j=j: e.transpose(g.bank[bank][:, P * j:P * (j + 1)], src[:, P * j:P * (j + 1)], g.ident[:, :]) for j in range(n_tiles)]
    return g.pe.do_all(emits, ready, g.bank_free[bank], g.const_ready)


def to_features(g, out, hi, lo, ready, free, gain=None):
    marks = []
    for k in range(KT):
        b, s = g.take_bank(), k % 2
        emits = [lambda e, t=t, k=k, b=b: e.transpose(g.bank[b][:, P * t:P * (t + 1)], out(t, k), g.ident[:, :]) for t in range(TT)]
        mm = g.pe.do_all(emits, ready, g.bank_free[b])
        x = g.normed[:, s, :]
        if gain is None:
            g.bank_free[b] = full = g.act.do(lambda e, x=x, b=b: e.activation(x, g.bank[b][:, :], ACT.Copy), mm, g.normed_free[s])
        else:
            g.bank_free[b] = full = g.act.do(lambda e, x=x, b=b: e.activation(x, g.bank[b][:, :], ACT.Copy, scale=gain), mm, g.normed_free[s])
        g.normed_free[s] = g.split_into(x, hi[:, k, :], lo[:, k, :], full, free)
        marks.append(g.normed_free[s])
    return marks


def odd_mixer(g):
    mul, add, sub = ALU.mult, ALU.add, ALU.subtract
    g.stat_free = g.out_ready = None
    g.cmp_free, g.turn_free, g.prob_free, g.part_free, g.low_free = [None] * 2, [None] * 3, [None] * 3, [None] * 2, {}
    R = NSA_HEADS // GROUPS
    outer = ExitStack()
    free = g.fence()
    out = g.tile("nsa_out", [P, TT, NSA_HEADS * NSA_HD], F32, outer)
    inner = ExitStack()
    q = g.tile("nsa_q", [P, KT, T], F32, inner)
    v = g.tile("nsa_v", [P, TT, 2 * KVW], F32, inner)
    gates = g.tile("nsa_gates", [P, TT, 3 * NSA_HEADS], F32, inner)
    kdup = [g.tile(f"nsa_k{i}", [P, GROUPS, T], F32, inner) for i in range(2)]
    kcmp = g.tile("nsa_k_cmp", [P, GROUPS, 2, NCP], F32, inner)
    vcmp = g.tile("nsa_v_cmp", [P, GROUPS, 4, NSA_HD], F32, inner)
    stats = g.tile("nsa_stats", [P, 6, NSA_HEADS], F32, inner)
    bias_c = g.tile("nsa_bias_cmp", [P, TT, NSA_HEADS, NCP], F32, inner)
    valid_c = g.tile("nsa_valid_cmp", [P, TT, NCP], F32, inner)
    cmp_bias_loaded = g.load("cmp_bias", g.pool, [(bias_c[:, :, :, :], g.dram["cmp_bias"]), (valid_c[:, :, :], g.dram["cmp_valid"])], free)
    cs = ExitStack()
    w1 = g.tile("cmp_w1", [P, CMP_BLOCK, P], F32, cs)
    w2 = g.tile("cmp_w2", [P, 2, P], F32, cs)
    pos = g.tile("cmp_pos", [P, 2, CMP_BLOCK], F32, cs)
    cmp_loaded = g.load("cmp_weights", g.pool, [(w1[:, :, :], g.dram["cmp_w1"][0]), (w2[:, :, :], g.dram["cmp_w2"]),
                                                (pos[:, :, :], g.dram["cmp_pos"])], free)
    kv_c = g.tile("cmp_kv", [P, 2, T], F32, cs)
    blocks = g.tile("cmp_blocks", [P, 2, CMP_BLOCK, NCP], F32, cs)
    hidden = g.tile("cmp_hidden", [P, 2, NCP], F32, cs)
    hidden4 = g.tile("cmp_hidden_repeated", [P, 4, NCP], F32, cs)
    xs = ExitStack()
    x_hi = g.tile("odd_x_hi", [P, KT, T], F32R, xs)
    x_lo = g.tile("odd_x_lo", [P, KT, T], F32R, xs)
    x_ready = g.normalise("odd", x_hi, x_lo, free)
    zeroed = [g.pool.do(lambda e: e.memset(hidden[:, :, :], 0.0), free), g.pool.do(lambda e: e.memset(vcmp[:, :, :, :], 0.0), free),
              g.pool.do(lambda e: e.memset(kcmp[:, :, :, :], 0.0), free)]
    kv_ready, w1_free, block_ready = [], None, []
    for i in range(2):
        b, done = g.project_features("odd_w_in", (ODD_KC, ODD_VC)[i], KT, x_hi, x_lo, x_ready)
        g.bank_free[b] = m = g.act.do(lambda e, i=i, b=b: e.activation(kv_c[:, i, :], g.bank[b][:, :], ACT.Copy), done, free)
        halves = kv_c[:, i, :].rearrange("p (m r) -> p r m", r=CMP_STRIDE)
        for a in range(2):
            pb = pos[:, i, CMP_STRIDE * a:CMP_STRIDE * (a + 1)].unsqueeze(2).broadcast_to([P, CMP_STRIDE, NC])
            ready = g.dve.do(lambda e, i=i, a=a, halves=halves, pb=pb: e.tensor_tensor(
                blocks[:, i, CMP_STRIDE * a:CMP_STRIDE * (a + 1), 0:NC], halves[:, :, a:a + NC], pb, add), m, cmp_loaded, free)
        block_ready.append(ready)
    keys_ready = []
    for i in range(2):
        b, done = g.project_features("odd_w_in", (ODD_KS, ODD_KW)[i], KT, x_hi, x_lo, x_ready)
        kd = kdup[i]
        for grp in range(GROUPS):
            for half in range(2):
                rows, src = slice(64 * half, 64 * half + 64), slice(64 * grp, 64 * grp + 64)
                m = g.act.do(lambda e, kd=kd, rows=rows, src=src, grp=grp, b=b: e.activation(kd[rows, grp, :], g.bank[b][src, :], ACT.Copy), done, free)
        g.bank_free[b] = m
        keys_ready.append(m)
    banks, done = g.project_tokens("odd_w_in", ODD_VALUES, ODD_VALUE_COLUMNS, x_hi, x_lo, x_ready)
    for t in range(TT):
        m = g.act.do(lambda e, t=t, b=banks[t]: e.activation(v[:, t, :], g.bank[b][:, 0:2 * KVW], ACT.Copy), done, free)
        gates_ready = g.act.do(lambda e, t=t, b=banks[t]: e.activation(gates[:, t, :], g.bank[b][:, 2 * KVW:2 * KVW + 3 * NSA_HEADS], ACT.Sigmoid), m)
        g.bank_free[banks[t]] = gates_ready
    v_ready = gates_ready

    def compress(i, loaded):
        emits = [lambda e, p=p: e.matmul(g.bank[7][:, 0:NC], w1[:, p, :], blocks[:, i, p, 0:NC], start=(p == 0), stop=(p == CMP_BLOCK - 1))
                 for p in range(CMP_BLOCK)]
        used = g.pe.do_all(emits, loaded, block_ready[i], g.bank_free[7])
        silu = g.act.do(lambda e: e.activation(hidden[:, i, 0:NC], g.bank[7][:, 0:NC], ACT.Silu), used, zeroed)
        g.bank_free[7] = silu
        return used, silu

    used, silu = compress(0, cmp_loaded)
    w1_loaded = g.load("cmp_w1_v", g.pool, [(w1[:, :, :], g.dram["cmp_w1"][1])], used)
    mm = g.pe.do(lambda e: e.matmul(g.bank[7][:, 0:NCP], w2[:, 0, :], hidden[:, 0, :], start=True, stop=True), silu)
    for grp in range(GROUPS):
        for half in range(2):
            rows, src = slice(64 * half, 64 * half + 64), slice(64 * grp, 64 * grp + 64)
            kcmp_ready = g.act.do(lambda e, rows=rows, src=src, grp=grp, half=half: e.activation(kcmp[rows, grp, half, :], g.bank[7][src, 0:NCP], ACT.Copy), mm, zeroed)
    g.bank_free[7] = kcmp_ready
    for n in range(KT):
        b, done = g.project_features("odd_w_in", P * n, KT, x_hi, x_lo, x_ready)
        g.bank_free[b] = q_ready = g.act.do(lambda e, n=n, b=b: e.activation(q[:, n, :], g.bank[b][:, :], ACT.Copy, scale=-(NSA_HD ** -0.5)), done, free)
    used, silu = compress(1, w1_loaded)
    repeated = g.dve.do(lambda e: e.tensor_copy(hidden4[:, :, :], hidden[:, 1, :].unsqueeze(1).broadcast_to([P, 4, NCP])), silu)
    mm = g.pe.do(lambda e: e.matmul(g.bank[7][:, 0:P], hidden4[:, :, :].rearrange("p r c -> p (r c)"), w2[:, 1, :], start=True, stop=True), repeated)
    for grp in range(GROUPS):
        for r in range(4):
            rows = slice(32 * r, 32 * r + 32)
            vcmp_ready = g.dve.do(lambda e, rows=rows, grp=grp, r=r: e.tensor_copy(vcmp[rows, grp, r, :], g.bank[7][rows, 64 * grp:64 * grp + 64]), mm, zeroed)
    g.bank_free[7] = vcmp_ready
    xs.close()
    cs.close()

    free = g.fence()
    work = ExitStack()
    bias = g.tile("nsa_bias", [P, NSA_HEADS, T], F32, work)
    probs = g.tile("nsa_probs", [P, 3, T], F32, work)
    turned = g.tile("nsa_turned", [P, 3, T], F32, work)
    cmp_probs = g.tile("nsa_cmp_probs", [P, 2, NSA_HEADS, NCP], F32, work)
    part = g.tile("nsa_part", [P, NSA_HEADS * NSA_HD], F32, work)
    stats2 = g.tile("nsa_stats2", [P, 2, 2, NSA_HEADS], F32, work)
    bias_loaded = g.load("alibi", g.pool, [(bias[:, :, :], g.dram["alibi"])], free)
    head_rows = lambda h: slice(64 * (h % 2), 64 * (h % 2) + 64)
    column = lambda t, h: t[:, h:h + 1]

    for t in range(TT):
        s = t % 2
        pr = cmp_probs[:, s, :, :]
        b = g.take_bank()
        emits = [lambda e, h=h, b=b, t=t: e.matmul(g.bank[b][:, NCP * h:NCP * (h + 2)], q[:, h // 2, P * t:P * (t + 1)],
                                                   kcmp[:, h // R, :, :].rearrange("p z c -> p (z c)"), start=True, stop=True) for h in range(0, NSA_HEADS, 2)]
        mm = g.pe.do_all(emits, q_ready, kcmp_ready, g.bank_free[b])
        low, total, scale = stats[:, 0, :], stats[:, 1, :], stats[:, 2, :]
        g.bank_free[b] = m = g.dve.do(lambda e, b=b, t=t, pr=pr: e.tensor_tensor(
            pr, g.bank[b][:, :].rearrange("p (h c) -> p h c", h=NSA_HEADS), bias_c[:, t, :, :], add), mm, cmp_bias_loaded, free,
            g.cmp_free[s] if t >= 2 else None)
        m = g.dve.do(lambda e, pr=pr: e.tensor_reduce(low, pr, AX.X, ALU.min), m, g.stat_free)
        m = g.dve.do(lambda e, pr=pr: e.tensor_tensor(pr, pr, low.unsqueeze(2).broadcast_to([P, NSA_HEADS, NCP]), sub), m)
        m = g.act.do(lambda e, pr=pr: e.activation(pr, pr, ACT.Exp, scale=-1.0), m)
        m = g.dve.do(lambda e, pr=pr: e.tensor_reduce(total, pr, AX.X, add), m)
        m = g.dve.do(lambda e: e.reciprocal(total, total), m)
        m = g.dve.do(lambda e, t=t: e.tensor_tensor(scale, total, gates[:, t, 0:3 * NSA_HEADS:3], mul), m, gates_ready)
        masked = g.pool.do(lambda e, pr=pr, t=t: e.tensor_tensor(pr, pr, valid_c[:, t, :].unsqueeze(1).broadcast_to([P, NSA_HEADS, NCP]), mul), m, cmp_bias_loaded)
        b = g.take_bank()
        turn = transpose_tiles(g, pr.rearrange("p h c -> p (h c)"), 4, b, masked)
        g.cmp_free[s] = turn
        ts = t % 3
        g.bank_free[b] = m = g.act.do(lambda e, b=b, ts=ts: e.activation(turned[:, ts, :], g.bank[b][:, :], ACT.Copy), turn, free, g.turn_free[ts])
        for half in range(2):
            ob = g.take_bank()
            emits = [lambda e, ob=ob, half=half, r=r, ts=ts: e.matmul(
                g.bank[ob][:, 256 * r:256 * (r + 1)], turned[:, ts, P * (2 * half + r):P * (2 * half + r + 1)],
                vcmp[:, half, :, :].rearrange("p r d -> p (r d)"), start=True, stop=True) for r in range(2)]
            mm = g.pe.do_all(emits, m, vcmp_ready, g.bank_free[ob])
            g.bank_free[ob] = scaled = g.dve.do(lambda e, ob=ob, half=half, t=t: e.tensor_tensor(
                out[:, t, 512 * half:512 * (half + 1)].rearrange("p (h d) -> p h d", d=NSA_HD), g.bank[ob][:, :].rearrange("p (h d) -> p h d", d=NSA_HD),
                scale[:, R * half:R * (half + 1)].unsqueeze(2).broadcast_to([P, R, NSA_HD]), mul), mm)
        g.turn_free[ts] = mm
        g.stat_free = scaled

    units = [(a, t, h) for a in range(2) for t in range(TT) for h in range(NSA_HEADS)]
    tile_stats = lambda a, t: (stats2[:, t % 2, 0, :], stats2[:, t % 2, 1, :])
    state, state_done = {}, {}
    total_free = [None, None]

    def scores(n):
        a, t, h = units[n]
        b, s, keys = n % 3, n % 3, P * (t + 1)
        low, total = tile_stats(a, t)
        mm = g.pe.do(lambda e: e.matmul(g.bank[b][:, 0:keys], q[head_rows(h), h // 2, P * t:P * (t + 1)], kdup[a][head_rows(h), h // R, 0:keys],
                                        start=True, stop=True), g.bank_free[b], q_ready, keys_ready)
        g.bank_free[b] = m = g.dve.do(lambda e: e.tensor_tensor_reduce(
            probs[:, s, 0:keys], g.bank[b][:, 0:keys], bias[:, h, T - keys:T], 1.0, 3.0e38, add, ALU.min, column(low, h)),
            mm, bias_loaded, g.prob_free[s], g.low_free.get((t % 2, h)))
        state[n] = state_done[n] = g.act.do(lambda e: e.activation(probs[:, s, 0:keys], probs[:, s, 0:keys], ACT.Exp, bias=column(low, h), scale=-1.0,
                                                   accum_out=column(total, h)), m, total_free[t % 2])
        g.low_free[t % 2, h] = state[n]

    def turn(n):
        a, t, h = units[n]
        s, b, keys = n % 3, 3 + n % 3, P * (t + 1)
        mm = transpose_tiles(g, probs[:, s, :], t + 1, b, state[n])
        g.prob_free[s] = mm
        dst = lambda e: e.tensor_copy(turned[:, s, 0:keys], g.bank[b][:, 0:keys])
        if n % 4 == 3:
            m = g.act.do(lambda e: e.activation(turned[:, s, 0:keys], g.bank[b][:, 0:keys], ACT.Copy), mm, g.turn_free[s])
        else:
            m = g.dve.do(dst, mm, g.turn_free[s])
        g.bank_free[b] = m
        state[n] = m

    def values(n):
        a, t, h = units[n]
        s = n % 3
        ob = g.bank[6 + h // R]
        c = slice(NSA_HD * (h % R), NSA_HD * (h % R + 1))
        vc = slice(KVW * a + NSA_HD * (h // R), KVW * a + NSA_HD * (h // R + 1))
        emits = [lambda e, j=j: e.matmul(ob[:, c], turned[:, s, P * j:P * (j + 1)], v[:, j, vc], start=(j == 0), stop=(j == t)) for j in range(t + 1)]
        mm = g.pe.do_all(emits, state[n], v_ready, g.bank_free[6 + h // R])
        g.turn_free[s] = mm
        if h == NSA_HEADS - 1:
            total = tile_stats(a, t)[1]
            m = g.dve.do(lambda e: e.reciprocal(stats[:, 5, :], total), mm, state_done[n])
            total_free[t % 2] = m
            m = g.dve.do(lambda e: e.tensor_tensor(stats[:, 5, :], stats[:, 5, :], gates[:, t, 1 + a:3 * NSA_HEADS:3], mul), m)
            for half in range(2):
                sc = stats[:, 5, R * half:R * (half + 1)].unsqueeze(2).broadcast_to([P, R, NSA_HD])
                cols = slice(512 * half, 512 * (half + 1))
                heads = lambda x: x.rearrange("p (h d) -> p h d", d=NSA_HD)
                g.bank_free[6 + half] = p = g.dve.do(lambda e, half=half, sc=sc, cols=cols: e.tensor_tensor(
                    heads(part[:, cols]), heads(g.bank[6 + half][:, :]), sc, mul), m, g.part_free[half])
                g.part_free[half] = g.out_ready = g.pool.do(lambda e, cols=cols: e.tensor_tensor(
                    out[:, t, cols], out[:, t, cols], part[:, cols], add), p, g.out_ready)

    g.out_ready = scaled
    n_units = len(units)
    for n in range(n_units + 2):
        if n < n_units:
            scores(n)
        if 1 <= n <= n_units:
            turn(n - 1)
        if n >= 2:
            values(n - 2)
    work.close()
    inner.close()
    free = g.fence()
    o_hi = g.tile("odd_o_hi", [P, KT, T], F32R, outer)
    o_lo = g.tile("odd_o_lo", [P, KT, T], F32R, outer)
    o_ready = to_features(g, lambda t, k: out[:, t, P * k:P * (k + 1)], o_hi, o_lo, g.out_ready, free)
    g.add_to_residual("odd_w_out", KT, o_hi, o_lo, o_ready)
    outer.close()


def rope_tables(g, cos, sin, work, free):
    mul, add, sub = ALU.mult, ALU.add, ALU.subtract
    parts = (6.28125, 0.0019350051879882812, 2 * math.pi - 6.28125 - 0.0019350051879882812)
    pos_i, pos_f, angle, turns, whole = (work[:, i, :] for i in range(5))
    loaded = g.load("positions", g.pool, [(pos_i.bitcast(I32), g.dram["positions"])], free)
    m = g.dve.do(lambda e: e.tensor_copy(pos_f, pos_i.bitcast(I32)), loaded)
    angled = g.dve.do(lambda e: e.tensor_scalar(angle, pos_f, g.inv_freq[:, 0:1], None, mul), m, g.const_ready)
    for i, (out, shift) in enumerate(((sin, 0.0), (cos, 0.25))):
        m = g.dve.do(lambda e, shift=shift: e.tensor_scalar(turns, angle, 1 / (2 * math.pi), shift, mul, add), angled)
        m = g.dve.do(lambda e: e.tensor_copy(whole.bitcast(I32), turns), m)
        m = g.dve.do(lambda e: e.tensor_copy(turns, whole.bitcast(I32)), m)
        m = g.dve.do(lambda e, out=out: e.scalar_tensor_tensor(out, turns, -parts[0], angle, mul, add), m)
        m = g.dve.do(lambda e, out=out: e.scalar_tensor_tensor(out, turns, -parts[1], out, mul, add), m)
        m = g.dve.do(lambda e, out=out: e.scalar_tensor_tensor(out, turns, -parts[2], out, mul, add), m)
        m = g.dve.do(lambda e, out=out, shift=shift: e.tensor_scalar(out, out, 2 * math.pi * shift, math.pi - 1e-6, add, ALU.min), m)
        m = g.dve.do(lambda e, out=out: e.tensor_scalar(out, out, -(math.pi - 1e-6), None, ALU.max), m)
        angled = m
        done = g.act.do(lambda e, out=out: e.activation(out, out, ACT.Sin), m)
    return done


def diff_mixer(g):
    mul, add, sub = ALU.mult, ALU.add, ALU.subtract
    hd = 64
    outer = ExitStack()
    free = g.fence()
    out = g.tile("diff_out", [P, TT, D], F32, outer)
    inner = ExitStack()
    q = g.tile("diff_q", [P, KT, T], F32, inner)
    k = g.tile("diff_k", [P, KT, T], F32, inner)
    v = g.tile("diff_v", [P, TT, D], F32, inner)
    rotate = g.tile("rope_rotate", [P, P], F32, inner)
    cos = g.tile("rope_cos", [P, T], F32, inner)
    sin = g.tile("rope_sin", [P, T], F32, inner)
    lam_in = g.tile("diff_lam_in", [P, 4, hd], F32, inner)
    lam = g.tile("diff_lam", [P, 8], F32, inner)
    ts = ExitStack()
    work = g.tile("rope_work", [P, 5, T], F32, ts)
    plain = g.tile("rope_plain", [P, 2, T], F32, ts)
    turned_part = g.tile("rope_turned", [P, 2, T], F32, ts)
    x_hi = g.tile("diff_x_hi", [P, KT, T], F32R, ts)
    x_lo = g.tile("diff_x_lo", [P, KT, T], F32R, ts)
    small_loaded = g.load("diff_tables", g.pool, [(rotate[:, :], g.dram["rope_rotate"]), (lam_in[:, :, :], g.dram["diff_lam"])], free)
    x_ready = g.normalise("diff", x_hi, x_lo, free)
    tables_ready = rope_tables(g, cos[:, :], sin[:, :], work, free)
    for i in range(2):
        m = g.dve.do(lambda e, i=i: e.tensor_tensor(lam_in[:, 2 * i, :], lam_in[:, 2 * i, :], lam_in[:, 2 * i + 1, :], mul), small_loaded)
        m = g.dve.do(lambda e, i=i: e.tensor_reduce(lam[:, i:i + 1], lam_in[:, 2 * i, :], AX.X, add), m)
    m = g.act.do(lambda e: e.activation(lam[:, 2:4], lam[:, 0:2], ACT.Exp), m)
    m = g.dve.do(lambda e: e.tensor_tensor(lam[:, 4:5], lam[:, 3:4], lam[:, 2:3], sub), m)
    lam_ready = g.dve.do(lambda e: e.tensor_scalar(lam[:, 5:6], lam[:, 4:5], LAM_INIT, None, sub), m)

    plain_free, part_free = [None, None], [None, None]
    pending = None

    def rope(n, plain_ready):
        s, dst = n % 2, (q if n < KT else k)[:, n % KT, :]
        b = 6 + n % 2
        mm = g.pe.do(lambda e: e.matmul(g.bank[b][:, :], rotate[:, :], plain[:, s, :], start=True, stop=True), plain_ready, g.bank_free[b], small_loaded)
        a = g.pool.do(lambda e: e.tensor_tensor(dst, plain[:, s, :], cos[:, :], mul), plain_ready, tables_ready)
        plain_free[s] = [mm, a]
        g.bank_free[b] = c = g.dve.do(lambda e: e.tensor_tensor(turned_part[:, s, :], g.bank[b][:, :], sin[:, :], mul), mm, tables_ready, part_free[s])
        part_free[s] = g.pool.do(lambda e: e.tensor_tensor(dst, dst, turned_part[:, s, :], add), a, c)
        return part_free[s]

    for n in range(2 * KT):
        s = n % 2
        b, done = g.project_features("diff_w_qkv_2", P * n, KT, x_hi, x_lo, x_ready)
        g.bank_free[b] = m = g.act.do(lambda e, s=s, b=b: e.activation(plain[:, s, :], g.bank[b][:, :], ACT.Copy), done, free, plain_free[s])
        if pending:
            rope(*pending)
        pending = (n, m)
    for half in range(2):
        banks, done = g.project_tokens("diff_w_qkv_2", 2 * D + 512 * half, 512, x_hi, x_lo, x_ready)
        if half == 0:
            qk_ready = rope(*pending)
        for t in range(TT):
            g.bank_free[banks[t]] = v_ready = g.act.do(lambda e, t=t, half=half, b=banks[t]: e.activation(
                v[:, t, 512 * half:512 * (half + 1)], g.bank[b][:, :], ACT.Copy), done, free)
    ts.close()
    free = g.fence()
    ws = ExitStack()
    probs = g.tile("diff_probs", [P, 3, 2, T], F32, ws)
    mixed = g.tile("diff_mixed", [P, 3, T], F32, ws)
    turned = g.tile("diff_turned", [P, 3, T], F32, ws)
    squares = g.tile("diff_squares", [P, D], F32, ws)
    stats = g.tile("diff_stats", [P, 2, 6, DIFF_HEADS, 2], F32, ws)
    rms = g.tile("diff_rms", [P, 3, DIFF_HEADS], F32, ws)
    units = [(t, h) for t in range(TT) for h in range(DIFF_HEADS)]
    probs_free, mixed_free, turned_free, squares_free = [None] * 3, [None] * 3, [None] * 3, None
    first, second, summed = {}, {}, {}
    stats_free = [None, None]
    scale = hd ** -0.5

    def scores(n):
        t, h = units[n]
        s = n % 3
        st = lambda i, c: stats[:, t % 2, i, h, c:c + 1]
        for c in range(2):
            b = (2 * n + c) % 3
            rows = slice(hd * c, hd * (c + 1))
            mm = g.pe.do(lambda e, b=b, rows=rows: e.matmul(g.bank[b][:, :], q[rows, h, P * t:P * (t + 1)], k[rows, h, :], start=True, stop=True),
                         g.bank_free[b], qk_ready)
            m = g.dve.do(lambda e, b=b, c=c: e.tensor_reduce(st(0, c), g.bank[b][:, :], AX.X, ALU.max), mm, stats_free[t % 2], free)
            m = g.dve.do(lambda e, c=c: e.tensor_scalar(st(1, c), st(0, c), -scale, None, mul), m)
            g.bank_free[b] = summed[n] = g.act.do(lambda e, b=b, c=c: e.activation(
                probs[:, s, c, :], g.bank[b][:, :], ACT.Exp, bias=st(1, c), scale=scale, accum_out=st(2, c)), m, probs_free[s])

    def mix(n):
        t, h = units[n]
        s, b = n % 3, 3 + n % 3
        st = lambda i, c: stats[:, t % 2, i, h, c:c + 1]
        m = g.dve.do(lambda e: e.reciprocal(stats[:, t % 2, 3, h, :], stats[:, t % 2, 2, h, :]), summed[n])
        m = g.dve.do(lambda e: e.tensor_scalar(st(4, 0), st(3, 1), st(2, 0), lam[:, 5:6], mul, mul), m, lam_ready)
        m = g.dve.do(lambda e: e.scalar_tensor_tensor(mixed[:, s, :], probs[:, s, 1, :], st(4, 0), probs[:, s, 0, :], mul, add), m, mixed_free[s])
        probs_free[s] = m
        mm = transpose_tiles(g, mixed[:, s, :], TT, b, m)
        mixed_free[s] = mm
        g.bank_free[b] = first[n] = g.act.do(lambda e: e.activation(turned[:, s, :], g.bank[b][:, :], ACT.Copy), mm, turned_free[s])

    def values(n):
        nonlocal squares_free
        t, h = units[n]
        s, ob = n % 3, 6 + h // 4
        cols = slice(P * (h % 4), P * (h % 4 + 1))
        emits = [lambda e, j=j: e.matmul(g.bank[ob][:, cols], turned[:, s, P * j:P * (j + 1)], v[:, j, P * h:P * (h + 1)],
                                         start=(j == 0), stop=(j == TT - 1)) for j in range(TT)]
        mm = g.pe.do_all(emits, first[n], v_ready, g.bank_free[ob])
        turned_free[s] = mm
        if h % 4 == 3:
            half = h // 4
            heads = lambda x: x.rearrange("p (h d) -> p h d", d=P)
            o = out[:, t, 512 * half:512 * (half + 1)]
            hs = slice(4 * half, 4 * half + 4)
            wide = lambda x: x.unsqueeze(2).broadcast_to([P, 4, P])
            inv = stats[:, t % 2, 3, hs, 0]
            g.bank_free[ob] = m = g.dve.do(lambda e: e.tensor_tensor(heads(o), heads(g.bank[ob][:, :]), wide(inv), mul), mm)
            stats_free[t % 2] = m
            sq = squares[:, 512 * half:512 * (half + 1)]
            m = g.pool.do(lambda e: e.tensor_tensor(sq, o, o, mul), m, squares_free)
            m = g.dve.do(lambda e: e.tensor_reduce(rms[:, 0, hs], heads(sq), AX.X, add), m)
            squares_free = m
            _, m = g.token_scales(rms[:, 0, hs], 4, P, SUBLN_EPS, m, rms[:, 2, hs], rms[:, 0, hs], rms[:, 1, hs])
            second[t] = g.pool.do(lambda e: e.tensor_tensor(heads(o), heads(o), wide(rms[:, 2, hs]), mul), m)

    for n in range(len(units) + 2):
        if n < len(units):
            scores(n)
        if 1 <= n <= len(units):
            mix(n - 1)
        if n >= 2:
            values(n - 2)
    ws.close()
    inner.close()
    free = g.fence()
    o_hi = g.tile("diff_o_hi", [P, KT, T], F32R, outer)
    o_lo = g.tile("diff_o_lo", [P, KT, T], F32R, outer)
    o_ready = to_features(g, lambda t, n: out[:, t, P * n:P * (n + 1)], o_hi, o_lo, second[TT - 1], free, gain=g.subln_gain[:, 0:1])
    g.add_to_residual("diff_w_o_2", KT, o_hi, o_lo, o_ready)
    outer.close()


def final_norm(g):
    scales = g.norm_scales()
    stores = [Transfers(g.sem(f"stored{i}")) for i in range(2)]
    marks = []
    for k in range(KT):
        s = k % 2
        x = g.normed[:, s, :]
        full = g.dve.do(lambda e, x=x, k=k: e.scalar_tensor_tensor(
            x, g.residual[:, k, :], g.norm_gain[:, NORM_OF["final"], k:k + 1], g.bank[6][:, :], ALU.mult, ALU.mult),
            scales, g.normed_free[s])
        g.normed_free[s] = stores[s].start(g.sp, g.dram["out"][P * k:P * (k + 1), :], x, full)
        marks.append(g.normed_free[s])
    g.sp.wait(marks)


def norm_between(g):
    scales = g.norm_scales()
    for k in range(KT):
        g.residual_ready[k] = g.dve.do(lambda e, k=k: e.scalar_tensor_tensor(
            g.residual[:, k, :], g.residual[:, k, :], g.norm_gain[:, NORM_OF["between"], k:k + 1], g.bank[6][:, :], ALU.mult, ALU.mult), scales)
        g.add_square(k)
    g.bank_free[6] = g.residual_ready[KT - 1]


MIXERS = {"between": norm_between, "even": even_mixer, "odd": odd_mixer, "pool": pool_mixer, "diff": diff_mixer}


def build(nc, dram, stages):
    units = [unit for stage in stages for unit in stage_units(stage)]
    with ExitStack() as ctx:
        g = Program(nc, ctx, dram, units)
        consts = {}
        for name, shape, dtype in (("lower_bounds", [P, 2, HG_HEADS], F32), ("hgrn_gain", [P, 1], F32), ("ret_gain", [P, 1], F32),
                                   ("pool_scale", [P, KT], F32), ("conv_w", [P, 6, HT], F32),
                                   ("conv_b", [P, 2, HT], F32), ("subln_gain", [P, 1], F32), ("inv_freq", [P, 1], F32),
                                   ("head_rms", [P, 3, 2 * HG_HEADS * TT], F32)):
            consts[name] = g.tile(name, shape, dtype)
        (g.lower_bounds, g.hgrn_gain, g.ret_gain, g.pool_scale, g.conv_w, g.conv_b, g.subln_gain, g.inv_freq,
         g.head_rms) = consts.values()
        for k in range(KT):
            mark = g.constants.start(g.act, g.residual[:, k, :], dram["x"][P * k:P * (k + 1), :])
        full = lambda t: t[tuple(slice(None) for _ in t.shape)]
        for name in ("norm_gain", "ident", "ones"):
            consts[name] = {"norm_gain": g.norm_gain, "ident": g.ident, "ones": g.ones}[name]
        del consts["head_rms"]
        for name, t in consts.items():
            mark = g.constants.start(g.sp, full(t), dram[name])
        g.const_ready = (g.constants.sem, g.constants.count)
        g.residual_ready = [g.const_ready] * KT
        g.dve.do(lambda e: e.tensor_scalar(g.subln_gain[:, :], g.subln_gain[:, :], 1.0 - LAM_INIT, None, ALU.mult), g.const_ready)
        g.start_weights()
        for k in range(KT):
            g.add_square(k)
        for stage in stages:
            if stage in MIXERS:
                MIXERS[stage](g)
            else:
                feed_forward(g, stage)
        assert g.unit_at == len(units)
        final_norm(g)

        block = ctx.enter_context(nc.Block())

        @block.sync
        def _(e):
            g.sp.run(e)

        @block.scalar
        def _(e):
            g.act.run(e)

        @block.vector
        def _(e):
            g.dve.run(e)

        @block.gpsimd
        def _(e):
            g.pool.run(e)

        @block.tensor
        def _(e):
            g.pe.run(e)


def shape_constants():
    p = np.arange(P)
    i = np.arange(T)
    gamma = 1.0 - 2.0 ** (-5.0 - np.arange(HG_HEADS))
    dist = i[None, :] - p[:, None]
    ret = np.where(dist[None] >= 0, gamma[:, None, None] ** np.maximum(dist, 0)[None], 0.0) * P ** -0.5
    mask = np.zeros((P, 7, 64), np.int32)
    for level, s in enumerate((64, 32, 16, 8, 4, 2, 1)):
        for c in range(64):
            start = (c // s) * 2 * s
            mask[start:start + s, level, c] = 1
    slopes = 2.0 ** (-8.0 * np.arange(1, NSA_HEADS + 1) / NSA_HEADS)
    slopes = slopes.astype(np.float32)
    back = (p[:, None] + T - P - i[None, :]).astype(np.float32)
    alibi = np.where(back[:, None, :] >= 0, slopes[None, :, None] * back[:, None, :], np.float32(MASKED))
    c_end = np.arange(NCP) * CMP_STRIDE + CMP_BLOCK - 1
    tok = (P * np.arange(TT)[None, :] + p[:, None]).astype(np.float32)
    far = tok[:, :, None] - c_end[None, None, :]
    valid = (far >= 0) & (np.arange(NCP) < NC)
    bias = np.where(valid[:, :, None, :], slopes[None, None, :, None] * far[:, :, None, :], MASKED)
    share = np.zeros((P, len(POOL_WINDOWS), T), np.float32)
    for n, w in enumerate(POOL_WINDOWS):
        share[:, n, :] = 1.0 / (np.clip(i + w - w // 2, 0, T) - np.clip(i - w // 2, 0, T))
    inv = np.float32(ROPE_THETA) ** (-np.arange(0, 64, 2, dtype=np.float32) / np.float32(64))
    rot = np.zeros((P, P), np.float32)
    for m in range(P):
        if m % 64 < 32:
            rot[m + 32, m] = -1.0
        else:
            rot[m - 32, m] = 1.0
    f = lambda a: np.ascontiguousarray(a, np.float32)
    return {"ret_decay": f(ret.transpose(1, 0, 2)), "level_mask": mask, "alibi": f(alibi), "cmp_bias": f(bias),
            "cmp_valid": f(valid), "pool_share": share, "inv_freq": f(np.tile(inv, 4)[:, None]), "rope_rotate": rot,
            "ident": np.eye(P, dtype=np.float32), "ones": np.ones((P, 1), np.float32)}


def by_feature(v):
    v = np.asarray(v)
    return np.ascontiguousarray(np.moveaxis(v.reshape(v.shape[:-1] + (-1, P)), -1, 0))


def lay_out(inputs, stages):
    a = {k: np.asarray(v) for k, v in inputs.items()}
    units = [unit for stage in stages for unit in stage_units(stage)]
    weights = np.zeros((len(units), P, UNIT), np.float32)
    for n, (name, layer, k0, k, c0, c) in enumerate(units):
        w = a[name][layer if name != "pool_w_2" else 0]
        if name == "pool_w_2":
            w = w[layer]
        pieces = c0 if isinstance(c0, tuple) else ((c0, c),)
        rows = w[k0 * P:(k0 + k) * P]
        block = np.concatenate([rows[:, a:a + n_cols] for a, n_cols in pieces], axis=1).reshape(k, P, c).transpose(1, 0, 2)
        weights[n, :, 0:k * c] = block.reshape(P, k * c)
    w1 = np.zeros((2, P, CMP_BLOCK, P), np.float32)
    w2 = np.zeros((P, 2, P), np.float32)
    pos = np.zeros((P, 2, CMP_BLOCK), np.float32)
    for i, kind in enumerate("kv"):
        m1 = a[f"cmp_w1_{kind}"][0].reshape(CMP_BLOCK, NSA_HD, NSA_HD).transpose(1, 0, 2)
        for grp in range(GROUPS):
            rows = slice(64 * grp, 64 * grp + 64)
            w1[i, rows, :, rows] = m1
            w2[rows, i, rows] = a[f"cmp_w2_{kind}"][0]
            pos[rows, i, :] = a[f"cmp_pos_{kind}"][0].T
    norms = np.stack([a["mix_norm"][0], a["ffn_norm"][0], a["mix_norm"][1], a["ffn_norm"][1],
                      a["mix_norm_2"][0], a["ffn_norm_2"][0], a["mix_norm_2"][1], a["ffn_norm_2"][1], a["final_norm"], a["final_norm_2"]])
    arrays = {
        "x": np.ascontiguousarray(a["x"][0].T), "weights": weights, "norm_gain": by_feature(norms),
        "lower_bounds": by_feature(a["hgrn_lower_bounds"]),
        "hgrn_gain": np.ascontiguousarray(a["hgrn_out_norm"][0][:, None]), "ret_gain": np.ascontiguousarray(a["ret_out_norm"][0][:, None]),
        "pool_scale": by_feature(a["pool_scale_2"][0]),
        "conv_w": by_feature(a["ffn_conv_w_2"].reshape(6, FFN2)), "conv_b": by_feature(a["ffn_conv_b_2"]),
        "subln_gain": np.ascontiguousarray(a["diff_subln_2"][0][:, None]),
        "diff_lam": np.ascontiguousarray(np.broadcast_to(np.stack([a[f"diff_lam_{n}_2"][0] for n in ("q1", "k1", "q2", "k2")]), (P, 4, 64))),
        "positions": np.ascontiguousarray(np.broadcast_to(a["positions_2"], (P, T))),
        "cmp_w1": w1, "cmp_w2": w2, "cmp_pos": pos,
    }
    arrays.update(shape_constants())
    return arrays


def kernel(**inputs):
    import concourse.bacc as _bacc
    from concourse.bass_utils import run_bass_kernel_spmd as _run

    arrays = lay_out(inputs, STAGES)
    nc = _bacc.Bacc("TRN2", target_bir_lowering=False, num_devices=1)
    dram = {name: nc.dram_tensor("in_" + name, a.shape, mybir.dt.from_np(a.dtype), kind="ExternalInput").ap() for name, a in arrays.items()}
    dram["out"] = nc.dram_tensor("out", (D, T), F32, kind="ExternalOutput").ap()
    build(nc, dram, STAGES)
    results = _run(nc, [{"in_" + name: a for name, a in arrays.items()}], core_ids=[0])
    return np.ascontiguousarray(results.results[0]["out"].T)[None]
```

```python
from contextlib import ExitStack
import math

import numpy as np
import concourse.bass as bass
from concourse import mybir

F32 = mybir.dt.float32
F32R = mybir.dt.float32r
I32 = mybir.dt.int32
ACT = mybir.ActivationFunctionType
ALU = mybir.AluOpType
AX = mybir.AxisListType

P = 128
T = 512
D = 1024
KT = D // P
TT = T // P
UNIT = 1024
RAW_SLOTS = 3
SPLIT_SLOTS = 3
RING_BANKS = 6

EPS = 1e-6
SUBLN_EPS = 1e-5
HG_HEADS = 4
CHUNK = 128
NSA_HEADS, NSA_HD, GROUPS = 16, 64, 2
KVW = GROUPS * NSA_HD
CMP_BLOCK, CMP_STRIDE = 32, 16
NC = T // CMP_STRIDE - CMP_BLOCK // CMP_STRIDE + 1
NCP = 32
MASKED = 1e30
ODD_KC, ODD_VC, ODD_KS, ODD_VS, ODD_KW, ODD_VW, ODD_GATES = (D + KVW * i for i in range(7))
ODD_VALUES = ((ODD_VS, KVW), (ODD_VW, KVW + 3 * NSA_HEADS))
ODD_VALUE_COLUMNS = 2 * KVW + 3 * NSA_HEADS
FFN1, FFN2 = 2816, 2816
HT = FFN1 // P
POOL_WINDOWS = (2, 4, 8, 16)
DIFF_HEADS = 8
LAM_INIT = 0.8 - 0.6 * math.exp(-0.3 * 1)
ROPE_THETA = 10000.0

STAGES = ("even", "ffn_a", "odd", "ffn_b", "between", "pool", "ffn_c", "diff", "ffn_d")
NORM_OF = {"even": 0, "ffn_a": 1, "odd": 2, "ffn_b": 3, "pool": 4, "ffn_c": 5, "diff": 6, "ffn_d": 7, "between": 8, "final": 9}


PREPARED = ("even", "ffn_a", "odd", "ffn_b", "ffn_c", "diff", "ffn_d")


def feature_units(matrix, layer, column, k_tiles):
    return [(matrix, layer, k, min(UNIT // P, k_tiles - k), column, P) for k in range(0, k_tiles, UNIT // P)]


def token_units(matrix, layer, column, columns, k_tiles):
    return [(matrix, layer, k, 2, column, columns) for k in range(0, k_tiles, 2)]


def stage_units(stage):
    units = []
    if stage == "even":
        hq, hf, hi, hg, rq, rk, rv, rg = (512 * i for i in range(8))
        heads = lambda *bases: [u for base in bases for h in range(HG_HEADS) for u in feature_units("even_w_in", 0, base + P * h, KT)]
        units += heads(hf, hq, rq, rk)
        units += token_units("even_w_in", 0, hi, 512, KT) + token_units("even_w_in", 0, rv, 512, KT)
        units += heads(hg, rg)
        for n in range(KT):
            units += feature_units("even_w_out", 0, P * n, KT)
    if stage == "odd":
        for col in (ODD_KC, ODD_VC, ODD_KS, ODD_KW):
            units += feature_units("odd_w_in", 0, col, KT)
        units += token_units("odd_w_in", 0, ODD_VALUES, ODD_VALUE_COLUMNS, KT)
        for n in range(KT):
            units += feature_units("odd_w_in", 0, P * n, KT)
        for n in range(KT):
            units += feature_units("odd_w_out", 0, P * n, KT)
    if stage in ("ffn_a", "ffn_b", "ffn_c", "ffn_d"):
        up, down = ("ffn_w_gate_up", "ffn_w_down") if stage in ("ffn_a", "ffn_b") else ("ffn_w_up_2", "ffn_w_down_2")
        layer = 0 if stage in ("ffn_a", "ffn_c") else 1
        for j in range(HT):
            units += feature_units(up, layer, P * j, KT) + feature_units(up, layer, FFN1 + P * j, KT)
        for n in range(KT):
            units += feature_units(down, layer, P * n, HT)
    if stage == "pool":
        for g in range(len(POOL_WINDOWS)):
            units += [("pool_w_2", g, 0, 2, 0, 256)]
    if stage == "diff":
        head = lambda h: feature_units("diff_w_qkv_2", 0, P * h, KT) + feature_units("diff_w_qkv_2", 0, D + P * h, KT)
        units += head(0)
        for half in range(2):
            units += token_units("diff_w_qkv_2", 0, 2 * D + 512 * half, 512, KT)
        for h in range(1, DIFF_HEADS):
            units += head(h)
        for n in range(KT):
            units += feature_units("diff_w_o_2", 0, P * n, KT)
    return units


class Lane:
    def __init__(self, sem):
        self.sem, self.count, self.queue, self.reached = sem, 0, [], {}

    def wait(self, *marks):
        for mark in marks:
            if mark is None:
                continue
            if isinstance(mark, list):
                self.wait(*mark)
                continue
            sem, value = mark
            if value > self.reached.get(sem.name, 0):
                self.reached[sem.name] = value
                self.queue.append(lambda e, s=sem, v=value: e.wait_ge(s, v))

    def put(self, emit):
        self.queue.append(emit)

    def do(self, emit, *after):
        self.wait(*after)
        self.count += 1
        self.queue.append(lambda e: emit(e).then_inc(self.sem, 1))
        return self.mark()

    def do_all(self, emits, *after):
        self.wait(*after)
        for emit in emits[:-1]:
            self.put(emit)
        return self.do(emits[-1])

    def mark(self):
        return (self.sem, self.count) if self.count else None

    def run(self, engine):
        for emit in self.queue:
            emit(engine)


class Transfers:
    def __init__(self, sem):
        self.sem, self.count = sem, 0

    def start(self, lane, dst, src, *after):
        lane.wait(*after)
        self.count += 16
        lane.put(lambda e: e.dma_start(dst, src).then_inc(self.sem, 16))
        return (self.sem, self.count)


class Program:

    def __init__(self, nc, ctx, dram, units):
        self.nc, self.ctx, self.dram, self.units = nc, ctx, dram, units
        self.pe, self.dve, self.act, self.pool, self.sp = (
            Lane(self.sem(f"{n}_done")) for n in ("pe", "dve", "act", "pool", "sp"))
        self.bank = [ctx.enter_context(nc.psum_tensor(f"bank{i}", [P, 512], F32)) for i in range(8)]
        self.bank_free = [None] * 8
        self.ring_at = 0
        self.open_banks = []
        self.ring_banks = RING_BANKS
        self.residual = self.tile("residual", [P, KT, T], F32)
        self.residual_ready = [None] * KT
        self.norm_gain = self.tile("norm_gain", [P, 10, KT], F32)
        self.ident = self.tile("ident", [P, P], F32)
        self.ones = self.tile("ones", [P, 1], F32)
        self.square = self.tile("square", [P, 2, T], F32)
        self.square_free = [None, None]
        self.square_sum = self.tile("square_sum", [P, T], F32)
        self.sum_free = None
        self.x_hi = self.tile("x_hi", [P, KT, T], F32R)
        self.x_lo = self.tile("x_lo", [P, KT, T], F32R)
        self.x_ready = [None] * KT
        self.scale_rows = self.tile("scale_rows", [P, 2, T], F32)
        self.layer = -1
        self.normed = self.tile("normed", [P, 2, T], F32)
        self.normed_free = [None, None]
        self.rms = self.tile("rms", [P, 3, TT], F32)
        self.last_layer_done = None
        self.constants = Transfers(self.sem("constants_loaded"))
        self.raw = self.tile("weight_raw", [P, RAW_SLOTS, UNIT], F32)
        self.w_hi = [self.tile(f"weight_hi{i}", [P, UNIT], F32R) for i in range(SPLIT_SLOTS)]
        self.w_lo = [self.tile(f"weight_lo{i}", [P, UNIT], F32R) for i in range(SPLIT_SLOTS)]
        self.raw_loads = [Transfers(self.sem(f"weights_loaded{i}")) for i in range(RAW_SLOTS)]
        self.loaded, self.is_split, self.used = {}, {}, {}
        self.unit_at = 0

    def sem(self, name):
        return self.ctx.enter_context(self.nc.semaphore(name))

    def tile(self, name, shape, dtype, scope=None):
        return (scope or self.ctx).enter_context(self.nc.sbuf_tensor(name, shape, dtype))

    def load(self, name, lane, moves, *after):
        transfers = Transfers(self.sem(name + "_loaded"))
        for dst, src in moves:
            mark = transfers.start(lane, dst, src, *after)
        return mark

    def fence(self):
        return [lane.mark() for lane in (self.pe, self.dve, self.act, self.pool)]

    def take_bank(self):
        i = self.ring_at % self.ring_banks
        while i in self.open_banks:
            i = (i + 1) % self.ring_banks
        self.ring_at = i + 1
        return i

    def load_unit(self, u):
        if u >= len(self.units):
            return
        _, _, _, k, _, c = self.units[u]
        slot = u % RAW_SLOTS
        self.loaded[u] = self.raw_loads[slot].start(
            self.sp, self.raw[:, slot, 0:k * c], self.dram["weights"][u, :, 0:k * c], self.is_split.get(u - RAW_SLOTS))

    def split_unit(self, u):
        if u >= len(self.units):
            return
        _, _, _, k, _, c = self.units[u]
        raw, hi, lo = self.raw[:, u % RAW_SLOTS, 0:k * c], self.w_hi[u % SPLIT_SLOTS], self.w_lo[u % SPLIT_SLOTS]
        high = self.act.do(lambda e: e.activation(hi[:, 0:k * c], raw, ACT.Copy), self.loaded[u], self.used.get(u - SPLIT_SLOTS))
        self.is_split[u] = self.dve.do(
            lambda e: e.tensor_tensor(lo[:, 0:k * c], raw, hi[:, 0:k * c].bitcast(F32), ALU.subtract), high)
        self.load_unit(u + RAW_SLOTS)

    def take_unit(self, matrix, column):
        u = self.unit_at
        self.unit_at += 1
        assert self.units[u][0] == matrix and self.units[u][4] == column, (self.units[u], matrix, column)
        if u + SPLIT_SLOTS - 1 not in self.is_split:
            self.split_unit(u + SPLIT_SLOTS - 1)
        _, _, _, k, _, c = self.units[u]
        view = lambda t: t[:, 0:k * c].rearrange("p (k c) -> p k c", k=k)
        return u, view(self.w_hi[u % SPLIT_SLOTS]), view(self.w_lo[u % SPLIT_SLOTS])

    def start_weights(self):
        for u in range(RAW_SLOTS):
            self.load_unit(u)
        for u in range(SPLIT_SLOTS - 1):
            self.split_unit(u)

    def feature_steps(self, matrix, column, k_tiles, x_hi, x_lo, x_ready):
        b = self.take_bank()
        out = self.bank[b]
        self.open_banks = [b]
        self.pe.wait(self.bank_free[b])
        k0 = 0
        while k0 < k_tiles:
            u, w_hi, w_lo = self.take_unit(matrix, column)
            self.pe.wait(self.is_split[u])
            n = self.units[u][3]
            for k in range(n):
                self.pe.wait(x_ready[k0 + k])
                for i, (w, x) in enumerate(((w_hi, x_hi), (w_lo, x_hi), (w_hi, x_lo))):
                    emit = lambda e, w=w, x=x, k=k, kk=k0 + k, i=i: e.matmul(
                        out[:, :], w[:, k, :], x[:, kk, :], start=(kk == 0 and i == 0), stop=(kk == k_tiles - 1 and i == 2))
                    if k == n - 1 and i == 2:
                        self.used[u] = self.pe.do(emit)
                    else:
                        self.pe.put(emit)
                if k < n - 1 or k0 + n < k_tiles:
                    yield
            k0 += n
        self.open_banks = []
        return b, self.used[u]

    def project_features(self, *args):
        steps = self.feature_steps(*args)
        while True:
            try:
                next(steps)
            except StopIteration as end:
                return end.value

    def project_tokens(self, *args):
        steps = self.token_steps(*args)
        while True:
            try:
                next(steps)
            except StopIteration as end:
                return end.value

    def token_steps(self, matrix, column, columns, x_hi, x_lo, x_ready):
        banks = [self.take_bank() for _ in range(TT)]
        self.open_banks = banks
        self.pe.wait(*[self.bank_free[b] for b in banks])
        for k0 in range(0, KT, 2):
            u, w_hi, w_lo = self.take_unit(matrix, column)
            self.pe.wait(self.is_split[u], x_ready[k0], x_ready[k0 + 1])
            for t in range(TT):
                for k in range(2):
                    for i, (w, x) in enumerate(((w_hi, x_hi), (w_lo, x_hi), (w_hi, x_lo))):
                        emit = lambda e, w=w, x=x, k=k, kk=k0 + k, i=i, t=t: e.matmul(
                            self.bank[banks[t]][:, 0:columns], x[:, kk, P * t:P * (t + 1)], w[:, k, :],
                            start=(kk == 0 and i == 0), stop=(kk == KT - 1 and i == 2))
                        last = k == 1 and i == 2 and t == TT - 1
                        if last:
                            self.used[u] = self.pe.do(emit)
                        else:
                            self.pe.put(emit)
                yield
        self.open_banks = []
        return banks, self.used[u]

    def add_square(self, k):
        s = k % 2
        if k == 0:
            self.summed = self.act.do(lambda e: e.activation(self.square_sum[:, :], self.residual[:, k, :], ACT.Square),
                                      self.residual_ready[k], self.sum_free)
            return
        squared = self.act.do(lambda e: e.activation(self.square[:, s, :], self.residual[:, k, :], ACT.Square),
                              self.residual_ready[k], self.square_free[s])
        self.summed = self.square_free[s] = self.pool.do(lambda e: e.tensor_tensor(
            self.square_sum[:, :], self.square_sum[:, :], self.square[:, s, :], ALU.add), squared, self.summed)
        if k == KT - 1:
            emits = [lambda e, t=t: e.matmul(self.bank[7][:, t:t + 1], self.square_sum[:, P * t:P * (t + 1)], self.ones[:, :],
                                             start=True, stop=True) for t in range(TT)]
            self.sum_free = self.pe.do_all(emits, self.summed, self.bank_free[7], self.const_ready)

    def token_scales(self, sums, n, count, eps, done, out, tmp, tmp2, free=None):
        mean = self.dve.do(lambda e: e.tensor_scalar(tmp, sums, 1.0 / count, eps, ALU.mult, ALU.add), done, free)
        root = self.act.do(lambda e: e.activation(tmp2, tmp, ACT.Sqrt), mean)
        return mean, self.dve.do(lambda e: e.reciprocal(out, tmp2), root)

    def spread_scales(self, column, bank, ready):
        self.pe.wait(self.bank_free[bank], ready, self.const_ready)
        for t in range(TT):
            emit = lambda e, t=t: e.matmul(self.bank[bank][:, P * t:P * (t + 1)], column(t).broadcast_to([P, P]),
                                           self.ident[:, :], start=True, stop=True)
            if t < TT - 1:
                self.pe.put(emit)
            else:
                return self.pe.do(emit)

    def norm_scales(self):
        sums = self.sum_free
        read, self.column_ready = self.token_scales(self.bank[7][:, 0:TT], TT, D, EPS, sums, self.rms[:, 2, :], self.rms[:, 0, :], self.rms[:, 1, :])
        self.bank_free[7] = read
        return self.spread_scales(lambda t: self.rms[:, 2, t:t + 1], 6, self.column_ready)

    def begin_layer(self):
        self.layer += 1
        self.scale = self.scale_rows[:, self.layer % 2, :]
        spread = self.norm_scales()
        self.scale_ready = self.bank_free[6] = self.act.do(lambda e, row=self.scale: e.activation(row, self.bank[6][:, :], ACT.Copy), spread, self.last_layer_done)
        self.last_layer_done = self.fence()
        return self.scale

    def split_into(self, x, hi, lo, ready, *free):
        high = self.act.do(lambda e: e.activation(hi, x, ACT.Copy), ready, *free)
        return self.dve.do(lambda e: e.tensor_tensor(lo, x, hi.bitcast(F32), ALU.subtract), high)

    def split_scaled(self, x, gain, hi, lo, ready, *free):
        high = self.act.do(lambda e: e.activation(hi, x, ACT.Copy, scale=gain), ready, *free)
        return self.dve.do(lambda e: e.scalar_tensor_tensor(lo, x, gain, hi.bitcast(F32), ALU.mult, ALU.subtract), high)

    def residual_done(self, n, mark, x_free):
        self.residual_ready[n] = mark
        if self.next_stage in PREPARED:
            row = NORM_OF[self.next_stage]
            self.x_ready[n] = self.split_scaled(self.residual[:, n, :], self.norm_gain[:, row, n:n + 1],
                                                self.x_hi[:, n, :], self.x_lo[:, n, :], mark, x_free, self.const_ready)
        if n:
            self.add_square(n - 1)
        if n == KT - 1:
            self.add_square(n)

    def add_to_residual(self, matrix, k_tiles, x_hi, x_lo, x_ready):
        x_free = self.pe.mark()
        for n in range(KT):
            b, done = self.project_features(matrix, P * n, k_tiles, x_hi, x_lo, x_ready)
            self.bank_free[b] = mark = self.dve.do(
                lambda e, n=n, b=b: e.tensor_tensor(self.residual[:, n, :], self.residual[:, n, :], self.bank[b][:, :], ALU.add), done)
            self.residual_done(n, mark, x_free)


def feed_forward(g, stage):
    swiglu = stage in ("ffn_a", "ffn_b")
    layer = 0 if stage in ("ffn_a", "ffn_c") else 1
    up, down = ("ffn_w_gate_up", "ffn_w_down") if swiglu else ("ffn_w_up_2", "ffn_w_down_2")
    with ExitStack() as scope:
        free = g.fence()
        h_hi = g.tile(f"{stage}_h_hi", [P, HT, T], F32R, scope)
        h_lo = g.tile(f"{stage}_h_lo", [P, HT, T], F32R, scope)
        gate = g.tile(f"{stage}_gate", [P, T], F32, scope)
        opened = g.tile(f"{stage}_opened", [P, 2, T], F32, scope)
        hidden = g.tile(f"{stage}_hidden", [P, 2, T], F32, scope)
        scale_row = g.begin_layer()
        gate_free, opened_free, hidden_free, h_ready = None, [None, None], [None, None], []
        for j in range(HT):
            s = j % 2
            bg, gate_done = g.project_features(up, P * j, KT, g.x_hi, g.x_lo, g.x_ready)
            bu, up_done = g.project_features(up, FFN1 + P * j, KT, g.x_hi, g.x_lo, g.x_ready)
            acc, u, op, hd = g.bank[bg], g.bank[bu], opened[:, s, :], hidden[:, s, :]
            g.bank_free[bg] = scaled = g.dve.do(lambda e, acc=acc: e.tensor_tensor(gate[:, :], acc[:, :], scale_row, ALU.mult),
                                                gate_done, g.scale_ready, gate_free, free)
            if swiglu:
                gate_free = m = g.act.do(lambda e, op=op: e.activation(op, gate[:, :], ACT.Silu), scaled, opened_free[s], free)
            else:
                w = lambda tap, j=j: g.conv_w[:, 3 * layer + tap, j:j + 1]
                mid = g.dve.do(lambda e, op=op, w=w, j=j: e.tensor_scalar(
                    op, gate[:, :], w(1), g.conv_b[:, layer, j:j + 1], ALU.mult, ALU.add), scaled, opened_free[s], g.const_ready, free)
                left = g.dve.do(lambda e, op=op, w=w: e.scalar_tensor_tensor(
                    op[:, 1:T], gate[:, 0:T - 1], w(0), op[:, 1:T], ALU.mult, ALU.add), mid)
                gate_free = g.dve.do(lambda e, op=op, w=w: e.scalar_tensor_tensor(
                    op[:, 0:T - 1], gate[:, 1:T], w(2), op[:, 0:T - 1], ALU.mult, ALU.add), left)
                m = g.act.do(lambda e, op=op: e.activation(op, op, ACT.Gelu), gate_free)
            g.bank_free[bu] = scaled = g.dve.do(lambda e, hd=hd, u=u: e.tensor_tensor(hd, u[:, :], scale_row, ALU.mult), up_done, hidden_free[s], free)
            opened_free[s] = product = g.pool.do(lambda e, op=op, hd=hd: e.tensor_tensor(hd, op, hd, ALU.mult), m, scaled)
            hidden_free[s] = g.split_into(hd, h_hi[:, j, :], h_lo[:, j, :], product)
            h_ready.append(hidden_free[s])
        g.add_to_residual(down, HT, h_hi, h_lo, h_ready)


def hgrn_levels(g, q, k, cum, diff, k_dec, q_dec, scores, level_mask, mask_loaded, ready, state):
    blocks = HG_HEADS * TT
    pairs = lambda t, s: t.rearrange("p (n z s) -> p n z s", z=2, s=s)

    def diagonal(part):
        half = blocks // 2
        emits = []
        for m in range(half):
            c = slice(P * (half * part + m), P * (half * part + m + 1))
            out = g.bank[6 + m // 4][:, P * (m % 4):P * (m % 4 + 1)]
            emits.append(lambda e, out=out, c=c: e.matmul(out, k[:, c], q[:, c], start=True, stop=True))
        mm = g.pe.do_all(emits, g.bank_free[6], g.bank_free[7], ready)
        for b in range(2):
            c = slice(P * (half * part + 4 * b), P * (half * part + 4 * b + 4))
            state["chosen"] = g.bank_free[6 + b] = g.dve.do(lambda e, b=b, c=c: e.tensor_tensor(
                scores[:, c].rearrange("p (m i) -> p m i", m=4), g.bank[6 + b][:, :].rearrange("p (m i) -> p m i", m=4),
                g.ident[:, :].unsqueeze(1).broadcast_to([P, 4, P]), ALU.mult), mm, g.const_ready)

    def decays(s):
        n = blocks * P // (2 * s)
        c4, d4 = pairs(cum[:, :], s), pairs(diff[:, :], s)
        rel = g.dve.do(lambda e: e.tensor_tensor(
            diff[:, :].rearrange("p (n t) -> p n t", n=n), cum[:, :].rearrange("p (n t) -> p n t", n=n),
            c4[:, :, 0, s - 1:s].broadcast_to([P, n, 2 * s]), ALU.subtract), ready, state["diff_free"])
        first = g.act.do(lambda e: e.activation(d4[:, :, 0, :], d4[:, :, 0, :], ACT.Exp, scale=-1.0), rel)
        second = g.act.do(lambda e: e.activation(d4[:, :, 1, :], d4[:, :, 1, :], ACT.Exp), rel)
        return first, second

    def decayed(s, first, second):
        d4, kd4, q4, k4 = (pairs(t[:, :], s) for t in (diff, k_dec, q, k))
        k_ready = g.pool.do(lambda e: e.tensor_tensor(kd4[:, :, 0, :], k4[:, :, 0, :], d4[:, :, 0, :], ALU.mult), first, state["products"], ready)
        q_ready = g.dve.do(lambda e: e.tensor_tensor(
            q_dec[:, :].rearrange("p (n s) -> p n s", s=s), q4[:, :, 1, :], d4[:, :, 1, :], ALU.mult), second, state["products"])
        state["diff_free"] = [k_ready, q_ready]

    def products(level, s):
        emits = []
        for m in range(blocks):
            out = g.bank[6 + m // 8][:, 64 * (m % 8):64 * (m % 8 + 1)]
            emits.append(lambda e, out=out, m=m: e.matmul(
                out, k_dec[:, P * m:P * (m + 1)], q_dec[:, 64 * m:64 * (m + 1)], start=True, stop=True))
        state["products"] = mm = g.pe.do_all(emits, state["diff_free"], g.bank_free[6], g.bank_free[7])
        mask = level_mask[:, level, :].rearrange("p (n s) -> p n s", s=s).unsqueeze(1).broadcast_to([P, 8, 64 // s, s])
        for b in range(2):
            rows = slice(P * 8 * b, P * 8 * (b + 1))
            state["chosen"] = g.bank_free[6 + b] = g.dve.do(lambda e, b=b, rows=rows: e.copy_predicated(
                scores[:, rows].rearrange("p (m n z s) -> p m n z s", m=8, z=2, s=s)[:, :, :, 1, :], mask,
                g.bank[6 + b][:, :].rearrange("p (m n s) -> p m n s", m=8, s=s)), mm, mask_loaded, state["chosen"])

    state.update(diff_free=None, products=None)
    levels = list(enumerate((64, 32, 16, 8, 4, 2, 1)))
    exps = decays(levels[0][1])
    yield True
    diagonal(0)
    yield True
    decayed(levels[0][1], *exps)
    diagonal(1)
    yield True
    for level, s in levels:
        if level + 1 < len(levels):
            exps = decays(levels[level + 1][1])
            yield True
        products(level, s)
        if level + 1 < len(levels):
            decayed(levels[level + 1][1], *exps)
        yield True


def even_mixer(g):
    mul, add, sub = ALU.mult, ALU.add, ALU.subtract
    width = HG_HEADS * T
    outer = ExitStack()
    free = g.fence()
    o = g.tile("even_o", [P, KT, T], F32, outer)
    bound = g.tile("hgrn_bound", [P, 6, HG_HEADS], F32, outer)
    inner = ExitStack()
    rq, rk, hv, rv = (g.tile(n, [P, width], F32, inner) for n in ("ret_q", "ret_k", "hgrn_v", "ret_v"))
    hs = ExitStack()
    hq, hk, cum, scores, k_dec = (g.tile(n, [P, width], F32, hs) for n in ("hgrn_q", "hgrn_k", "hgrn_cum", "hgrn_scores", "hgrn_k_dec"))
    diff_and_q = g.tile("hgrn_diff_and_q_dec", [P, width + width // 2], F32, hs)
    diff, q_dec = diff_and_q[:, 0:width], diff_and_q[:, width:]
    level_mask = g.tile("hgrn_level_mask", [P, 7, 64], I32, hs)
    mask_loaded = g.load("hgrn_level_mask", g.pool, [(level_mask[:, :, :], g.dram["level_mask"])], free)
    scale_row = g.begin_layer()

    b0, b1 = g.lower_bounds[:, 0, :], g.lower_bounds[:, 1, :]
    top, e0, e1, total, low, rest = (bound[:, i, :] for i in range(6))
    m = g.dve.do(lambda e: e.tensor_tensor(top, b0, b1, ALU.max), g.const_ready, free)
    m = g.dve.do(lambda e: e.tensor_tensor(e0, b0, top, sub), m)
    m = g.dve.do(lambda e: e.tensor_tensor(e1, b1, top, sub), m)
    m = g.act.do(lambda e: e.activation(bound[:, 1:3, :], bound[:, 1:3, :], ACT.Exp), m)
    m = g.dve.do(lambda e: e.tensor_tensor(total, e0, e1, add), m)
    m = g.dve.do(lambda e: e.reciprocal(total, total), m)
    m = g.dve.do(lambda e: e.tensor_tensor(low, e0, total, mul), m)
    bound_ready = g.dve.do(lambda e: e.tensor_scalar(rest, low, -1.0, 1.0, mul, add), m)

    steps = lambda base, h: g.feature_steps("even_w_in", 512 * base + P * h, KT, g.x_hi, g.x_lo, g.x_ready)
    part = lambda t, h: t[:, T * h:T * (h + 1)]
    HQ, HF, HI, HG, RQ, RK, RV, RG = range(8)

    def scaled_to(out, b, done, *after):
        g.bank_free[b] = mark = g.dve.do(lambda e: e.tensor_tensor(out, g.bank[b][:, :], scale_row, mul), done, g.scale_ready, *after)
        return mark

    restart = g.pool.do(lambda e: e.memset(k_dec[:, :], 1.0), free)
    restart = g.pool.do(lambda e: e.memset(k_dec[:, :].rearrange("p (m t) -> p m t", t=CHUNK)[:, :, 0:1], 0.0), restart)
    for h in range(HG_HEADS):
        b, done = g.project_features("even_w_in", 512 * HF + P * h, KT, g.x_hi, g.x_lo, g.x_ready)
        m = scaled_to(part(diff, h), b, done, free)
        m = g.act.do(lambda e, h=h: e.activation(part(diff, h), part(diff, h), ACT.Sigmoid), m)
        m = g.dve.do(lambda e, h=h: e.tensor_scalar(part(diff, h), part(diff, h), rest[:, h:h + 1], low[:, h:h + 1], mul, add), m, bound_ready)
        f_ready = g.pool.do(lambda e, h=h: e.tensor_scalar(part(hk, h), part(diff, h), -1.0, 1.0, mul, add), m, free)
    for h in range(HG_HEADS):
        b, done = g.project_features("even_w_in", 512 * HQ + P * h, KT, g.x_hi, g.x_lo, g.x_ready)
        if h == 0:
            logged = g.act.do(lambda e: e.activation(diff, diff, ACT.Ln), f_ready)
        m = scaled_to(part(hq, h), b, done, free)
        q_ready = g.act.do(lambda e, h=h: e.activation(part(hq, h), part(hq, h), ACT.Silu), m)
        if h == 0:
            summed = g.dve.do(lambda e: e.tensor_tensor_scan(cum[:, :], k_dec[:, :], diff, 0.0, mul, add), logged, restart, free)
            cleared = g.pool.do(lambda e: e.memset(k_dec[:, :], 0.0), summed)

    marks = {}

    def rest_of_projections():
        for base, dst in ((RQ, rq), (RK, rk)):
            for h in range(HG_HEADS):
                b, done = yield from steps(base, h)
                marks["ret_qk"] = scaled_to(part(dst, h), b, done, free)
                yield
        for base, dst in ((HI, hv), (RV, rv)):
            banks, done = yield from g.token_steps("even_w_in", 512 * base, 512, g.x_hi, g.x_lo, g.x_ready)
            for t in range(TT):
                g.bank_free[banks[t]] = marks["v"] = g.act.do(
                    lambda e, dst=dst, t=t, b=banks[t]: e.activation(part(dst, t), g.bank[b][:, :], ACT.Copy, scale=g.rms[:, 2, t:t + 1]),
                    done, g.column_ready, free)
            yield

    state = {}
    across = g.head_rms[:, 0, 0:HG_HEADS * TT]
    tiles = lambda t: t.rearrange("p (m t) -> p m t", t=P)
    heads = lambda t: t.rearrange("p (h m t) -> p h m t", h=HG_HEADS, t=P)
    k_far = cum[:, 0:3 * HG_HEADS * P].rearrange("p (h i t) -> p h i t", h=HG_HEADS, i=3)
    cross = diff_and_q[:, :].rearrange("p (h i t) -> p h i t", h=HG_HEADS, i=6)

    def within_and_ends():
        yield from hgrn_levels(g, hq, hk, cum, diff, k_dec, q_dec, scores, level_mask, mask_loaded, [summed, cleared, q_ready, f_ready], state)
        ends = tiles(cum[:, :])[:, :, P - 1:P]
        m = g.act.do(lambda e: e.activation(diff, cum[:, :], ACT.Exp), state["diff_free"])
        whole = g.act.do(lambda e: e.activation(across, ends.rearrange("p m o -> p (m o)"), ACT.Exp), summed)
        yield True
        state["q_start"] = g.dve.do(lambda e: e.tensor_tensor(k_dec[:, :], hq[:, :], diff, mul), m, state["products"])
        m = g.dve.do(lambda e: e.tensor_tensor(tiles(diff), tiles(cum[:, :]), ends.broadcast_to([P, HG_HEADS * TT, P]), sub), state["q_start"])
        m = g.act.do(lambda e: e.activation(diff, diff, ACT.Exp, scale=-1.0), m)
        yield True
        kend = g.dve.do(lambda e: e.tensor_tensor(hk[:, :], hk[:, :], diff, mul), m)
        far = lambda i: k_far[:, :, i, :]
        one = lambda m: across.rearrange("p (h m) -> p h m", m=TT)[:, :, m:m + 1].broadcast_to([P, HG_HEADS, P])
        m = g.pool.do(lambda e: e.tensor_tensor(far(0), heads(hk[:, :])[:, :, 0, :], one(1), mul), kend, whole)
        g.pool.do(lambda e: e.tensor_tensor(far(1), heads(hk[:, :])[:, :, 1, :], one(2), mul), kend)
        state["k_far"] = g.pool.do(lambda e: e.tensor_tensor(far(2), far(0), one(2), mul), m)
        yield True

    def spread(front, back, per):
        for i, _ in enumerate(front):
            if i % per == per - 1:
                next(back, None)
        for _ in back:
            pass

    spread(rest_of_projections(), within_and_ends(), 4)

    PAIRS = ((0, 1), (1, 2), (2, 3), (0, 2), (1, 3), (0, 3))
    gates_ready, outs, o_ready = {}, {}, {}
    gate_of = (HG,) * HG_HEADS + (RG,) * HG_HEADS

    def gates():
        for head in range(KT):
            b, done = yield from steps(gate_of[head], head % HG_HEADS)
            m = scaled_to(o[:, head, :], b, done, free)
            gates_ready[head] = g.act.do(lambda e, head=head: e.activation(o[:, head, :], o[:, head, :], ACT.Silu), m)
            yield

    def cross_pairs(h):
        banks = [6, 7]
        emits = []
        for i, (kj, qi) in enumerate(PAIRS):
            lhs = hk[:, T * h + P * kj:T * h + P * (kj + 1)] if i < 3 else k_far[:, h, i - 3, :]
            emits.append(lambda e, i=i, lhs=lhs, qi=qi: e.matmul(
                g.bank[banks[i // 3]][:, P * (i % 3):P * (i % 3 + 1)], lhs, k_dec[:, T * h + P * qi:T * h + P * (qi + 1)], start=True, stop=True))
        mm = g.pe.do_all(emits, state["q_start"], state["k_far"], *[g.bank_free[b] for b in banks])
        for i, lane in enumerate((g.act, g.dve)):
            dst, src = cross[:, h, 3 * i:3 * i + 3, :].rearrange("p m t -> p (m t)"), g.bank[banks[i]][:, 0:3 * P]
            copy = (lambda e, dst=dst, src=src: e.activation(dst, src, ACT.Copy)) if i == 0 else (lambda e, dst=dst, src=src: e.tensor_copy(dst, src))
            g.bank_free[banks[i]] = state["cross", h, i] = lane.do(copy, mm)

    def finish_head(bank, done, head, gain):
        s = head % 2
        sq = g.act.do(lambda e: e.activation(g.square[:, s, :], g.bank[bank][:, :], ACT.Square), done, g.square_free[s])
        outs[head] = g.bank_free[bank] = g.dve.do(lambda e: e.scalar_tensor_tensor(
            o[:, head, :], g.bank[bank][:, :], gain, o[:, head, :], mul, mul), sq, gates_ready[head], g.const_ready)
        return sq

    def sum_squares(sq, head):
        s = head % 2
        emits = []
        for t in range(TT):
            col = TT * head + t
            emits.append(lambda e, t=t, col=col: e.matmul(g.bank[7][:, col:col + 1], g.square[:, s, P * t:P * (t + 1)], g.ones[:, :],
                                                          start=True, stop=True))
        g.square_free[s] = g.pe.do_all(emits, sq, g.bank_free[7])
        return g.square_free[s]

    def hgrn_values(h):
        b = g.take_bank()
        emits = []
        for i in range(TT):
            for j in range(i + 1):
                rhs = scores[:, T * h + P * i:T * h + P * (i + 1)] if j == i else cross[:, h, PAIRS.index((j, i)), :]
                emits.append(lambda e, j=j, rhs=rhs, i=i: e.matmul(
                    g.bank[b][:, P * i:P * (i + 1)], hv[:, T * j + P * h:T * j + P * (h + 1)], rhs, start=(j == 0), stop=(j == i)))
        mm = g.pe.do_all(emits, g.bank_free[b], marks["v"], state["cross", h, 0], state["cross", h, 1], state["chosen"])
        return finish_head(b, mm, h, g.hgrn_gain[:, :])

    spans = [(j, T - P * j) for j in range(TT)]
    offset = [0, 512, 896, 1152]
    late = ExitStack()

    def ret_score(h, decay, ret_scores):
        s = h % 2
        for j, n in spans:
            b = g.take_bank()
            g.pe.wait(g.bank_free[b], marks["ret_qk"])
            mm = g.pe.do(lambda e, b=b, j=j, n=n: e.matmul(
                g.bank[b][:, 0:n], rk[:, T * h + P * j:T * h + P * (j + 1)], rq[:, T * h + P * j:T * (h + 1)], start=True, stop=True))
            g.bank_free[b] = state["ret_scores", h] = g.dve.do(lambda e, b=b, j=j, n=n: e.tensor_tensor(
                ret_scores[:, s, offset[j]:offset[j] + n], g.bank[b][:, 0:n], decay[:, h, 0:n], mul),
                mm, state["decay_loaded"], state.get(("ret_free", s)), state["late_free"])

    def ret_values(h, ret_scores):
        s, b = h % 2, g.take_bank()
        emits = [lambda e, j=j, n=n: e.matmul(g.bank[b][:, P * j:T], rv[:, T * j + P * h:T * j + P * (h + 1)], ret_scores[:, s, offset[j]:offset[j] + n],
                                              start=(j == 0), stop=(j == TT - 1)) for j, n in spans]
        state["ret_free", s] = mm = g.pe.do_all(emits, g.bank_free[b], marks["v"], state["ret_scores", h])
        return finish_head(b, mm, HG_HEADS + h, g.ret_gain[:, :])

    def group_scales(group, sums):
        n = HG_HEADS * TT
        cols = slice(n * group, n * (group + 1))
        g.bank_free[7], ready = g.token_scales(g.bank[7][:, cols], n, P, EPS, sums, *(g.head_rms[:, i, cols] for i in (2, 0, 1)))
        return ready

    def normalise_head(head, ready, o_hi, o_lo):
        b = g.take_bank()
        rows = g.spread_scales(lambda t: g.head_rms[:, 2, TT * head + t:TT * head + t + 1], b, ready)
        x = o[:, head, :]
        g.bank_free[b] = full = g.dve.do(lambda e: e.tensor_tensor(x, x, g.bank[b][:, :], mul), rows, outs[head])
        o_ready[head] = g.split_into(x, o_hi[:, head, :], o_lo[:, head, :], full, state["late_free"])

    def outputs():
        for h in range(HG_HEADS):
            cross_pairs(h)
            yield True
        pending = None
        for h in range(HG_HEADS):
            while h not in gates_ready:
                yield False
            sq = hgrn_values(h)
            yield True
            if pending:
                sum_squares(*pending)
            pending = (sq, h)
        hs.close()
        state["late_free"] = g.fence()
        o_hi, o_lo = (g.tile(f"even_{n}", [P, KT, T], F32R, late) for n in ("o_hi", "o_lo"))
        state["o_hi"], state["o_lo"] = o_hi, o_lo
        decay = g.tile("ret_decay", [P, HG_HEADS, T], F32, late)
        ret_scores = g.tile("ret_scores", [P, 2, 1280], F32, late)
        state["decay_loaded"] = g.load("ret_decay", g.pool, [(decay[:, :, :], g.dram["ret_decay"])], state["late_free"])
        yield True
        sums = sum_squares(*pending)
        hgrn_scales = group_scales(0, sums)
        yield True
        ret_score(0, decay, ret_scores)
        yield True
        pending = None
        for h in range(HG_HEADS):
            if h + 1 < HG_HEADS:
                ret_score(h + 1, decay, ret_scores)
                yield True
            normalise_head(h, hgrn_scales, o_hi, o_lo)
            yield True
            while HG_HEADS + h not in gates_ready:
                yield False
            sq = ret_values(h, ret_scores)
            yield True
            if pending:
                sum_squares(*pending)
            pending = (sq, HG_HEADS + h)
        ret_scales = group_scales(1, sum_squares(*pending))
        for h in range(HG_HEADS):
            normalise_head(HG_HEADS + h, ret_scales, o_hi, o_lo)

    spread(gates(), outputs(), 2)
    g.add_to_residual("even_w_out", KT, state["o_hi"], state["o_lo"], o_ready)
    late.close()
    inner.close()
    outer.close()


def pool_mixer(g):
    with ExitStack() as scope:
        free = g.fence()
        PAD = max(POOL_WINDOWS)
        W = T + 2 * PAD
        x_hi = g.tile("pool_x_hi", [P, KT, T], F32R, scope)
        x_lo = g.tile("pool_x_lo", [P, KT, T], F32R, scope)
        padded = g.tile("pool_padded", [P, KT, W], F32, scope)
        sums = g.tile("pool_sums", [P, 2, W], F32, scope)
        pooled = g.tile("pool_pooled", [P, 2, T], F32, scope)
        share = g.tile("pool_share", [P, len(POOL_WINDOWS), T], F32, scope)
        share_loaded = g.load("pool_share", g.pool, [(share[:, :, :], g.dram["pool_share"])], free)
        zeroed = g.pool.do(lambda e: e.memset(padded[:, :, :], 0.0), free)
        scales = g.norm_scales()
        x_ready, sums_free, pooled_free = [], [None, None], [None, None]
        for k in range(KT):
            s, window = k % 2, POOL_WINDOWS[k // 2]
            x = padded[:, k, PAD:PAD + T]
            full = g.dve.do(lambda e, x=x, k=k: e.scalar_tensor_tensor(
                x, g.residual[:, k, :], g.norm_gain[:, NORM_OF["pool"], k:k + 1], g.bank[6][:, :], ALU.mult, ALU.mult),
                scales, g.const_ready, zeroed)
            g.bank_free[6] = full
            src = padded[:, k, :]
            lo, hi = 1, W
            span, which = 2, 0
            back, ahead = 1, 0
            m = full
            while True:
                dst = sums[:, which, :]
                m = g.pool.do(lambda e, dst=dst, src=src, lo=lo, hi=hi, back=back, ahead=ahead: e.tensor_tensor(
                    dst[:, lo:hi], src[:, lo - back:hi - back], src[:, lo + ahead:hi + ahead], ALU.add), m, sums_free[0], free)
                if span == window:
                    break
                src = dst
                back = ahead = span // 2
                lo, hi = lo + back, hi - ahead
                span *= 2
                which = 1 - which
            out = pooled[:, s, :]
            m = g.dve.do(lambda e, out=out, dst=dst, k=k: e.tensor_tensor(out, dst[:, PAD:PAD + T], share[:, k // 2, :], ALU.mult),
                         m, share_loaded, pooled_free[s])
            sums_free = [m]
            m = g.dve.do(lambda e, out=out, x=x: e.tensor_tensor(out, out, x, ALU.subtract), m)
            pooled_free[s] = g.split_into(out, x_hi[:, k, :], x_lo[:, k, :], m, free)
            x_ready.append(pooled_free[s])
        for group in range(len(POOL_WINDOWS)):
            u, w_hi, w_lo = g.take_unit("pool_w_2", 0)
            for half in range(2):
                b, n = g.take_bank(), 2 * group + half
                c = slice(P * half, P * (half + 1))
                emits = []
                for k in range(2):
                    for i, (w, x) in enumerate(((w_hi, x_hi), (w_hi, x_lo), (w_lo, x_hi))):
                        emits.append(lambda e, b=b, w=w, x=x, k=k, i=i, c=c, group=group: e.matmul(
                            g.bank[b][:, :], w[:, k, c], x[:, 2 * group + k, :], start=(k == 0 and i == 0), stop=(k == 1 and i == 2)))
                mm = g.pe.do_all(emits, g.is_split[u], g.bank_free[b], x_ready[2 * group], x_ready[2 * group + 1])
                g.bank_free[b] = mark = g.dve.do(lambda e, n=n, b=b: e.scalar_tensor_tensor(
                    g.residual[:, n, :], g.bank[b][:, :], g.pool_scale[:, n:n + 1], g.residual[:, n, :], ALU.mult, ALU.add), mm)
                g.residual_done(n, mark, None)
            g.used[u] = mm


def transpose_tiles(g, src, n_tiles, bank, ready):
    emits = [lambda e, j=j: e.transpose(g.bank[bank][:, P * j:P * (j + 1)], src[:, P * j:P * (j + 1)], g.ident[:, :]) for j in range(n_tiles)]
    return g.pe.do_all(emits, ready, g.bank_free[bank], g.const_ready)


def to_features(g, out, k, hi, lo, ready, free, gain):
    b = g.take_bank()
    emits = [lambda e, t=t: e.transpose(g.bank[b][:, P * t:P * (t + 1)], out(t), g.ident[:, :]) for t in range(TT)]
    mm = g.pe.do_all(emits, ready, g.bank_free[b])
    g.bank_free[b] = mark = g.split_scaled(g.bank[b][:, :], gain, hi[:, k, :], lo[:, k, :], mm, free)
    return mark


def run_together(front, back, per_step):
    for _ in front:
        for _ in range(per_step):
            if next(back, None) is False:
                break
    for _ in back:
        pass


def odd_mixer(g):
    mul, add, sub = ALU.mult, ALU.add, ALU.subtract
    R = NSA_HEADS // GROUPS
    PAIRS = NSA_HEADS // 2
    outer = ExitStack()
    free = g.fence()
    out = g.tile("nsa_out", [P, TT, NSA_HEADS * NSA_HD], F32, outer)
    inner = ExitStack()
    q_hi = g.tile("nsa_q_hi", [P, 3, T], F32R, inner)
    q_lo = g.tile("nsa_q_lo", [P, 3, T], F32R, inner)
    v = g.tile("nsa_v", [P, TT, 2 * KVW], F32, inner)
    gates = g.tile("nsa_gates", [P, TT, 3 * NSA_HEADS], F32, inner)
    k_hi = g.tile("nsa_k_hi", [P, 2, GROUPS, T], F32R, inner)
    k_lo = g.tile("nsa_k_lo", [P, 2, GROUPS, T], F32R, inner)
    kcmp_hi = g.tile("nsa_k_cmp_hi", [P, GROUPS, 2, NCP], F32R, inner)
    kcmp_lo = g.tile("nsa_k_cmp_lo", [P, GROUPS, 2, NCP], F32R, inner)
    vcmp = g.tile("nsa_v_cmp", [P, GROUPS, 4, NSA_HD], F32, inner)
    bias_c = g.tile("nsa_bias_cmp", [P, TT, NSA_HEADS, NCP], F32, inner)
    valid_c = g.tile("nsa_valid_cmp", [P, TT, NCP], F32, inner)
    cmp_bias_loaded = g.load("cmp_bias", g.pool, [(bias_c[:, :, :, :], g.dram["cmp_bias"]), (valid_c[:, :, :], g.dram["cmp_valid"])], free)
    cs = ExitStack()
    w1 = g.tile("cmp_w1", [P, CMP_BLOCK, P], F32, cs)
    w2 = g.tile("cmp_w2", [P, 2, P], F32, cs)
    pos = g.tile("cmp_pos", [P, 2, CMP_BLOCK], F32, cs)
    cmp_loaded = g.load("cmp_weights", g.pool, [(w1[:, :, :], g.dram["cmp_w1"][0]), (w2[:, :, :], g.dram["cmp_w2"]),
                                                (pos[:, :, :], g.dram["cmp_pos"])], free)
    kv_c = g.tile("cmp_kv", [P, 2, T], F32, cs)
    blocks = g.tile("cmp_blocks", [P, 2, CMP_BLOCK, NCP], F32, cs)
    hidden = g.tile("cmp_hidden", [P, 2, NCP], F32, cs)
    hidden4 = g.tile("cmp_hidden_repeated", [P, 4, NCP], F32, cs)
    scale_row = g.begin_layer()
    out_zeroed = g.pool.do(lambda e: e.memset(out[:, :, :], 0.0), free)
    zeroed = [g.pool.do(lambda e: e.memset(hidden[:, :, :], 0.0), free), g.pool.do(lambda e: e.memset(vcmp[:, :, :, :], 0.0), free),
              g.pool.do(lambda e: e.memset(kcmp_hi[:, :, :, :].bitcast(F32), 0.0), free), g.pool.do(lambda e: e.memset(kcmp_lo[:, :, :, :].bitcast(F32), 0.0), free)]
    project = lambda column: g.project_features("odd_w_in", column, KT, g.x_hi, g.x_lo, g.x_ready)
    both = ((slice(0, 64), slice(64, 128)), (slice(64, 128), slice(0, 64)))
    block_ready = []
    for i in range(2):
        b, done = project((ODD_KC, ODD_VC)[i])
        g.bank_free[b] = m = g.dve.do(lambda e, i=i, b=b: e.tensor_tensor(kv_c[:, i, :], g.bank[b][:, :], scale_row, mul), done, g.scale_ready, free)
        halves = kv_c[:, i, :].rearrange("p (m r) -> p r m", r=CMP_STRIDE)
        for a in range(2):
            pb = pos[:, i, CMP_STRIDE * a:CMP_STRIDE * (a + 1)].unsqueeze(2).broadcast_to([P, CMP_STRIDE, NC])
            ready = g.dve.do(lambda e, i=i, a=a, halves=halves, pb=pb: e.tensor_tensor(
                blocks[:, i, CMP_STRIDE * a:CMP_STRIDE * (a + 1), 0:NC], halves[:, :, a:a + NC], pb, add), m, cmp_loaded, free)
        block_ready.append(ready)
    keys_ready = []
    for i in range(2):
        b, done = project((ODD_KS, ODD_KW)[i])
        x, s = g.normed[:, i, :], i
        g.bank_free[b] = m = g.dve.do(lambda e, x=x, b=b: e.tensor_tensor(x, g.bank[b][:, :], scale_row, mul), done, g.normed_free[i], free)
        for grp, (own, other) in enumerate(both):
            high = g.act.do(lambda e, i=i, grp=grp, own=own, x=x: e.activation(k_hi[own, i, grp, :], x[own, :], ACT.Copy), m)
            low = g.dve.do(lambda e, i=i, grp=grp, own=own, x=x: e.tensor_tensor(k_lo[own, i, grp, :], x[own, :], k_hi[own, i, grp, :].bitcast(F32), sub), high)
            keys_ready.append(g.act.do(lambda e, i=i, grp=grp, own=own, other=other: e.activation(
                k_hi[other, i, grp, :], k_hi[own, i, grp, :].bitcast(F32), ACT.Copy), high))
            keys_ready.append(g.act.do(lambda e, i=i, grp=grp, own=own, other=other: e.activation(
                k_lo[other, i, grp, :], k_lo[own, i, grp, :].bitcast(F32), ACT.Copy), low))
        g.normed_free[i] = low

    def compress(i, loaded):
        emits = [lambda e, p=p: e.matmul(g.bank[7][:, 0:NC], w1[:, p, :], blocks[:, i, p, 0:NC], start=(p == 0), stop=(p == CMP_BLOCK - 1))
                 for p in range(CMP_BLOCK)]
        used = g.pe.do_all(emits, loaded, block_ready[i], g.bank_free[7])
        silu = g.act.do(lambda e: e.activation(hidden[:, i, 0:NC], g.bank[7][:, 0:NC], ACT.Silu), used, zeroed)
        g.bank_free[7] = silu
        return used, silu

    used, silu = compress(0, cmp_loaded)
    w1_loaded = g.load("cmp_w1_v", g.pool, [(w1[:, :, :], g.dram["cmp_w1"][1])], used)
    banks, done = g.project_tokens("odd_w_in", ODD_VALUES, ODD_VALUE_COLUMNS, g.x_hi, g.x_lo, g.x_ready)
    mm = g.pe.do(lambda e: e.matmul(g.bank[7][:, 0:NCP], w2[:, 0, :], hidden[:, 0, :], start=True, stop=True), silu)
    for grp, (own, other) in enumerate(both):
        for half, rows in enumerate((slice(0, 64), slice(64, 128))):
            high = g.act.do(lambda e, rows=rows, own=own, grp=grp, half=half: e.activation(kcmp_hi[rows, grp, half, :], g.bank[7][own, 0:NCP], ACT.Copy), mm, zeroed)
            if rows == own:
                low = g.dve.do(lambda e, own=own, grp=grp, half=half: e.tensor_tensor(
                    kcmp_lo[own, grp, half, :], g.bank[7][own, 0:NCP], kcmp_hi[own, grp, half, :].bitcast(F32), sub), high, zeroed)
                g.act.wait(low)
        kcmp_ready = g.act.do(lambda e, own=own, other=other, grp=grp: e.activation(
            kcmp_lo[other, grp, 1 - grp, :], kcmp_lo[own, grp, grp, :].bitcast(F32), ACT.Copy), low)
    g.bank_free[7] = kcmp_ready
    for t in range(TT):
        column = g.rms[:, 2, t:t + 1]
        m = g.act.do(lambda e, t=t, b=banks[t], column=column: e.activation(v[:, t, :], g.bank[b][:, 0:2 * KVW], ACT.Copy, scale=column), done, g.column_ready, free)
        gates_ready = g.act.do(lambda e, t=t, b=banks[t], column=column: e.activation(
            gates[:, t, :], g.bank[b][:, 2 * KVW:2 * KVW + 3 * NSA_HEADS], ACT.Sigmoid, scale=column), m)
        g.bank_free[banks[t]] = gates_ready
    v_ready = gates_ready
    q_ready = {}

    def queries():
        for n in range(PAIRS):
            s = n % 3
            b, done = yield from g.feature_steps("odd_w_in", P * n, KT, g.x_hi, g.x_lo, g.x_ready)
            x = g.normed[:, n % 2, :]
            g.bank_free[b] = m = g.dve.do(lambda e, x=x, b=b: e.tensor_tensor(x, g.bank[b][:, :], scale_row, mul), done, g.normed_free[n % 2])
            g.normed_free[n % 2] = q_ready[n] = g.split_scaled(x, -(NSA_HD ** -0.5), q_hi[:, s, :], q_lo[:, s, :], m, pair_used.get(n - 3), free)
            yield

    pair_used = {}
    front = queries()
    for _ in range(KT // 2):
        next(front)
    used, silu = compress(1, w1_loaded)
    repeated = g.dve.do(lambda e: e.tensor_copy(hidden4[:, :, :], hidden[:, 1, :].unsqueeze(1).broadcast_to([P, 4, NCP])), silu)
    for _ in range(KT // 2):
        next(front)
    mm = g.pe.do(lambda e: e.matmul(g.bank[7][:, 0:P], hidden4[:, :, :].rearrange("p r c -> p (r c)"), w2[:, 1, :], start=True, stop=True), repeated)
    for grp in range(GROUPS):
        for r in range(4):
            rows = slice(32 * r, 32 * r + 32)
            vcmp_ready = g.dve.do(lambda e, rows=rows, grp=grp, r=r: e.tensor_copy(vcmp[rows, grp, r, :], g.bank[7][rows, 64 * grp:64 * grp + 64]), mm, zeroed)
    g.bank_free[7] = vcmp_ready
    cs.close()

    free2 = g.fence()
    work = ExitStack()
    bias = g.tile("nsa_bias", [P, 3, 2, T], F32, work)
    probs = g.tile("nsa_probs", [P, 5, T], F32, work)
    turned = g.tile("nsa_turned", [P, 3, T], F32, work)
    part = g.tile("nsa_part", [P, 2, T], F32, work)
    stats = g.tile("nsa_stats", [P, 2, 3, 16], F32, work)
    cmp_probs = g.tile("nsa_cmp_probs", [P, TT, R, NCP], F32, work)
    cmp_stats = g.tile("nsa_cmp_stats", [P, 3, TT, R], F32, work)
    bias_loads = [Transfers(g.sem(f"alibi_loaded{i}")) for i in range(3)]
    bias_loaded, bias_used = {}, {}
    g.ring_banks = 2
    units = [(n, a, z, t) for n in range(PAIRS) for a in range(2) for z in range(2) for t in range(TT)]
    exp_done, turned_ready, least_ready = {}, {}, {}
    prob_free, turn_free, low_free, total_free, part_free = [None] * 5, [None] * 3, {}, [None] * 2, [None] * 2
    state = {"cmp_free": None, "cmp_stats_free": None, "out": out_zeroed, "cmp_scores": None}

    def load_bias(n):
        if n < PAIRS:
            bias_loaded[n] = bias_loads[n % 3].start(g.pool, bias[:, n % 3, :, :], g.dram["alibi"][:, 2 * n:2 * n + 2, :], bias_used.get(n - 3), free2)

    for n in range(2):
        load_bias(n)

    def scores(i):
        n, a, z, t = units[i]
        b, s, keys, sq = 2 + i % 2, i % 5, P * (t + 1), n % 3
        rows = slice(64 * z, 64 * z + 64)
        low = stats[:, n % 2, 0, 8 * a + 2 * t + z:8 * a + 2 * t + z + 1]
        grp = 2 * n // R
        emits = [lambda e, x=x, k=k, j=j: e.matmul(g.bank[b][:, 0:keys], x[rows, sq, P * t:P * (t + 1)], k[rows, a, grp, 0:keys], start=(j == 0), stop=(j == 2))
                 for j, (x, k) in enumerate(((q_hi, k_hi), (q_hi, k_lo), (q_lo, k_hi)))]
        mm = g.pe.do_all(emits, g.bank_free[b], q_ready[n], keys_ready)
        pair_used[n] = mm
        g.bank_free[b] = m = g.dve.do(lambda e: e.tensor_tensor_reduce(
            probs[:, s, 0:keys], g.bank[b][:, 0:keys], bias[:, n % 3, z, T - keys:T], 1.0, 3.0e38, add, ALU.min, low),
            mm, bias_loaded[n], prob_free[s], low_free.get((n % 2, a, z, t)), free2)
        bias_used[n] = least_ready[i] = m

    def exponentials(i):
        n, a, z, t = units[i]
        s, keys = i % 5, P * (t + 1)
        low, total = (stats[:, n % 2, j, 8 * a + 2 * t + z:8 * a + 2 * t + z + 1] for j in (0, 1))
        exp_done[i] = g.act.do(lambda e: e.activation(probs[:, s, 0:keys], probs[:, s, 0:keys], ACT.Exp, bias=low, scale=-1.0, accum_out=total),
                               least_ready[i], total_free[n % 2])
        low_free[n % 2, a, z, t] = exp_done[i]

    def turn(i):
        _, _, _, t = units[i]
        s, b, keys = i % 5, 4 + i % 2, P * (t + 1)
        prob_free[s] = mm = transpose_tiles(g, probs[:, s, :], t + 1, b, exp_done[i])
        if i % 2:
            m = g.act.do(lambda e: e.activation(turned[:, i % 3, 0:keys], g.bank[b][:, 0:keys], ACT.Copy), mm, turn_free[i % 3])
        else:
            m = g.dve.do(lambda e: e.tensor_copy(turned[:, i % 3, 0:keys], g.bank[b][:, 0:keys]), mm, turn_free[i % 3])
        g.bank_free[b] = turned_ready[i] = m

    def values(i):
        n, a, z, t = units[i]
        grp = 2 * n // R
        ob = g.bank[6 + a]
        c = slice(P * t + NSA_HD * z, P * t + NSA_HD * (z + 1))
        vc = slice(KVW * a + NSA_HD * grp, KVW * a + NSA_HD * (grp + 1))
        emits = [lambda e, j=j: e.matmul(ob[:, c], turned[:, i % 3, P * j:P * (j + 1)], v[:, j, vc], start=(j == 0), stop=(j == t)) for j in range(t + 1)]
        turn_free[i % 3] = mm = g.pe.do_all(emits, turned_ready[i], v_ready, g.bank_free[6 + a] if (z, t) == (0, 0) else None)
        if (z, t) == (1, TT - 1):
            cols = slice(8 * a, 8 * a + 8)
            inv = stats[:, n % 2, 2, cols]
            m = g.dve.do(lambda e: e.reciprocal(inv, stats[:, n % 2, 1, cols]), exp_done[i])
            gate = gates[:, :, 6 * n + 1 + a:6 * n + 1 + a + 4:3]
            grid = inv.rearrange("p (t z) -> p t z", t=TT)
            m = g.dve.do(lambda e: e.tensor_tensor(grid, grid, gate, mul), m)
            total_free[n % 2] = m
            wide = inv.unsqueeze(2).broadcast_to([P, 8, NSA_HD])
            g.bank_free[6 + a] = part_ready = g.dve.do(lambda e: e.tensor_tensor(
                part[:, a, :].rearrange("p (h d) -> p h d", h=8), ob[:, :].rearrange("p (h d) -> p h d", h=8), wide, mul), m, mm, part_free[a])
            dst = out[:, :, P * n:P * (n + 1)]
            src = part[:, a, :].rearrange("p (t c) -> p t c", t=TT)
            part_free[a] = state["out"] = g.pool.do(lambda e: e.tensor_tensor(dst, dst, src, add), part_ready, state["out"])

    def compressed_scores(n):
        b, s, grp = g.take_bank(), n % 3, 2 * n // R
        emits = []
        for t in range(TT):
            for j, (x, k) in enumerate(((q_hi, kcmp_hi), (q_hi, kcmp_lo), (q_lo, kcmp_hi))):
                emits.append(lambda e, x=x, k=k, j=j, t=t: e.matmul(g.bank[b][:, 64 * t:64 * (t + 1)], x[:, s, P * t:P * (t + 1)],
                                                                   k[:, grp, :, :].rearrange("p z c -> p (z c)"), start=(j == 0), stop=(j == 2)))
        mm = g.pe.do_all(emits, q_ready[n], kcmp_ready, g.bank_free[b])
        first = 2 * n - R * grp
        g.bank_free[b] = state["cmp_scores"] = g.dve.do(lambda e: e.tensor_tensor(
            cmp_probs[:, :, first:first + 2, :].rearrange("p t z c -> p t (z c)"), g.bank[b][:, 0:4 * 64].rearrange("p (t c) -> p t c", t=TT),
            bias_c[:, :, 2 * n:2 * n + 2, :].rearrange("p t z c -> p t (z c)"), add), mm, cmp_bias_loaded, free2, state["cmp_free"])

    def compressed_attention(grp):
        low, total = (cmp_stats[:, j, :, :].rearrange("p t h -> p (t h)") for j in range(2))
        flat = cmp_probs[:, :, :, :].rearrange("p t h c -> p (t h) c")
        wide = lambda x: x.unsqueeze(2).broadcast_to([P, TT * R, NCP])
        m = g.dve.do(lambda e: e.tensor_reduce(low, flat, AX.X, ALU.min), state["cmp_scores"])
        m = g.dve.do(lambda e: e.tensor_tensor(flat, flat, wide(low), sub), m)
        m = g.act.do(lambda e: e.activation(flat, flat, ACT.Exp, scale=-1.0), m)
        yield
        m = g.dve.do(lambda e: e.tensor_reduce(total, flat, AX.X, add), m)
        m2 = g.dve.do(lambda e: e.reciprocal(total, total), m)
        gate = gates[:, :, 3 * R * grp:3 * R * (grp + 1):3]
        scale_ready = g.dve.do(lambda e: e.tensor_tensor(cmp_stats[:, 2, :, :], cmp_stats[:, 1, :, :], gate, mul), m2, state["cmp_stats_free"])
        masked = g.pool.do(lambda e: e.tensor_tensor(cmp_probs[:, :, :, :], cmp_probs[:, :, :, :],
                                                     valid_c[:, :, :].unsqueeze(2).broadcast_to([P, TT, R, NCP]), mul), m, cmp_bias_loaded)
        yield
        for t in range(TT):
            b, s = g.take_bank(), t % 2
            turn = transpose_tiles(g, cmp_probs[:, t, :, :].rearrange("p h c -> p (h c)"), 2, b, masked)
            state["cmp_free"] = turn
            x = g.square[:, s, 0:2 * P]
            g.bank_free[b] = m = g.act.do(lambda e, b=b, x=x: e.activation(x, g.bank[b][:, 0:2 * P], ACT.Copy), turn, g.square_free[s])
            yield
            b = g.take_bank()
            emits = [lambda e, b=b, r=r, x=x: e.matmul(g.bank[b][:, 256 * r:256 * (r + 1)], x[:, P * r:P * (r + 1)],
                                                       vcmp[:, grp, :, :].rearrange("p r d -> p (r d)"), start=True, stop=True) for r in range(2)]
            g.square_free[s] = mm = g.pe.do_all(emits, m, vcmp_ready, g.bank_free[b])
            cols = slice(512 * grp, 512 * (grp + 1))
            heads = lambda x: x.rearrange("p (h d) -> p h d", h=R)
            y = g.normed[:, s, :]
            g.bank_free[b] = m = g.dve.do(lambda e, b=b, y=y, t=t: e.tensor_tensor(
                heads(y), heads(g.bank[b][:, :]), cmp_stats[:, 2, t, :].unsqueeze(2).broadcast_to([P, R, NSA_HD]), mul), mm, scale_ready, g.normed_free[s])
            state["cmp_stats_free"] = m
            g.normed_free[s] = state["out"] = g.pool.do(lambda e, y=y, t=t, cols=cols: e.tensor_tensor(out[:, t, cols], out[:, t, cols], y, add),
                                                            m, state["out"])
            yield

    def attention():
        extra = iter(())
        for i in range(len(units) + 4):
            if i < len(units):
                n, a, z, t = units[i]
                while n not in q_ready:
                    yield False
                if (a, z, t) == (0, 0, 0):
                    load_bias(n + 2)
                    compressed_scores(n)
                    if n % (PAIRS // GROUPS) == PAIRS // GROUPS - 1:
                        extra = compressed_attention(2 * n // R)
                scores(i)
            if 3 <= i < len(units) + 3:
                turn(i - 3)
            if i < len(units):
                exponentials(i)
            if i >= 4:
                values(i - 4)
            next(extra, None)
            yield True

    run_together(front, attention(), 2)
    work.close()
    inner.close()
    g.ring_banks = RING_BANKS
    free = g.fence()
    o_hi = g.tile("odd_o_hi", [P, KT, T], F32R, outer)
    o_lo = g.tile("odd_o_lo", [P, KT, T], F32R, outer)
    o_ready = [to_features(g, lambda t, k=k: out[:, t, P * k:P * (k + 1)], k, o_hi, o_lo, state["out"], free, 1.0) for k in range(KT)]
    g.add_to_residual("odd_w_out", KT, o_hi, o_lo, o_ready)
    outer.close()


def rope_tables(g, cos, sin, work, free):
    mul, add = ALU.mult, ALU.add
    parts = (6.28125, 0.0019350051879882812, 2 * math.pi - 6.28125 - 0.0019350051879882812)
    pos_i, pos_f, angle, turns, whole = (work[:, i, :] for i in range(5))
    loaded = g.load("positions", g.pool, [(pos_i.bitcast(I32), g.dram["positions"])], free)
    m = g.dve.do(lambda e: e.tensor_copy(pos_f, pos_i.bitcast(I32)), loaded)
    angled = g.dve.do(lambda e: e.tensor_scalar(angle, pos_f, g.inv_freq[:, 0:1], None, mul), m, g.const_ready)
    for i, (out, shift) in enumerate(((sin, 0.0), (cos, 0.25))):
        m = g.dve.do(lambda e, shift=shift: e.tensor_scalar(turns, angle, 1 / (2 * math.pi), shift, mul, add), angled)
        m = g.dve.do(lambda e: e.tensor_copy(whole.bitcast(I32), turns), m)
        m = g.dve.do(lambda e: e.tensor_copy(turns, whole.bitcast(I32)), m)
        m = g.dve.do(lambda e, out=out: e.scalar_tensor_tensor(out, turns, -parts[0], angle, mul, add), m)
        m = g.dve.do(lambda e, out=out: e.scalar_tensor_tensor(out, turns, -parts[1], out, mul, add), m)
        m = g.dve.do(lambda e, out=out: e.scalar_tensor_tensor(out, turns, -parts[2], out, mul, add), m)
        m = g.dve.do(lambda e, out=out, shift=shift: e.tensor_scalar(out, out, 2 * math.pi * shift, math.pi - 1e-6, add, ALU.min), m)
        m = g.dve.do(lambda e, out=out: e.tensor_scalar(out, out, -(math.pi - 1e-6), None, ALU.max), m)
        angled = m
        done = g.act.do(lambda e, out=out: e.activation(out, out, ACT.Sin), m)
    return done


def diff_mixer(g):
    mul, add, sub = ALU.mult, ALU.add, ALU.subtract
    hd = 64
    outer = ExitStack()
    free = g.fence()
    out = g.tile("diff_out", [P, TT, D], F32, outer)
    inner = ExitStack()
    qk_hi = g.tile("diff_qk_hi", [P, 2, 3, T], F32R, inner)
    qk_lo = g.tile("diff_qk_lo", [P, 2, 3, T], F32R, inner)
    v = g.tile("diff_v", [P, TT, D], F32, inner)
    rotate = g.tile("rope_rotate", [P, P], F32, inner)
    cos = g.tile("rope_cos", [P, T], F32, inner)
    sin = g.tile("rope_sin", [P, T], F32, inner)
    plain = g.tile("rope_plain", [P, 2, T], F32, inner)
    turned_part = g.tile("rope_turned", [P, 2, T], F32, inner)
    lam_in = g.tile("diff_lam_in", [P, 4, hd], F32, inner)
    lam = g.tile("diff_lam", [P, 8], F32, inner)
    probs = g.tile("diff_probs", [P, 3, 2, T], F32, inner)
    mixed = g.tile("diff_mixed", [P, 2, T], F32, inner)
    turned = g.tile("diff_turned", [P, 2, T], F32, inner)
    stats = g.tile("diff_stats", [P, 5, DIFF_HEADS, TT, 2], F32, inner)
    rms = g.tile("diff_rms", [P, 3, DIFF_HEADS, TT], F32, inner)
    scale_row = g.begin_layer()
    small_loaded = g.load("diff_tables", g.pool, [(rotate[:, :], g.dram["rope_rotate"]), (lam_in[:, :, :], g.dram["diff_lam"])], free)
    tables_ready = rope_tables(g, cos[:, :], sin[:, :], probs[:, :, :, :].rearrange("p s c t -> p (s c) t"), free)
    for i in range(2):
        m = g.dve.do(lambda e, i=i: e.tensor_tensor(lam_in[:, 2 * i, :], lam_in[:, 2 * i, :], lam_in[:, 2 * i + 1, :], mul), small_loaded)
        m = g.dve.do(lambda e, i=i: e.tensor_reduce(lam[:, i:i + 1], lam_in[:, 2 * i, :], AX.X, add), m)
    m = g.act.do(lambda e: e.activation(lam[:, 2:4], lam[:, 0:2], ACT.Exp), m)
    m = g.dve.do(lambda e: e.tensor_tensor(lam[:, 4:5], lam[:, 3:4], lam[:, 2:3], sub), m)
    lam_ready = g.dve.do(lambda e: e.tensor_scalar(lam[:, 5:6], lam[:, 4:5], LAM_INIT, None, sub), m)

    plain_free, part_free = [None, None], [None, None]
    head_used, qk_ready = {}, {}

    def rope(h, which, plain_ready):
        s, b = which, g.take_bank()
        x = g.normed[:, s, :]
        mm = g.pe.do(lambda e: e.matmul(g.bank[b][:, :], rotate[:, :], plain[:, s, :], start=True, stop=True), plain_ready, g.bank_free[b], small_loaded)
        a = g.pool.do(lambda e: e.tensor_tensor(x, plain[:, s, :], cos[:, :], mul), plain_ready, tables_ready, g.normed_free[s])
        plain_free[s] = [mm, a]
        g.bank_free[b] = c = g.dve.do(lambda e: e.tensor_tensor(turned_part[:, s, :], g.bank[b][:, :], sin[:, :], mul), mm, tables_ready, part_free[s], free)
        part_free[s] = m = g.pool.do(lambda e: e.tensor_tensor(x, x, turned_part[:, s, :], add), a, c)
        g.normed_free[s] = m = g.split_into(x, qk_hi[:, which, h % 3, :], qk_lo[:, which, h % 3, :], m, head_used.get(h - 3), free)
        qk_ready.setdefault(h, []).append(m)

    pending = []
    started = set()

    def heads(first, last):
        for h in range(first, last):
            for which in range(2):
                steps = g.feature_steps("diff_w_qkv_2", D * which + P * h, KT, g.x_hi, g.x_lo, g.x_ready)
                for _ in range(3):
                    yield next(steps)
                if pending:
                    rope(*pending.pop())
                b, done = yield from steps
                if which == 0:
                    started.add(h)
                g.bank_free[b] = m = g.dve.do(lambda e, which=which, b=b: e.tensor_tensor(plain[:, which, :], g.bank[b][:, :], scale_row, mul),
                                              done, g.scale_ready, free, plain_free[which])
                pending.append((h, which, m))
                yield
        if last == DIFF_HEADS:
            rope(*pending.pop())
            started.add(last)

    for _ in heads(0, 1):
        pass
    for half in range(2):
        banks, done = g.project_tokens("diff_w_qkv_2", 2 * D + 512 * half, 512, g.x_hi, g.x_lo, g.x_ready)
        if half == 0:
            rope(*pending.pop())
        for t in range(TT):
            g.bank_free[banks[t]] = v_ready = g.act.do(lambda e, t=t, half=half, b=banks[t]: e.activation(
                v[:, t, 512 * half:512 * (half + 1)], g.bank[b][:, :], ACT.Copy, scale=g.rms[:, 2, t:t + 1]), done, g.column_ready, free)
    g.ring_banks = 2
    units = [(h, t) for h in range(DIFF_HEADS) for t in range(TT)]
    probs_free, mixed_free, turned_free = [None] * 3, [None] * 2, [None] * 2
    highest, summed, mixed_ready, turned_ready, squared = {}, {}, {}, {}, {}
    scaled = []
    scale = hd ** -0.5
    by_head = lambda x: x.rearrange("p h t -> p (h t)")

    def scores(n):
        h, t = units[n]
        for c in range(2):
            b = 2 + (2 * n + c) % 3
            rows = slice(hd * c, hd * (c + 1))
            emits = [lambda e, b=b, rows=rows, q=q, k=k, i=i: e.matmul(
                g.bank[b][:, :], q[rows, 0, h % 3, P * t:P * (t + 1)], k[rows, 1, h % 3, :], start=(i == 0), stop=(i == 2))
                for i, (q, k) in enumerate(((qk_hi, qk_hi), (qk_hi, qk_lo), (qk_lo, qk_hi)))]
            head_used[h] = mm = g.pe.do_all(emits, g.bank_free[b], qk_ready[h])
            m = g.dve.do(lambda e, b=b, c=c: e.tensor_reduce(stats[:, 0, h, t, c:c + 1], g.bank[b][:, :], AX.X, ALU.max), mm, free)
            highest[n, c] = g.dve.do(lambda e, c=c: e.tensor_scalar(stats[:, 1, h, t, c:c + 1], stats[:, 0, h, t, c:c + 1], -scale, None, mul), m)
            if c == 0:
                exponentials(n, c)

    def exponentials(n, c):
        h, t = units[n]
        b = 2 + (2 * n + c) % 3
        g.bank_free[b] = summed[n] = g.act.do(lambda e: e.activation(
            probs[:, n % 3, c, :], g.bank[b][:, :], ACT.Exp, bias=stats[:, 1, h, t, c:c + 1], scale=scale,
            accum_out=stats[:, 2, h, t, c:c + 1]), highest[n, c], probs_free[n % 3], tables_ready)

    def mix(n):
        h, t = units[n]
        st = lambda i, c: stats[:, i, h, t, c:c + 1]
        m = g.dve.do(lambda e: e.reciprocal(stats[:, 3, h, t, :], stats[:, 2, h, t, :]), summed[n])
        m = g.dve.do(lambda e: e.tensor_scalar(st(4, 0), st(3, 1), st(2, 0), lam[:, 5:6], mul, mul), m, lam_ready)
        probs_free[n % 3] = mixed_ready[n] = g.dve.do(lambda e: e.scalar_tensor_tensor(
            mixed[:, n % 2, :], probs[:, n % 3, 1, :], st(4, 0), probs[:, n % 3, 0, :], mul, add), m, mixed_free[n % 2])

    def turn(n):
        mixed_free[n % 2] = mm = transpose_tiles(g, mixed[:, n % 2, :], TT, 5, mixed_ready[n])
        g.bank_free[5] = turned_ready[n] = g.act.do(lambda e: e.activation(turned[:, n % 2, :], g.bank[5][:, :], ACT.Copy), mm, turned_free[n % 2], free)

    def values(n):
        h, t = units[n]
        ob = 6 + h % 2
        emits = [lambda e, j=j: e.matmul(g.bank[ob][:, P * t:P * (t + 1)], turned[:, n % 2, P * j:P * (j + 1)], v[:, j, P * h:P * (h + 1)],
                                         start=(j == 0), stop=(j == TT - 1)) for j in range(TT)]
        turned_free[n % 2] = mm = g.pe.do_all(emits, turned_ready[n], v_ready, g.bank_free[ob] if t == 0 else None)
        if t < TT - 1:
            return
        tiles = lambda x: x.rearrange("p (t d) -> p t d", d=P)
        o = out[:, :, P * h:P * (h + 1)]
        s = h % 2
        g.bank_free[ob] = m = g.dve.do(lambda e: e.tensor_tensor(o, tiles(g.bank[ob][:, :]), stats[:, 3, h, :, 0:1].broadcast_to([P, TT, P]), mul), mm)
        m = g.pool.do(lambda e: e.tensor_tensor(tiles(g.square[:, s, :]), o, o, mul), m, g.square_free[s])
        g.square_free[s] = squared[h] = g.dve.do(lambda e: e.tensor_reduce(rms[:, 0, h, :], tiles(g.square[:, s, :]), AX.X, add), m)

    def sub_norm(first, last):
        hs, n = slice(first, last), (last - first) * TT
        _, m = g.token_scales(by_head(rms[:, 0, hs, :]), n, P, SUBLN_EPS, squared[last - 1], *(by_head(rms[:, i, hs, :]) for i in (2, 0, 1)))
        for h in range(first, last):
            o = out[:, :, P * h:P * (h + 1)]
            lane = g.pool if h % 2 or last < DIFF_HEADS else g.dve
            scaled.append(lane.do(lambda e, o=o, h=h: e.tensor_tensor(o, o, rms[:, 2, h, :].unsqueeze(2).broadcast_to([P, TT, P]), mul), m))
            yield

    def attention():
        norming = iter(())
        for i in range(len(units) + 3):
            if i < len(units):
                while units[i][0] + 1 not in started:
                    yield False
                scores(i)
                yield True
            next(norming, None)
            if 2 <= i < len(units) + 2:
                turn(i - 2)
            if i < len(units):
                exponentials(i, 1)
            if 1 <= i < len(units) + 1:
                mix(i - 1)
            yield True
            if i >= 3:
                values(i - 3)
                if units[i - 3] == (4, 0):
                    norming = sub_norm(0, 4)
            yield True
        for _ in sub_norm(4, DIFF_HEADS):
            pass

    run_together(heads(1, DIFF_HEADS), attention(), 1)
    inner.close()
    g.ring_banks = RING_BANKS
    free = g.fence()
    o_hi = g.tile("diff_o_hi", [P, KT, T], F32R, outer)
    o_lo = g.tile("diff_o_lo", [P, KT, T], F32R, outer)
    o_ready = [to_features(g, lambda t, h=h: out[:, t, P * h:P * (h + 1)], h, o_hi, o_lo, scaled[h], free, g.subln_gain[:, 0:1]) for h in range(KT)]
    g.add_to_residual("diff_w_o_2", KT, o_hi, o_lo, o_ready)
    outer.close()


def final_norm(g):
    scales = g.norm_scales()
    stores = [Transfers(g.sem(f"stored{i}")) for i in range(2)]
    marks = []
    for k in range(KT):
        s = k % 2
        x = g.normed[:, s, :]
        full = g.dve.do(lambda e, x=x, k=k: e.scalar_tensor_tensor(
            x, g.residual[:, k, :], g.norm_gain[:, NORM_OF["final"], k:k + 1], g.bank[6][:, :], ALU.mult, ALU.mult),
            scales, g.normed_free[s])
        g.normed_free[s] = stores[s].start(g.sp, g.dram["out"][P * k:P * (k + 1), :], x, full)
        marks.append(g.normed_free[s])
    g.sp.wait(marks)


def norm_between(g):
    scales = g.norm_scales()
    for k in range(KT):
        mark = g.dve.do(lambda e, k=k: e.scalar_tensor_tensor(
            g.residual[:, k, :], g.residual[:, k, :], g.norm_gain[:, NORM_OF["between"], k:k + 1], g.bank[6][:, :], ALU.mult, ALU.mult), scales)
        g.residual_done(k, mark, None)
    g.bank_free[6] = mark


MIXERS = {"between": norm_between, "even": even_mixer, "odd": odd_mixer, "pool": pool_mixer, "diff": diff_mixer}


def build(nc, dram, stages):
    units = [unit for stage in stages for unit in stage_units(stage)]
    with ExitStack() as ctx:
        g = Program(nc, ctx, dram, units)
        consts = {}
        for name, shape, dtype in (("lower_bounds", [P, 2, HG_HEADS], F32), ("hgrn_gain", [P, 1], F32), ("ret_gain", [P, 1], F32),
                                   ("pool_scale", [P, KT], F32), ("conv_w", [P, 6, HT], F32),
                                   ("conv_b", [P, 2, HT], F32), ("subln_gain", [P, 1], F32), ("inv_freq", [P, 1], F32),
                                   ("head_rms", [P, 3, 2 * HG_HEADS * TT], F32)):
            consts[name] = g.tile(name, shape, dtype)
        (g.lower_bounds, g.hgrn_gain, g.ret_gain, g.pool_scale, g.conv_w, g.conv_b, g.subln_gain, g.inv_freq,
         g.head_rms) = consts.values()
        for k in range(KT):
            g.constants.start(g.act, g.residual[:, k, :], dram["x"][P * k:P * (k + 1), :])
        full = lambda t: t[tuple(slice(None) for _ in t.shape)]
        for name in ("norm_gain", "ident", "ones"):
            consts[name] = {"norm_gain": g.norm_gain, "ident": g.ident, "ones": g.ones}[name]
        del consts["head_rms"]
        for name, t in consts.items():
            g.constants.start(g.sp, full(t), dram[name])
        g.const_ready = (g.constants.sem, g.constants.count)
        g.dve.do(lambda e: e.tensor_scalar(g.subln_gain[:, :], g.subln_gain[:, :], 1.0 - LAM_INIT, None, ALU.mult), g.const_ready)
        g.start_weights()
        g.next_stage = stages[0]
        for k in range(KT):
            g.residual_done(k, g.const_ready, None)
        for i, stage in enumerate(stages):
            g.next_stage = stages[i + 1] if i + 1 < len(stages) else "final"
            if stage in MIXERS:
                MIXERS[stage](g)
            else:
                feed_forward(g, stage)
        assert g.unit_at == len(units)
        final_norm(g)

        block = ctx.enter_context(nc.Block())

        @block.sync
        def _(e):
            g.sp.run(e)

        @block.scalar
        def _(e):
            g.act.run(e)

        @block.vector
        def _(e):
            g.dve.run(e)

        @block.gpsimd
        def _(e):
            g.pool.run(e)

        @block.tensor
        def _(e):
            g.pe.run(e)


def shape_constants():
    p = np.arange(P)
    i = np.arange(T)
    gamma = 1.0 - 2.0 ** (-5.0 - np.arange(HG_HEADS))
    dist = i[None, :] - p[:, None]
    ret = np.where(dist[None] >= 0, gamma[:, None, None] ** np.maximum(dist, 0)[None], 0.0) * P ** -0.5
    mask = np.zeros((P, 7, 64), np.int32)
    for level, s in enumerate((64, 32, 16, 8, 4, 2, 1)):
        for c in range(64):
            start = (c // s) * 2 * s
            mask[start:start + s, level, c] = 1
    slopes = 2.0 ** (-8.0 * np.arange(1, NSA_HEADS + 1) / NSA_HEADS)
    slopes = slopes.astype(np.float32)
    back = (p[:, None] + T - P - i[None, :]).astype(np.float32)
    alibi = np.where(back[:, None, :] >= 0, slopes[None, :, None] * back[:, None, :], np.float32(MASKED))
    c_end = np.arange(NCP) * CMP_STRIDE + CMP_BLOCK - 1
    tok = (P * np.arange(TT)[None, :] + p[:, None]).astype(np.float32)
    far = tok[:, :, None] - c_end[None, None, :]
    valid = (far >= 0) & (np.arange(NCP) < NC)
    bias = np.where(valid[:, :, None, :], slopes[None, None, :, None] * far[:, :, None, :], MASKED)
    share = np.zeros((P, len(POOL_WINDOWS), T), np.float32)
    for n, w in enumerate(POOL_WINDOWS):
        share[:, n, :] = 1.0 / (np.clip(i + w - w // 2, 0, T) - np.clip(i - w // 2, 0, T))
    inv = np.float32(ROPE_THETA) ** (-np.arange(0, 64, 2, dtype=np.float32) / np.float32(64))
    rot = np.zeros((P, P), np.float32)
    for m in range(P):
        if m % 64 < 32:
            rot[m + 32, m] = -1.0
        else:
            rot[m - 32, m] = 1.0
    f = lambda a: np.ascontiguousarray(a, np.float32)
    return {"ret_decay": f(ret.transpose(1, 0, 2)), "level_mask": mask, "alibi": f(alibi), "cmp_bias": f(bias),
            "cmp_valid": f(valid), "pool_share": share, "inv_freq": f(np.tile(inv, 4)[:, None]), "rope_rotate": rot,
            "ident": np.eye(P, dtype=np.float32), "ones": np.ones((P, 1), np.float32)}


def by_feature(v):
    v = np.asarray(v)
    return np.ascontiguousarray(np.moveaxis(v.reshape(v.shape[:-1] + (-1, P)), -1, 0))


def lay_out(inputs, stages):
    a = {k: np.asarray(v) for k, v in inputs.items()}
    units = [unit for stage in stages for unit in stage_units(stage)]
    weights = np.zeros((len(units), P, UNIT), np.float32)
    for n, (name, layer, k0, k, c0, c) in enumerate(units):
        w = a[name][layer if name != "pool_w_2" else 0]
        if name == "pool_w_2":
            w = w[layer]
        pieces = c0 if isinstance(c0, tuple) else ((c0, c),)
        rows = w[k0 * P:(k0 + k) * P]
        block = np.concatenate([rows[:, a:a + n_cols] for a, n_cols in pieces], axis=1).reshape(k, P, c).transpose(1, 0, 2)
        weights[n, :, 0:k * c] = block.reshape(P, k * c)
    w1 = np.zeros((2, P, CMP_BLOCK, P), np.float32)
    w2 = np.zeros((P, 2, P), np.float32)
    pos = np.zeros((P, 2, CMP_BLOCK), np.float32)
    for i, kind in enumerate("kv"):
        m1 = a[f"cmp_w1_{kind}"][0].reshape(CMP_BLOCK, NSA_HD, NSA_HD).transpose(1, 0, 2)
        for grp in range(GROUPS):
            rows = slice(64 * grp, 64 * grp + 64)
            w1[i, rows, :, rows] = m1
            w2[rows, i, rows] = a[f"cmp_w2_{kind}"][0]
            pos[rows, i, :] = a[f"cmp_pos_{kind}"][0].T
    norms = np.stack([a["mix_norm"][0], a["ffn_norm"][0], a["mix_norm"][1], a["ffn_norm"][1],
                      a["mix_norm_2"][0], a["ffn_norm_2"][0], a["mix_norm_2"][1], a["ffn_norm_2"][1], a["final_norm"], a["final_norm_2"]])
    arrays = {
        "x": np.ascontiguousarray(a["x"][0].T), "weights": weights, "norm_gain": by_feature(norms),
        "lower_bounds": by_feature(a["hgrn_lower_bounds"]),
        "hgrn_gain": np.ascontiguousarray(a["hgrn_out_norm"][0][:, None]), "ret_gain": np.ascontiguousarray(a["ret_out_norm"][0][:, None]),
        "pool_scale": by_feature(a["pool_scale_2"][0]),
        "conv_w": by_feature(a["ffn_conv_w_2"].reshape(6, FFN2)), "conv_b": by_feature(a["ffn_conv_b_2"]),
        "subln_gain": np.ascontiguousarray(a["diff_subln_2"][0][:, None]),
        "diff_lam": np.ascontiguousarray(np.broadcast_to(np.stack([a[f"diff_lam_{n}_2"][0] for n in ("q1", "k1", "q2", "k2")]), (P, 4, 64))),
        "positions": np.ascontiguousarray(np.broadcast_to(a["positions_2"], (P, T))),
        "cmp_w1": w1, "cmp_w2": w2, "cmp_pos": pos,
    }
    arrays.update(shape_constants())
    return arrays


def kernel(**inputs):
    import concourse.bacc as _bacc
    from concourse.bass_utils import run_bass_kernel_spmd as _run

    arrays = lay_out(inputs, STAGES)
    nc = _bacc.Bacc("TRN2", target_bir_lowering=False, num_devices=1)
    dram = {name: nc.dram_tensor("in_" + name, a.shape, mybir.dt.from_np(a.dtype), kind="ExternalInput").ap() for name, a in arrays.items()}
    dram["out"] = nc.dram_tensor("out", (D, T), F32, kind="ExternalOutput").ap()
    build(nc, dram, STAGES)
    results = _run(nc, [{"in_" + name: a for name, a in arrays.items()}], core_ids=[0])
    return np.ascontiguousarray(results.results[0]["out"].T)[None]
```

```python
from contextlib import ExitStack
import math

import numpy as np
import concourse.bass as bass
from concourse import mybir

F32 = mybir.dt.float32
F32R = mybir.dt.float32r
I32 = mybir.dt.int32
ACT = mybir.ActivationFunctionType
ALU = mybir.AluOpType
AX = mybir.AxisListType

P = 128
T = 512
D = 1024
KT = D // P
TT = T // P
UNIT = 1024
RAW_SLOTS = 3
SPLIT_SLOTS = 3
RING_BANKS = 6

EPS = 1e-6
SUBLN_EPS = 1e-5
HG_HEADS = 4
CHUNK = 128
NSA_HEADS, NSA_HD, GROUPS = 16, 64, 2
KVW = GROUPS * NSA_HD
CMP_BLOCK, CMP_STRIDE = 32, 16
NC = T // CMP_STRIDE - CMP_BLOCK // CMP_STRIDE + 1
NCP = 32
MASKED = 1e30
ODD_KC, ODD_VC, ODD_KS, ODD_VS, ODD_KW, ODD_VW, ODD_GATES = (D + KVW * i for i in range(7))
ODD_VALUES = ((ODD_VS, KVW), (ODD_VW, KVW + 3 * NSA_HEADS))
ODD_VALUE_COLUMNS = 2 * KVW + 3 * NSA_HEADS
FFN1, FFN2 = 2816, 2816
HT = FFN1 // P
POOL_WINDOWS = (2, 4, 8, 16)
PAD = max(POOL_WINDOWS)
DIFF_HEADS = 8
LAM_INIT = 0.8 - 0.6 * math.exp(-0.3 * 1)
ROPE_THETA = 10000.0

STAGES = ("even", "ffn_a", "odd", "ffn_b", "pool", "ffn_c", "diff", "ffn_d")
NORM_OF = {"even": 0, "ffn_a": 1, "odd": 2, "ffn_b": 3, "pool": 4, "ffn_c": 5, "diff": 6, "ffn_d": 7, "first_final": 8, "final": 9}


PREPARED = ("even", "ffn_a", "odd", "ffn_b", "ffn_c", "diff", "ffn_d")


def feature_units(matrix, layer, column, k_tiles):
    return [(matrix, layer, k, min(UNIT // P, k_tiles - k), column, P) for k in range(0, k_tiles, UNIT // P)]


def token_units(matrix, layer, column, columns, k_tiles):
    return [(matrix, layer, k, 2, column, columns) for k in range(0, k_tiles, 2)]


def stage_units(stage):
    units = []
    if stage == "even":
        hq, hf, hi, hg, rq, rk, rv, rg = (512 * i for i in range(8))
        heads = lambda *bases: [u for base in bases for h in range(HG_HEADS) for u in feature_units("even_w_in", 0, base + P * h, KT)]
        units += heads(hf, hq, rq, rk)
        units += token_units("even_w_in", 0, hi, 512, KT) + token_units("even_w_in", 0, rv, 512, KT)
        units += heads(hg, rg)
        for n in range(KT):
            units += feature_units("even_w_out", 0, P * n, KT)
    if stage == "odd":
        for col in (ODD_KC, ODD_VC, ODD_KS, ODD_KW):
            units += feature_units("odd_w_in", 0, col, KT)
        units += token_units("odd_w_in", 0, ODD_VALUES, ODD_VALUE_COLUMNS, KT)
        for n in range(KT):
            units += feature_units("odd_w_in", 0, P * n, KT)
        for n in range(KT):
            units += feature_units("odd_w_out", 0, P * n, KT)
    if stage in ("ffn_a", "ffn_b", "ffn_c", "ffn_d"):
        up, down = ("ffn_w_gate_up", "ffn_w_down") if stage in ("ffn_a", "ffn_b") else ("ffn_w_up_2", "ffn_w_down_2")
        layer = 0 if stage in ("ffn_a", "ffn_c") else 1
        for j in range(HT):
            units += feature_units(up, layer, P * j, KT) + feature_units(up, layer, FFN1 + P * j, KT)
        for n in range(KT):
            units += feature_units(down, layer, P * n, HT)
    if stage == "pool":
        for g in range(len(POOL_WINDOWS)):
            units += [("pool_w_2", g, 0, 2, 0, 256)]
    if stage == "diff":
        head = lambda h: feature_units("diff_w_qkv_2", 0, P * h, KT) + feature_units("diff_w_qkv_2", 0, D + P * h, KT)
        units += head(0)
        for half in range(2):
            units += token_units("diff_w_qkv_2", 0, 2 * D + 512 * half, 512, KT)
        for h in range(1, DIFF_HEADS):
            units += head(h)
        for n in range(KT):
            units += feature_units("diff_w_o_2", 0, P * n, KT)
    return units


class Lane:
    def __init__(self, sem):
        self.sem, self.count, self.queue, self.reached = sem, 0, [], {}

    def wait(self, *marks):
        for mark in marks:
            if mark is None:
                continue
            if isinstance(mark, list):
                self.wait(*mark)
                continue
            sem, value = mark
            if value > self.reached.get(sem.name, 0):
                self.reached[sem.name] = value
                self.queue.append(lambda e, s=sem, v=value: e.wait_ge(s, v))

    def put(self, emit):
        self.queue.append(emit)

    def do(self, emit, *after):
        self.wait(*after)
        self.count += 1
        self.queue.append(lambda e: emit(e).then_inc(self.sem, 1))
        return self.mark()

    def do_all(self, emits, *after):
        self.wait(*after)
        for emit in emits[:-1]:
            self.put(emit)
        return self.do(emits[-1])

    def mark(self):
        return (self.sem, self.count) if self.count else None

    def run(self, engine):
        for emit in self.queue:
            emit(engine)


class Transfers:
    def __init__(self, sem):
        self.sem, self.count = sem, 0

    def start(self, lane, dst, src, *after):
        lane.wait(*after)
        self.count += 16
        lane.put(lambda e: e.dma_start(dst, src).then_inc(self.sem, 16))
        return (self.sem, self.count)


class Program:

    def __init__(self, nc, ctx, dram, units):
        self.nc, self.ctx, self.dram, self.units = nc, ctx, dram, units
        self.pe, self.dve, self.act, self.pool, self.sp = (
            Lane(self.sem(f"{n}_done")) for n in ("pe", "dve", "act", "pool", "sp"))
        self.bank = [ctx.enter_context(nc.psum_tensor(f"bank{i}", [P, 512], F32)) for i in range(8)]
        self.bank_free = [None] * 8
        self.ring_at = 0
        self.open_banks = []
        self.errands = []
        self.ring_banks = RING_BANKS
        self.residual = self.tile("residual", [P, KT, T], F32)
        self.residual_ready = [None] * KT
        self.norm_gain = self.tile("norm_gain", [P, 10, KT], F32)
        self.ident = self.tile("ident", [P, P], F32)
        self.ones = self.tile("ones", [P, 1], F32)
        self.square = self.tile("square", [P, 2, T], F32)
        self.square_free = [None, None]
        self.square_sum = self.tile("square_sum", [P, T], F32)
        self.gain_product = self.tile("gain_product", [P, KT], F32)
        self.window_share = self.tile("window_share", [P, len(POOL_WINDOWS), 2, PAD], F32)
        self.sum_free = None
        self.x_hi = self.tile("x_hi", [P, KT, T], F32R)
        self.x_lo = self.tile("x_lo", [P, KT, T], F32R)
        self.x_ready = [None] * KT
        self.scale_rows = self.tile("scale_rows", [P, 2, T], F32)
        self.layer = -1
        self.normed = self.tile("normed", [P, 2, T], F32)
        self.normed_free = [None, None]
        self.rms = self.tile("rms", [P, 5, TT], F32)
        self.last_layer_done = None
        self.constants = Transfers(self.sem("constants_loaded"))
        self.raw = self.tile("weight_raw", [P, RAW_SLOTS, UNIT], F32)
        self.w_hi = [self.tile(f"weight_hi{i}", [P, UNIT], F32R) for i in range(SPLIT_SLOTS)]
        self.w_lo = [self.tile(f"weight_lo{i}", [P, UNIT], F32R) for i in range(SPLIT_SLOTS)]
        self.raw_loads = [Transfers(self.sem(f"weights_loaded{i}")) for i in range(RAW_SLOTS)]
        self.low_part = None
        self.loaded, self.is_split, self.used = {}, {}, {}
        self.unit_at = 0

    def sem(self, name):
        return self.ctx.enter_context(self.nc.semaphore(name))

    def tile(self, name, shape, dtype, scope=None):
        return (scope or self.ctx).enter_context(self.nc.sbuf_tensor(name, shape, dtype))

    def load(self, name, lane, moves, *after):
        transfers = Transfers(self.sem(name + "_loaded"))
        for dst, src in moves:
            mark = transfers.start(lane, dst, src, *after)
        return mark

    def fence(self):
        return [lane.mark() for lane in (self.pe, self.dve, self.act, self.pool)]

    def take_bank(self):
        i = self.ring_at % self.ring_banks
        while i in self.open_banks:
            i = (i + 1) % self.ring_banks
        self.ring_at = i + 1
        return i

    def load_unit(self, u):
        if u >= len(self.units):
            return
        _, _, _, k, _, c = self.units[u]
        slot = u % RAW_SLOTS
        self.loaded[u] = self.raw_loads[slot].start(
            self.sp, self.raw[:, slot, 0:k * c], self.dram["weights"][u, :, 0:k * c], self.is_split.get(u - RAW_SLOTS))

    def split_unit(self, u):
        if u >= len(self.units):
            return
        _, _, _, k, _, c = self.units[u]
        raw, hi, lo = self.raw[:, u % RAW_SLOTS, 0:k * c], self.w_hi[u % SPLIT_SLOTS], self.w_lo[u % SPLIT_SLOTS]
        high = self.act.do(lambda e: e.activation(hi[:, 0:k * c], raw, ACT.Copy), self.loaded[u], self.used.get(u - SPLIT_SLOTS))

        def low():
            self.is_split[u] = self.dve.do(
                lambda e: e.tensor_tensor(lo[:, 0:k * c], raw, hi[:, 0:k * c].bitcast(F32), ALU.subtract), high)
            self.load_unit(u + RAW_SLOTS)

        self.low_part = low

    def split_low(self):
        if self.low_part:
            self.low_part()
            self.low_part = None

    def take_unit(self, matrix, column):
        u = self.unit_at
        self.unit_at += 1
        assert self.units[u][0] == matrix and self.units[u][4] == column, (self.units[u], matrix, column)
        self.split_low()
        self.split_unit(u + SPLIT_SLOTS - 1)
        _, _, _, k, _, c = self.units[u]
        view = lambda t: t[:, 0:k * c].rearrange("p (k c) -> p k c", k=k)
        return u, view(self.w_hi[u % SPLIT_SLOTS]), view(self.w_lo[u % SPLIT_SLOTS])

    def feature_steps(self, matrix, column, k_tiles, x_hi, x_lo, x_ready):
        b = self.take_bank()
        out = self.bank[b]
        self.open_banks = [b]
        self.pe.wait(self.bank_free[b])
        k0 = 0
        while k0 < k_tiles:
            u, w_hi, w_lo = self.take_unit(matrix, column)
            self.pe.wait(self.is_split[u])
            n = self.units[u][3]
            for k in range(n):
                self.pe.wait(x_ready[k0 + k])
                for i, (w, x) in enumerate(((w_hi, x_hi), (w_lo, x_hi), (w_hi, x_lo))):
                    emit = lambda e, w=w, x=x, k=k, kk=k0 + k, i=i: e.matmul(
                        out[:, :], w[:, k, :], x[:, kk, :], start=(kk == 0 and i == 0), stop=(kk == k_tiles - 1 and i == 2))
                    if k == n - 1 and i == 2:
                        self.used[u] = self.pe.do(emit)
                    else:
                        self.pe.put(emit)
                if k == 1:
                    self.split_low()
                if k0 + k == 5:
                    self.run_errand()
                if k < n - 1 or k0 + n < k_tiles:
                    yield
            k0 += n
        self.open_banks = []
        self.run_errand()
        return b, self.used[u]

    def project_features(self, *args):
        steps = self.feature_steps(*args)
        while True:
            try:
                next(steps)
            except StopIteration as end:
                return end.value

    def project_tokens(self, *args):
        steps = self.token_steps(*args)
        while True:
            try:
                next(steps)
            except StopIteration as end:
                return end.value

    def token_steps(self, matrix, column, columns, x_hi, x_lo, x_ready):
        banks = [self.take_bank() for _ in range(TT)]
        self.open_banks = banks
        self.pe.wait(*[self.bank_free[b] for b in banks])
        for k0 in range(0, KT, 2):
            u, w_hi, w_lo = self.take_unit(matrix, column)
            self.pe.wait(self.is_split[u], x_ready[k0], x_ready[k0 + 1])
            for t in range(TT):
                for k in range(2):
                    for i, (w, x) in enumerate(((w_hi, x_hi), (w_lo, x_hi), (w_hi, x_lo))):
                        emit = lambda e, w=w, x=x, k=k, kk=k0 + k, i=i, t=t: e.matmul(
                            self.bank[banks[t]][:, 0:columns], x[:, kk, P * t:P * (t + 1)], w[:, k, :],
                            start=(kk == 0 and i == 0), stop=(kk == KT - 1 and i == 2))
                        last = k == 1 and i == 2 and t == TT - 1
                        if last:
                            self.used[u] = self.pe.do(emit)
                        else:
                            self.pe.put(emit)
                if t == 0:
                    self.split_low()
                yield
        self.open_banks = []
        return banks, self.used[u]

    def tokens_out(self, banks, done, out, free):
        marks = []
        for t, b in enumerate(banks):
            dst, src, scale = out(t), self.bank[b][:, :], self.rms[:, 2, t:t + 1]
            if t % 2:
                m = self.dve.do(lambda e, dst=dst, src=src, scale=scale: e.tensor_scalar(dst, src, scale, None, ALU.mult), done, self.column_ready, free)
            else:
                m = self.act.do(lambda e, dst=dst, src=src, scale=scale: e.activation(dst, src, ACT.Copy, scale=scale), done, self.column_ready, free)
            self.bank_free[b] = m
            marks.append(m)
        return marks

    def add_square(self, k):
        s = k % 2
        if self.next_stage == "pool":
            gain = self.norm_gain[:, NORM_OF["first_final"], k:k + 1]
            dst = self.normed[:, 1 if k else 0, :]
            gained = self.act.do(lambda e: e.activation(dst, self.residual[:, k, :], ACT.Square, scale=gain), self.residual_ready[k], self.normed_free)
            if k:
                gained = self.dve.do(lambda e: e.tensor_tensor(self.normed[:, 0, :], self.normed[:, 0, :], dst, ALU.add), gained)
            self.normed_free = [gained, gained]
        if k == 0:
            self.summed = self.act.do(lambda e: e.activation(self.square_sum[:, :], self.residual[:, k, :], ACT.Square),
                                      self.residual_ready[k], self.sum_free)
            return
        squared = self.act.do(lambda e: e.activation(self.square[:, s, :], self.residual[:, k, :], ACT.Square),
                              self.residual_ready[k], self.square_free[s])
        lane = self.dve if self.layer < 0 else self.pool
        self.summed = self.square_free[s] = lane.do(lambda e: e.tensor_tensor(
            self.square_sum[:, :], self.square_sum[:, :], self.square[:, s, :], ALU.add), squared, self.summed)
        if k == KT - 1:
            self.errands = [None, self.sum_features]

    def sum_features(self):
        emits = [lambda e, t=t: e.matmul(self.bank[7][:, t:t + 1], self.square_sum[:, P * t:P * (t + 1)], self.ones[:, :],
                                         start=True, stop=True) for t in range(TT)]
        self.sum_free = self.pe.do_all(emits, self.summed, self.bank_free[7], self.const_ready)
        read, self.column_ready = self.token_scales(self.bank[7][:, 0:TT], TT, D, EPS, self.sum_free, self.rms[:, 2, :], self.rms[:, 0, :], self.rms[:, 1, :])
        self.bank_free[7] = read

    def run_errand(self):
        if self.errands:
            errand = self.errands.pop(0)
            if errand:
                errand()

    def token_scales(self, sums, n, count, eps, done, out, tmp, tmp2, free=None):
        mean = self.dve.do(lambda e: e.tensor_scalar(tmp, sums, 1.0 / count, eps, ALU.mult, ALU.add), done, free)
        root = self.act.do(lambda e: e.activation(tmp2, tmp, ACT.Sqrt), mean)
        return mean, self.dve.do(lambda e: e.reciprocal(out, tmp2), root)

    def spread_scales(self, column, bank, ready):
        self.pe.wait(self.bank_free[bank], ready, self.const_ready)
        for t in range(TT):
            emit = lambda e, t=t: e.matmul(self.bank[bank][:, P * t:P * (t + 1)], column(t).broadcast_to([P, P]),
                                           self.ident[:, :], start=True, stop=True)
            if t < TT - 1:
                self.pe.put(emit)
            else:
                return self.pe.do(emit)

    def norm_scales(self):
        while self.errands:
            self.run_errand()
        return self.spread_scales(lambda t: self.rms[:, 2, t:t + 1], 6, self.column_ready)

    def begin_layer(self):
        self.layer += 1
        row = self.scale_rows[:, self.layer % 2, :]
        free, self.last_layer_done = self.last_layer_done, self.fence()

        def spread():
            done = self.spread_scales(lambda t: self.rms[:, 2, t:t + 1], 6, self.column_ready)
            self.scale_ready = self.bank_free[6] = self.act.do(lambda e: e.activation(row, self.bank[6][:, :], ACT.Copy), done, free)

        self.errands.append(spread)
        return row

    def split_into(self, x, hi, lo, ready, *free):
        high = self.act.do(lambda e: e.activation(hi, x, ACT.Copy), ready, *free)
        return self.dve.do(lambda e: e.tensor_tensor(lo, x, hi.bitcast(F32), ALU.subtract), high)

    def split_scaled(self, x, gain, hi, lo, ready, *free):
        high = self.act.do(lambda e: e.activation(hi, x, ACT.Copy, scale=gain), ready, *free)
        return self.dve.do(lambda e: e.scalar_tensor_tensor(lo, x, gain, hi.bitcast(F32), ALU.mult, ALU.subtract), high)

    def residual_done(self, n, mark, x_free, later=None):
        self.residual_ready[n] = mark
        if self.next_stage in PREPARED:
            x, gain, hi, lo = (self.residual[:, n, :], self.norm_gain[:, NORM_OF[self.next_stage], n:n + 1],
                               self.x_hi[:, n, :], self.x_lo[:, n, :])
            if later is None:
                self.x_ready[n] = self.split_scaled(x, gain, hi, lo, mark, x_free, self.gain_ready)
            else:
                high = self.act.do(lambda e: e.activation(hi, x, ACT.Copy, scale=gain), mark, x_free)

                def low():
                    self.x_ready[n] = self.dve.do(lambda e: e.scalar_tensor_tensor(lo, x, gain, hi.bitcast(F32), ALU.mult, ALU.subtract), high)
                later.append(low)
        if n:
            self.add_square(n - 1)
        if n == KT - 1:
            self.add_square(n)

    def add_to_residual(self, matrix, k_tiles, x_hi, x_lo, x_ready):
        x_free = self.pe.mark()
        for n in range(KT):
            b, done = self.project_features(matrix, P * n, k_tiles, x_hi, x_lo, x_ready)
            self.bank_free[b] = mark = self.dve.do(
                lambda e, n=n, b=b: e.tensor_tensor(self.residual[:, n, :], self.residual[:, n, :], self.bank[b][:, :], ALU.add), done)
            self.residual_done(n, mark, x_free)


def run_between(front, back, every):
    for i, _ in enumerate(front):
        if i % every == every - 1:
            next(back, None)
    for _ in back:
        pass


def run_together(front, back, per_step):
    for _ in front:
        for _ in range(per_step):
            if next(back, None) is False:
                break
    for _ in back:
        pass


def feed_forward(g, stage):
    swiglu = stage in ("ffn_a", "ffn_b")
    layer = 0 if stage in ("ffn_a", "ffn_c") else 1
    up, down = ("ffn_w_gate_up", "ffn_w_down") if swiglu else ("ffn_w_up_2", "ffn_w_down_2")
    with ExitStack() as scope:
        free = g.fence()
        h_hi = g.tile(f"{stage}_h_hi", [P, HT, T], F32R, scope)
        h_lo = g.tile(f"{stage}_h_lo", [P, HT, T], F32R, scope)
        gate = g.tile(f"{stage}_gate", [P, T], F32, scope)
        opened = g.tile(f"{stage}_opened", [P, 2, T], F32, scope)
        hidden = g.tile(f"{stage}_hidden", [P, 2, T], F32, scope)
        scale_row = g.begin_layer()
        gate_free, opened_free, hidden_free, h_ready = None, [None, None], [None, None], []
        for j in range(HT):
            s = j % 2
            bg, gate_done = g.project_features(up, P * j, KT, g.x_hi, g.x_lo, g.x_ready)
            bu, up_done = g.project_features(up, FFN1 + P * j, KT, g.x_hi, g.x_lo, g.x_ready)
            acc, u, op, hd = g.bank[bg], g.bank[bu], opened[:, s, :], hidden[:, s, :]
            g.bank_free[bg] = scaled = g.dve.do(lambda e, acc=acc: e.tensor_tensor(gate[:, :], acc[:, :], scale_row, ALU.mult),
                                                gate_done, g.scale_ready, gate_free, free)
            if swiglu:
                gate_free = m = g.act.do(lambda e, op=op: e.activation(op, gate[:, :], ACT.Silu), scaled, opened_free[s], free)
            else:
                w = lambda tap, j=j: g.conv_w[:, 3 * layer + tap, j:j + 1]
                mid = g.dve.do(lambda e, op=op, w=w, j=j: e.tensor_scalar(
                    op, gate[:, :], w(1), g.conv_b[:, layer, j:j + 1], ALU.mult, ALU.add), scaled, opened_free[s], g.const_ready, free)
                left = g.dve.do(lambda e, op=op, w=w: e.scalar_tensor_tensor(
                    op[:, 1:T], gate[:, 0:T - 1], w(0), op[:, 1:T], ALU.mult, ALU.add), mid)
                gate_free = g.dve.do(lambda e, op=op, w=w: e.scalar_tensor_tensor(
                    op[:, 0:T - 1], gate[:, 1:T], w(2), op[:, 0:T - 1], ALU.mult, ALU.add), left)
                m = g.act.do(lambda e, op=op: e.activation(op, op, ACT.Gelu), gate_free)
            g.bank_free[bu] = scaled = g.dve.do(lambda e, hd=hd, u=u: e.tensor_tensor(hd, u[:, :], scale_row, ALU.mult), up_done, hidden_free[s], free)
            opened_free[s] = product = g.pool.do(lambda e, op=op, hd=hd: e.tensor_tensor(hd, op, hd, ALU.mult), m, scaled)
            hidden_free[s] = g.split_into(hd, h_hi[:, j, :], h_lo[:, j, :], product)
            h_ready.append(hidden_free[s])
        g.add_to_residual(down, HT, h_hi, h_lo, h_ready)


def hgrn_levels(g, q, k, cum, diff, k_dec, q_dec, scores, level_mask, mask_loaded, ready, state):
    blocks = HG_HEADS * TT
    pairs = lambda t, s: t.rearrange("p (n z s) -> p n z s", z=2, s=s)

    def diagonal(part):
        half = blocks // 2
        emits = []
        for m in range(half):
            c = slice(P * (half * part + m), P * (half * part + m + 1))
            out = g.bank[6 + m // 4][:, P * (m % 4):P * (m % 4 + 1)]
            emits.append(lambda e, out=out, c=c: e.matmul(out, k[:, c], q[:, c], start=True, stop=True))
        mm = g.pe.do_all(emits, g.bank_free[6], g.bank_free[7], ready)
        for b in range(2):
            c = slice(P * (half * part + 4 * b), P * (half * part + 4 * b + 4))
            state["chosen"] = g.bank_free[6 + b] = g.dve.do(lambda e, b=b, c=c: e.tensor_tensor(
                scores[:, c].rearrange("p (m i) -> p m i", m=4), g.bank[6 + b][:, :].rearrange("p (m i) -> p m i", m=4),
                g.ident[:, :].unsqueeze(1).broadcast_to([P, 4, P]), ALU.mult), mm, g.const_ready)

    def decays(s):
        n = blocks * P // (2 * s)
        c4, d4 = pairs(cum[:, :], s), pairs(diff[:, :], s)
        rel = g.dve.do(lambda e: e.tensor_tensor(
            diff[:, :].rearrange("p (n t) -> p n t", n=n), cum[:, :].rearrange("p (n t) -> p n t", n=n),
            c4[:, :, 0, s - 1:s].broadcast_to([P, n, 2 * s]), ALU.subtract), ready, state["diff_free"])
        first = g.act.do(lambda e: e.activation(d4[:, :, 0, :], d4[:, :, 0, :], ACT.Exp, scale=-1.0), rel)
        second = g.act.do(lambda e: e.activation(d4[:, :, 1, :], d4[:, :, 1, :], ACT.Exp), rel)
        return first, second

    def decayed(s, first, second):
        d4, kd4, q4, k4 = (pairs(t[:, :], s) for t in (diff, k_dec, q, k))
        k_ready = g.pool.do(lambda e: e.tensor_tensor(kd4[:, :, 0, :], k4[:, :, 0, :], d4[:, :, 0, :], ALU.mult), first, state["products"], ready)
        q_ready = g.dve.do(lambda e: e.tensor_tensor(
            q_dec[:, :].rearrange("p (n s) -> p n s", s=s), q4[:, :, 1, :], d4[:, :, 1, :], ALU.mult), second, state["products"])
        state["diff_free"] = [k_ready, q_ready]

    def products(level, s):
        emits = []
        for m in range(blocks):
            out = g.bank[6 + m // 8][:, 64 * (m % 8):64 * (m % 8 + 1)]
            emits.append(lambda e, out=out, m=m: e.matmul(
                out, k_dec[:, P * m:P * (m + 1)], q_dec[:, 64 * m:64 * (m + 1)], start=True, stop=True))
        state["products"] = mm = g.pe.do_all(emits, state["diff_free"], g.bank_free[6], g.bank_free[7])
        mask = level_mask[:, level, :].rearrange("p (n s) -> p n s", s=s).unsqueeze(1).broadcast_to([P, 8, 64 // s, s])
        for b in range(2):
            rows = slice(P * 8 * b, P * 8 * (b + 1))
            state["chosen"] = g.bank_free[6 + b] = g.dve.do(lambda e, b=b, rows=rows: e.copy_predicated(
                scores[:, rows].rearrange("p (m n z s) -> p m n z s", m=8, z=2, s=s)[:, :, :, 1, :], mask,
                g.bank[6 + b][:, :].rearrange("p (m n s) -> p m n s", m=8, s=s)), mm, mask_loaded, state["chosen"])

    state.update(diff_free=None, products=None)
    levels = list(enumerate((64, 32, 16, 8, 4, 2, 1)))
    exps = decays(levels[0][1])
    yield True
    diagonal(0)
    yield True
    decayed(levels[0][1], *exps)
    diagonal(1)
    yield True
    for level, s in levels:
        if level + 1 < len(levels):
            exps = decays(levels[level + 1][1])
            yield True
        products(level, s)
        if level + 1 < len(levels):
            decayed(levels[level + 1][1], *exps)
        yield True


def even_mixer(g):
    mul, add, sub = ALU.mult, ALU.add, ALU.subtract
    width = HG_HEADS * T
    outer = ExitStack()
    free = g.fence()
    o = g.tile("even_o", [P, KT, T], F32, outer)
    bound = g.tile("hgrn_bound", [P, 6, HG_HEADS], F32, outer)
    inner = ExitStack()
    rq, rk, hv, rv = (g.tile(n, [P, width], F32, inner) for n in ("ret_q", "ret_k", "hgrn_v", "ret_v"))
    hs = ExitStack()
    hq, hk, cum, scores, k_dec = (g.tile(n, [P, width], F32, hs) for n in ("hgrn_q", "hgrn_k", "hgrn_cum", "hgrn_scores", "hgrn_k_dec"))
    diff_and_q = g.tile("hgrn_diff_and_q_dec", [P, width + width // 2], F32, hs)
    diff, q_dec = diff_and_q[:, 0:width], diff_and_q[:, width:]
    level_mask = g.tile("hgrn_level_mask", [P, 7, 64], I32, hs)
    mask_loaded = g.load("hgrn_level_mask", g.pool, [(level_mask[:, :, :], g.dram["level_mask"])], free)
    scale_row = g.begin_layer()
    HQ, HF, HI, HG, RQ, RK, RV, RG = range(8)
    project_forget = lambda h: g.project_features("even_w_in", 512 * HF + P * h, KT, g.x_hi, g.x_lo, g.x_ready)
    projected = [project_forget(0), project_forget(1)]
    b0, b1 = g.lower_bounds[:, 0, :], g.lower_bounds[:, 1, :]
    top, e0, e1, total, low, rest = (bound[:, i, :] for i in range(6))
    m = g.dve.do(lambda e: e.tensor_tensor(top, b0, b1, ALU.max), g.const_ready, free)
    m = g.dve.do(lambda e: e.tensor_tensor(e0, b0, top, sub), m)
    m = g.dve.do(lambda e: e.tensor_tensor(e1, b1, top, sub), m)
    m = g.act.do(lambda e: e.activation(bound[:, 1:3, :], bound[:, 1:3, :], ACT.Exp), m)
    m = g.dve.do(lambda e: e.tensor_tensor(total, e0, e1, add), m)
    m = g.dve.do(lambda e: e.reciprocal(total, total), m)
    m = g.dve.do(lambda e: e.tensor_tensor(low, e0, total, mul), m)
    bound_ready = g.dve.do(lambda e: e.tensor_scalar(rest, low, -1.0, 1.0, mul, add), m)

    steps = lambda base, h: g.feature_steps("even_w_in", 512 * base + P * h, KT, g.x_hi, g.x_lo, g.x_ready)
    part = lambda t, h: t[:, T * h:T * (h + 1)]

    def scaled_to(out, b, done, *after):
        g.bank_free[b] = mark = g.dve.do(lambda e: e.tensor_tensor(out, g.bank[b][:, :], scale_row, mul), done, g.scale_ready, *after)
        return mark

    restart = g.pool.do(lambda e: e.memset(k_dec[:, :], 1.0), free)
    restart = g.pool.do(lambda e: e.memset(k_dec[:, :].rearrange("p (m t) -> p m t", t=CHUNK)[:, :, 0:1], 0.0), restart)
    for h in range(HG_HEADS):
        b, done = projected[h] if h < 2 else project_forget(h)
        m = scaled_to(part(diff, h), b, done, free)
        m = g.act.do(lambda e, h=h: e.activation(part(diff, h), part(diff, h), ACT.Sigmoid), m)
        m = g.dve.do(lambda e, h=h: e.tensor_scalar(part(diff, h), part(diff, h), rest[:, h:h + 1], low[:, h:h + 1], mul, add), m, bound_ready)
        f_ready = g.pool.do(lambda e, h=h: e.tensor_scalar(part(hk, h), part(diff, h), -1.0, 1.0, mul, add), m, free)
    for h in range(HG_HEADS):
        b, done = g.project_features("even_w_in", 512 * HQ + P * h, KT, g.x_hi, g.x_lo, g.x_ready)
        if h == 0:
            logged = g.act.do(lambda e: e.activation(diff, diff, ACT.Ln), f_ready)
        m = scaled_to(part(hq, h), b, done, free)
        q_ready = g.act.do(lambda e, h=h: e.activation(part(hq, h), part(hq, h), ACT.Silu), m)
        if h == 0:
            summed = g.dve.do(lambda e: e.tensor_tensor_scan(cum[:, :], k_dec[:, :], diff, 0.0, mul, add), logged, restart, free)
            cleared = g.pool.do(lambda e: e.memset(k_dec[:, :], 0.0), summed)

    marks = {}

    def rest_of_projections():
        for base, dst in ((RQ, rq), (RK, rk)):
            for h in range(HG_HEADS):
                b, done = yield from steps(base, h)
                marks["ret_qk"] = scaled_to(part(dst, h), b, done, free)
                yield
        for base, dst in ((HI, hv), (RV, rv)):
            banks, done = yield from g.token_steps("even_w_in", 512 * base, 512, g.x_hi, g.x_lo, g.x_ready)
            marks.setdefault("v", []).append(g.tokens_out(banks, done, lambda t: part(dst, t), free))
            yield

    state = {}
    across = g.head_rms[:, 0, 0:HG_HEADS * TT]
    tiles = lambda t: t.rearrange("p (m t) -> p m t", t=P)
    heads = lambda t: t.rearrange("p (h m t) -> p h m t", h=HG_HEADS, t=P)
    k_far = cum[:, 0:3 * HG_HEADS * P].rearrange("p (h i t) -> p h i t", h=HG_HEADS, i=3)
    cross = diff_and_q[:, :].rearrange("p (h i t) -> p h i t", h=HG_HEADS, i=6)

    def within_and_ends():
        yield from hgrn_levels(g, hq, hk, cum, diff, k_dec, q_dec, scores, level_mask, mask_loaded, [summed, cleared, q_ready, f_ready], state)
        ends = tiles(cum[:, :])[:, :, P - 1:P]
        m = g.act.do(lambda e: e.activation(diff, cum[:, :], ACT.Exp), state["diff_free"])
        whole = g.act.do(lambda e: e.activation(across, ends.rearrange("p m o -> p (m o)"), ACT.Exp), summed)
        yield True
        state["q_start"] = g.dve.do(lambda e: e.tensor_tensor(k_dec[:, :], hq[:, :], diff, mul), m, state["products"])
        m = g.dve.do(lambda e: e.tensor_tensor(tiles(diff), tiles(cum[:, :]), ends.broadcast_to([P, HG_HEADS * TT, P]), sub), state["q_start"])
        m = g.act.do(lambda e: e.activation(diff, diff, ACT.Exp, scale=-1.0), m)
        yield True
        kend = g.dve.do(lambda e: e.tensor_tensor(hk[:, :], hk[:, :], diff, mul), m)
        far = lambda i: k_far[:, :, i, :]
        one = lambda m: across.rearrange("p (h m) -> p h m", m=TT)[:, :, m:m + 1].broadcast_to([P, HG_HEADS, P])
        m = g.pool.do(lambda e: e.tensor_tensor(far(0), heads(hk[:, :])[:, :, 0, :], one(1), mul), kend, whole)
        g.pool.do(lambda e: e.tensor_tensor(far(1), heads(hk[:, :])[:, :, 1, :], one(2), mul), kend)
        state["k_far"] = g.pool.do(lambda e: e.tensor_tensor(far(2), far(0), one(2), mul), m)
        yield True

    run_between(rest_of_projections(), within_and_ends(), 4)

    PAIRS = ((0, 1), (1, 2), (2, 3), (0, 2), (1, 3), (0, 3))
    gates_ready, outs, o_ready = {}, {}, {}
    gate_of = (HG,) * HG_HEADS + (RG,) * HG_HEADS

    def gates():
        for head in range(KT):
            b, done = yield from steps(gate_of[head], head % HG_HEADS)
            m = scaled_to(o[:, head, :], b, done, free)
            gates_ready[head] = g.act.do(lambda e, head=head: e.activation(o[:, head, :], o[:, head, :], ACT.Silu), m)
            yield

    def cross_pairs(h):
        banks = [6, 7]
        emits = []
        for i, (kj, qi) in enumerate(PAIRS):
            lhs = hk[:, T * h + P * kj:T * h + P * (kj + 1)] if i < 3 else k_far[:, h, i - 3, :]
            emits.append(lambda e, i=i, lhs=lhs, qi=qi: e.matmul(
                g.bank[banks[i // 3]][:, P * (i % 3):P * (i % 3 + 1)], lhs, k_dec[:, T * h + P * qi:T * h + P * (qi + 1)], start=True, stop=True))
        mm = g.pe.do_all(emits, state["q_start"], state["k_far"], *[g.bank_free[b] for b in banks])
        for i, lane in enumerate((g.act, g.dve)):
            dst, src = cross[:, h, 3 * i:3 * i + 3, :].rearrange("p m t -> p (m t)"), g.bank[banks[i]][:, 0:3 * P]
            copy = (lambda e, dst=dst, src=src: e.activation(dst, src, ACT.Copy)) if i == 0 else (lambda e, dst=dst, src=src: e.tensor_copy(dst, src))
            g.bank_free[banks[i]] = state["cross", h, i] = lane.do(copy, mm)

    def finish_head(bank, done, head, gain):
        s = head % 2
        sq = g.act.do(lambda e: e.activation(g.square[:, s, :], g.bank[bank][:, :], ACT.Square), done, g.square_free[s])
        outs[head] = g.bank_free[bank] = g.dve.do(lambda e: e.scalar_tensor_tensor(
            o[:, head, :], g.bank[bank][:, :], gain, o[:, head, :], mul, mul), sq, gates_ready[head], g.const_ready)
        return sq

    def sum_squares(sq, head):
        s = head % 2
        emits = []
        for t in range(TT):
            col = TT * head + t
            emits.append(lambda e, t=t, col=col: e.matmul(g.bank[7][:, col:col + 1], g.square[:, s, P * t:P * (t + 1)], g.ones[:, :],
                                                          start=True, stop=True))
        g.square_free[s] = g.pe.do_all(emits, sq, g.bank_free[7])
        return g.square_free[s]

    def hgrn_values(h):
        b = g.take_bank()
        emits = []
        for i in range(TT):
            for j in range(i + 1):
                rhs = scores[:, T * h + P * i:T * h + P * (i + 1)] if j == i else cross[:, h, PAIRS.index((j, i)), :]
                emits.append(lambda e, j=j, rhs=rhs, i=i: e.matmul(
                    g.bank[b][:, P * i:P * (i + 1)], hv[:, T * j + P * h:T * j + P * (h + 1)], rhs, start=(j == 0), stop=(j == i)))
        mm = g.pe.do_all(emits, g.bank_free[b], marks["v"], state["cross", h, 0], state["cross", h, 1], state["chosen"])
        return finish_head(b, mm, h, g.hgrn_gain[:, :])

    spans = [(j, T - P * j) for j in range(TT)]
    offset = [0, 512, 896, 1152]
    late = ExitStack()

    def ret_score(h, decay, ret_scores):
        s = h % 2
        for j, n in spans:
            b = g.take_bank()
            g.pe.wait(g.bank_free[b], marks["ret_qk"])
            mm = g.pe.do(lambda e, b=b, j=j, n=n: e.matmul(
                g.bank[b][:, 0:n], rk[:, T * h + P * j:T * h + P * (j + 1)], rq[:, T * h + P * j:T * (h + 1)], start=True, stop=True))
            g.bank_free[b] = state["ret_scores", h] = g.dve.do(lambda e, b=b, j=j, n=n: e.tensor_tensor(
                ret_scores[:, s, offset[j]:offset[j] + n], g.bank[b][:, 0:n], decay[:, h, 0:n], mul),
                mm, state["decay_loaded"], state.get(("ret_free", s)), state["late_free"])

    def ret_values(h, ret_scores):
        s, b = h % 2, g.take_bank()
        emits = [lambda e, j=j, n=n: e.matmul(g.bank[b][:, P * j:T], rv[:, T * j + P * h:T * j + P * (h + 1)], ret_scores[:, s, offset[j]:offset[j] + n],
                                              start=(j == 0), stop=(j == TT - 1)) for j, n in spans]
        state["ret_free", s] = mm = g.pe.do_all(emits, g.bank_free[b], marks["v"], state["ret_scores", h])
        return finish_head(b, mm, HG_HEADS + h, g.ret_gain[:, :])

    def group_scales(group, sums):
        n = HG_HEADS * TT
        cols = slice(n * group, n * (group + 1))
        g.bank_free[7], ready = g.token_scales(g.bank[7][:, cols], n, P, EPS, sums, *(g.head_rms[:, i, cols] for i in (2, 0, 1)))
        return ready

    def normalise_head(head, ready, o_hi, o_lo):
        b = g.take_bank()
        rows = g.spread_scales(lambda t: g.head_rms[:, 2, TT * head + t:TT * head + t + 1], b, ready)
        x = o[:, head, :]
        g.bank_free[b] = full = g.dve.do(lambda e: e.tensor_tensor(x, x, g.bank[b][:, :], mul), rows, outs[head])
        o_ready[head] = g.split_into(x, o_hi[:, head, :], o_lo[:, head, :], full, state["late_free"])

    def outputs():
        for h in range(HG_HEADS):
            cross_pairs(h)
            yield True
        pending = None
        for h in range(HG_HEADS):
            while h not in gates_ready:
                yield False
            sq = hgrn_values(h)
            yield True
            if pending:
                sum_squares(*pending)
            pending = (sq, h)
        hs.close()
        state["late_free"] = g.fence()
        o_hi, o_lo = (g.tile(f"even_{n}", [P, KT, T], F32R, late) for n in ("o_hi", "o_lo"))
        state["o_hi"], state["o_lo"] = o_hi, o_lo
        decay = g.tile("ret_decay", [P, HG_HEADS, T], F32, late)
        ret_scores = g.tile("ret_scores", [P, 2, 1280], F32, late)
        state["decay_loaded"] = g.load("ret_decay", g.pool, [(decay[:, :, :], g.dram["ret_decay"])], state["late_free"])
        yield True
        sums = sum_squares(*pending)
        hgrn_scales = group_scales(0, sums)
        yield True
        ret_score(0, decay, ret_scores)
        yield True
        pending = None
        for h in range(HG_HEADS):
            if h + 1 < HG_HEADS:
                ret_score(h + 1, decay, ret_scores)
                yield True
            normalise_head(h, hgrn_scales, o_hi, o_lo)
            yield True
            while HG_HEADS + h not in gates_ready:
                yield False
            sq = ret_values(h, ret_scores)
            yield True
            if pending:
                sum_squares(*pending)
            pending = (sq, HG_HEADS + h)
        ret_scales = group_scales(1, sum_squares(*pending))
        for h in range(HG_HEADS):
            normalise_head(HG_HEADS + h, ret_scales, o_hi, o_lo)

    run_between(gates(), outputs(), 2)
    g.add_to_residual("even_w_out", KT, state["o_hi"], state["o_lo"], o_ready)
    late.close()
    inner.close()
    outer.close()


def two_norms(g):
    g.errands = []
    sums = [(g.square_sum[:, :], 0), (g.normed[:, 0, :], TT)]
    emits = [lambda e, src=src, c=c + t, t=t: e.matmul(g.bank[5][:, c:c + 1], src[:, P * t:P * (t + 1)], g.ones[:, :], start=True, stop=True)
             for src, c in sums for t in range(TT)]
    g.sum_free = done = g.pe.do_all(emits, g.summed, g.normed_free, g.bank_free[5], g.const_ready)
    means, roots = g.rms[:, 0:2, :], g.rms[:, 2:4, :]
    m = g.dve.do(lambda e: e.tensor_scalar(means[:, 0, :], g.bank[5][:, 0:TT], 1.0 / D, EPS, ALU.mult, ALU.add), done)
    m = g.dve.do(lambda e: e.tensor_scalar(means[:, 1, :], means[:, 0, :], EPS, None, ALU.mult), m)
    g.bank_free[5] = m = g.dve.do(lambda e: e.scalar_tensor_tensor(means[:, 1, :], g.bank[5][:, TT:2 * TT], 1.0 / D, means[:, 1, :], ALU.mult, ALU.add), m)
    m = g.act.do(lambda e: e.activation(roots, means, ACT.Sqrt), m)
    m = g.dve.do(lambda e: e.reciprocal(roots, roots), m)
    second = g.spread_scales(lambda t: g.rms[:, 3, t:t + 1], 7, m)
    return g.spread_scales(lambda t: g.rms[:, 2, t:t + 1], 6, m), second


def pool_mixer(g):
    mul, add, sub = ALU.mult, ALU.add, ALU.subtract
    with ExitStack() as scope:
        free = g.fence()
        W = T + 2 * PAD
        padded = g.tile("pool_padded", [P, KT, W], F32, scope)
        sums = g.tile("pool_sums", [P, KT, W], F32, scope)
        scratch = g.tile("pool_scratch", [P, 2, 2, W], F32, scope)
        near = g.tile("pool_near", [P, 2, 2, PAD], F32, scope)
        row = g.tile("pool_first_scale", [P, T], F32, scope)
        zeroed = [g.pool.do(lambda e, c=c: e.memset(padded[:, :, c], 0.0), free) for c in (slice(0, PAD), slice(PAD + T, W))]
        gains = g.dve.do(lambda e: e.tensor_tensor(g.gain_product[:, :], g.norm_gain[:, NORM_OF["first_final"], :], g.norm_gain[:, NORM_OF["pool"], :], mul), g.const_ready)
        first, second = two_norms(g)
        normed, summed, high, output = {}, {}, {}, {}
        scratch_free, near_free = [None, None], None
        pair = lambda t, group: t[:, 2 * group:2 * group + 2, PAD:PAD + T]
        ends = lambda t: t.rearrange("p k (n e) -> p k n e", e=PAD)[:, :, 0:T // PAD:T // PAD - 1, :]
        first_gain = lambda k: g.norm_gain[:, NORM_OF["first_final"], k:k + 1]

        def normalise(group):
            for k in (2 * group, 2 * group + 1):
                normed[k] = g.dve.do(lambda e, k=k: e.scalar_tensor_tensor(
                    padded[:, k, PAD:PAD + T], g.residual[:, k, :], g.gain_product[:, k:k + 1], g.bank[7][:, :], mul, mul), second, gains, free)

        def window_sum(group, lane):
            tiles, which = slice(2 * group, 2 * group + 2), 0 if lane is g.dve else 1
            src, m = padded[:, tiles, :], [normed[2 * group + 1], zeroed]
            rounds = POOL_WINDOWS[group].bit_length() - 1
            lo, hi = 1, W
            for i in range(rounds):
                back, ahead = (1, 0) if i == 0 else (1 << (i - 1), 1 << (i - 1))
                if i:
                    lo, hi = lo + back, hi - ahead
                dst = sums[:, tiles, :] if (rounds - 1 - i) % 2 == 0 else scratch[:, which, :, :]
                m = lane.do(lambda e, dst=dst, src=src, lo=lo, hi=hi, back=back, ahead=ahead: e.tensor_tensor(
                    dst[:, :, lo:hi], src[:, :, lo - back:hi - back], src[:, :, lo + ahead:hi + ahead], add), m, free, scratch_free[which])
                src = dst
            summed[group] = scratch_free[which] = m

        def subtract_token(group):
            nonlocal near_free
            a, x = pair(sums, group), pair(padded, group)
            share = g.window_share[:, group, :, :].unsqueeze(1).broadcast_to([P, 2, 2, PAD])
            m = g.dve.do(lambda e: e.tensor_tensor(near[:, :, :, :], ends(a), share, mul), summed[group], near_free, free)
            m = g.dve.do(lambda e: e.scalar_tensor_tensor(a, a, 1.0 / POOL_WINDOWS[group], x, mul, sub), m)
            near_free = m = g.dve.do(lambda e: e.tensor_tensor(ends(a), near[:, :, :, :], ends(x), sub), m)
            high[group] = g.act.do(lambda e: e.activation(g.x_hi[:, 2 * group:2 * group + 2, :], a, ACT.Copy), m, free)

        def low(group):
            x = slice(2 * group, 2 * group + 2)
            g.x_ready[2 * group] = g.x_ready[2 * group + 1] = g.dve.do(lambda e: e.tensor_tensor(
                g.x_lo[:, x, :], pair(sums, group), g.x_hi[:, x, :].bitcast(F32), sub), high[group])

        def first_output(group):
            for k in (2 * group, 2 * group + 1):
                x = g.residual[:, k, :]
                if group < 2:
                    g.residual_ready[k] = g.dve.do(lambda e, x=x, k=k: e.scalar_tensor_tensor(x, x, first_gain(k), g.bank[6][:, :], mul, mul), first)
                else:
                    gained = g.act.do(lambda e, x=x, k=k: e.activation(x, x, ACT.Copy, scale=first_gain(k)), normed[k])
                    g.residual_ready[k] = g.pool.do(lambda e, x=x: e.tensor_tensor(x, x, row[:, :], mul), gained, row_ready)

        def project(group):
            u, w_hi, w_lo = g.take_unit("pool_w_2", 0)
            output[group] = []
            for half in range(2):
                b = g.take_bank()
                c = slice(P * half, P * (half + 1))
                emits = []
                for k in range(2):
                    for i, (w, x) in enumerate(((w_hi, g.x_hi), (w_lo, g.x_hi), (w_hi, g.x_lo))):
                        emits.append(lambda e, b=b, w=w, x=x, k=k, i=i, c=c: e.matmul(
                            g.bank[b][:, :], w[:, k, c], x[:, 2 * group + k, :], start=(k == 0 and i == 0), stop=(k == 1 and i == 2)))
                mm = g.pe.do_all(emits, g.is_split[u], g.bank_free[b], g.x_ready[2 * group])
                output[group].append((b, mm))
            g.used[u] = mm

        def update(group):
            x_free = output[group][1][1]
            for half, (b, done) in enumerate(output[group]):
                n = 2 * group + half
                g.bank_free[b] = mark = g.dve.do(lambda e, n=n, b=b: e.scalar_tensor_tensor(
                    g.residual[:, n, :], g.bank[b][:, :], g.pool_scale[:, n:n + 1], g.residual[:, n, :], mul, add), done, g.residual_ready[n])
                g.residual_done(n, mark, x_free, later)

        later = []

        def lows():
            while later:
                later.pop(0)()

        normalise(2)
        window_sum(2, g.pool)
        normalise(3)
        window_sum(3, g.pool)
        row_ready = g.act.do(lambda e: e.activation(row[:, :], g.bank[6][:, :], ACT.Copy), first, free)
        normalise(0)
        window_sum(0, g.dve)
        subtract_token(0)
        normalise(1)
        g.bank_free[7] = normed[3]
        low(0)
        project(0)
        window_sum(1, g.dve)
        subtract_token(1)
        first_output(0)
        low(1)
        project(1)
        first_output(1)
        g.bank_free[6] = [row_ready, g.residual_ready[3]]
        first_output(2)
        first_output(3)
        update(0)
        subtract_token(2)
        lows()
        low(2)
        project(2)
        update(1)
        subtract_token(3)
        lows()
        low(3)
        project(3)
        update(2)
        lows()
        update(3)
        lows()


def transpose_tiles(g, src, n_tiles, bank, ready):
    emits = [lambda e, j=j: e.transpose(g.bank[bank][:, P * j:P * (j + 1)], src[:, P * j:P * (j + 1)], g.ident[:, :]) for j in range(n_tiles)]
    return g.pe.do_all(emits, ready, g.bank_free[bank], g.const_ready)


def to_features(g, out, k, hi, lo, ready, free, gain):
    b = g.take_bank()
    emits = [lambda e, t=t: e.transpose(g.bank[b][:, P * t:P * (t + 1)], out(t), g.ident[:, :]) for t in range(TT)]
    mm = g.pe.do_all(emits, ready, g.bank_free[b])
    g.bank_free[b] = mark = g.split_scaled(g.bank[b][:, :], gain, hi[:, k, :], lo[:, k, :], mm, free)
    return mark


def odd_mixer(g):
    mul, add, sub = ALU.mult, ALU.add, ALU.subtract
    R = NSA_HEADS // GROUPS
    PAIRS = NSA_HEADS // 2
    outer = ExitStack()
    free = g.fence()
    out = g.tile("nsa_out", [P, TT, NSA_HEADS * NSA_HD], F32, outer)
    inner = ExitStack()
    q_hi = g.tile("nsa_q_hi", [P, 3, T], F32R, inner)
    q_lo = g.tile("nsa_q_lo", [P, 3, T], F32R, inner)
    v = g.tile("nsa_v", [P, TT, 2 * KVW], F32, inner)
    gates = g.tile("nsa_gates", [P, TT, 3 * NSA_HEADS], F32, inner)
    k_hi = g.tile("nsa_k_hi", [P, 2, GROUPS, T], F32R, inner)
    k_lo = g.tile("nsa_k_lo", [P, 2, GROUPS, T], F32R, inner)
    kcmp_hi = g.tile("nsa_k_cmp_hi", [P, GROUPS, 2, NCP], F32R, inner)
    kcmp_lo = g.tile("nsa_k_cmp_lo", [P, GROUPS, 2, NCP], F32R, inner)
    vcmp = g.tile("nsa_v_cmp", [P, GROUPS, 4, NSA_HD], F32, inner)
    bias_c = g.tile("nsa_bias_cmp", [P, TT, NSA_HEADS, NCP], F32, inner)
    valid_c = g.tile("nsa_valid_cmp", [P, TT, NCP], F32, inner)
    cmp_bias_loaded = g.load("cmp_bias", g.pool, [(bias_c[:, :, :, :], g.dram["cmp_bias"]), (valid_c[:, :, :], g.dram["cmp_valid"])], free)
    bias = g.tile("nsa_bias", [P, 3, 2, T], F32, inner)
    cs = ExitStack()
    w1 = g.tile("cmp_w1", [P, CMP_BLOCK, P], F32, cs)
    w2 = g.tile("cmp_w2", [P, 2, P], F32, cs)
    pos = g.tile("cmp_pos", [P, 2, CMP_BLOCK], F32, cs)
    cmp_loaded = g.load("cmp_weights", g.pool, [(w1[:, :, :], g.dram["cmp_w1"][0]), (w2[:, :, :], g.dram["cmp_w2"]),
                                                (pos[:, :, :], g.dram["cmp_pos"])], free)
    kv_c = g.tile("cmp_kv", [P, 2, T], F32, cs)
    blocks = g.tile("cmp_blocks", [P, 2, CMP_BLOCK, NCP], F32, cs)
    hidden = g.tile("cmp_hidden", [P, 2, NCP], F32, cs)
    hidden4 = g.tile("cmp_hidden_repeated", [P, 4, NCP], F32, cs)
    scale_row = g.begin_layer()
    out_zeroed = g.pool.do(lambda e: e.memset(out[:, :, :], 0.0), free)
    zeroed = [g.pool.do(lambda e: e.memset(hidden[:, :, :], 0.0), free), g.pool.do(lambda e: e.memset(vcmp[:, :, :, :], 0.0), free),
              g.pool.do(lambda e: e.memset(kcmp_hi[:, :, :, :].bitcast(F32), 0.0), free), g.pool.do(lambda e: e.memset(kcmp_lo[:, :, :, :].bitcast(F32), 0.0), free)]
    project = lambda column: g.project_features("odd_w_in", column, KT, g.x_hi, g.x_lo, g.x_ready)
    both = ((slice(0, 64), slice(64, 128)), (slice(64, 128), slice(0, 64)))
    block_ready = []
    projected = [project(ODD_KC), project(ODD_VC)]
    for i in range(2):
        b, done = projected[i]
        g.bank_free[b] = m = g.dve.do(lambda e, i=i, b=b: e.tensor_tensor(kv_c[:, i, :], g.bank[b][:, :], scale_row, mul), done, g.scale_ready, free)
        halves = kv_c[:, i, :].rearrange("p (m r) -> p r m", r=CMP_STRIDE)
        for a in range(2):
            pb = pos[:, i, CMP_STRIDE * a:CMP_STRIDE * (a + 1)].unsqueeze(2).broadcast_to([P, CMP_STRIDE, NC])
            ready = g.dve.do(lambda e, i=i, a=a, halves=halves, pb=pb: e.tensor_tensor(
                blocks[:, i, CMP_STRIDE * a:CMP_STRIDE * (a + 1), 0:NC], halves[:, :, a:a + NC], pb, add), m, cmp_loaded, free)
        block_ready.append(ready)
    bias_loads = [Transfers(g.sem(f"alibi_loaded{i}")) for i in range(3)]
    bias_loaded, bias_used = {}, {}

    def load_bias(n):
        if n < PAIRS:
            bias_loaded[n] = bias_loads[n % 3].start(g.pool, bias[:, n % 3, :, :], g.dram["alibi"][:, 2 * n:2 * n + 2, :], bias_used.get(n - 3), free)

    for n in range(2):
        load_bias(n)

    keys_ready = []
    for i in range(2):
        b, done = project((ODD_KS, ODD_KW)[i])
        x, s = g.normed[:, i, :], i
        g.bank_free[b] = m = g.dve.do(lambda e, x=x, b=b: e.tensor_tensor(x, g.bank[b][:, :], scale_row, mul), done, g.normed_free[i], free)
        for grp, (own, other) in enumerate(both):
            high = g.act.do(lambda e, i=i, grp=grp, own=own, x=x: e.activation(k_hi[own, i, grp, :], x[own, :], ACT.Copy), m)
            low = g.dve.do(lambda e, i=i, grp=grp, own=own, x=x: e.tensor_tensor(k_lo[own, i, grp, :], x[own, :], k_hi[own, i, grp, :].bitcast(F32), sub), high)
            keys_ready.append(g.act.do(lambda e, i=i, grp=grp, own=own, other=other: e.activation(
                k_hi[other, i, grp, :], k_hi[own, i, grp, :].bitcast(F32), ACT.Copy), high))
            keys_ready.append(g.act.do(lambda e, i=i, grp=grp, own=own, other=other: e.activation(
                k_lo[other, i, grp, :], k_lo[own, i, grp, :].bitcast(F32), ACT.Copy), low))
        g.normed_free[i] = low

    def compress(i, loaded):
        emits = [lambda e, p=p: e.matmul(g.bank[7][:, 0:NC], w1[:, p, :], blocks[:, i, p, 0:NC], start=(p == 0), stop=(p == CMP_BLOCK - 1))
                 for p in range(CMP_BLOCK)]
        used = g.pe.do_all(emits, loaded, block_ready[i], g.bank_free[7])
        silu = g.act.do(lambda e: e.activation(hidden[:, i, 0:NC], g.bank[7][:, 0:NC], ACT.Silu), used, zeroed)
        g.bank_free[7] = silu
        return used, silu

    used, silu = compress(0, cmp_loaded)
    w1_loaded = g.load("cmp_w1_v", g.pool, [(w1[:, :, :], g.dram["cmp_w1"][1])], used)
    banks, done = g.project_tokens("odd_w_in", ODD_VALUES, ODD_VALUE_COLUMNS, g.x_hi, g.x_lo, g.x_ready)
    mm = g.pe.do(lambda e: e.matmul(g.bank[7][:, 0:NCP], w2[:, 0, :], hidden[:, 0, :], start=True, stop=True), silu)
    for grp, (own, other) in enumerate(both):
        for half, rows in enumerate((slice(0, 64), slice(64, 128))):
            high = g.act.do(lambda e, rows=rows, own=own, grp=grp, half=half: e.activation(kcmp_hi[rows, grp, half, :], g.bank[7][own, 0:NCP], ACT.Copy), mm, zeroed)
            if rows == own:
                low = g.dve.do(lambda e, own=own, grp=grp, half=half: e.tensor_tensor(
                    kcmp_lo[own, grp, half, :], g.bank[7][own, 0:NCP], kcmp_hi[own, grp, half, :].bitcast(F32), sub), high, zeroed)
                g.act.wait(low)
        kcmp_ready = g.act.do(lambda e, own=own, other=other, grp=grp: e.activation(
            kcmp_lo[other, grp, 1 - grp, :], kcmp_lo[own, grp, grp, :].bitcast(F32), ACT.Copy), low)
    g.bank_free[7] = kcmp_ready
    for t in range(TT):
        column = g.rms[:, 2, t:t + 1]
        m = g.act.do(lambda e, t=t, b=banks[t], column=column: e.activation(v[:, t, :], g.bank[b][:, 0:2 * KVW], ACT.Copy, scale=column), done, g.column_ready, free)
        gates_ready = g.act.do(lambda e, t=t, b=banks[t], column=column: e.activation(
            gates[:, t, :], g.bank[b][:, 2 * KVW:2 * KVW + 3 * NSA_HEADS], ACT.Sigmoid, scale=column), m)
        g.bank_free[banks[t]] = gates_ready
    v_ready = gates_ready
    q_ready = {}

    def queries():
        for n in range(PAIRS):
            s = n % 3
            b, done = yield from g.feature_steps("odd_w_in", P * n, KT, g.x_hi, g.x_lo, g.x_ready)
            x = g.normed[:, n % 2, :]
            g.bank_free[b] = m = g.dve.do(lambda e, x=x, b=b: e.tensor_tensor(x, g.bank[b][:, :], scale_row, mul), done, g.normed_free[n % 2])
            g.normed_free[n % 2] = q_ready[n] = g.split_scaled(x, -(NSA_HD ** -0.5), q_hi[:, s, :], q_lo[:, s, :], m, pair_used.get(n - 3), free)
            yield

    pair_used = {}
    front = queries()
    for _ in range(KT // 2):
        next(front)
    used, silu = compress(1, w1_loaded)
    repeated = g.dve.do(lambda e: e.tensor_copy(hidden4[:, :, :], hidden[:, 1, :].unsqueeze(1).broadcast_to([P, 4, NCP])), silu)
    for _ in range(KT // 2):
        next(front)
    mm = g.pe.do(lambda e: e.matmul(g.bank[7][:, 0:P], hidden4[:, :, :].rearrange("p r c -> p (r c)"), w2[:, 1, :], start=True, stop=True), repeated)
    for grp in range(GROUPS):
        for r in range(4):
            rows = slice(32 * r, 32 * r + 32)
            vcmp_ready = g.dve.do(lambda e, rows=rows, grp=grp, r=r: e.tensor_copy(vcmp[rows, grp, r, :], g.bank[7][rows, 64 * grp:64 * grp + 64]), mm, zeroed)
    g.bank_free[7] = vcmp_ready
    cs.close()

    free2 = g.fence()
    work = ExitStack()
    probs = g.tile("nsa_probs", [P, 5, T], F32, work)
    turned = g.tile("nsa_turned", [P, 3, T], F32, work)
    part = g.tile("nsa_part", [P, 2, T], F32, work)
    stats = g.tile("nsa_stats", [P, 2, 3, 16], F32, work)
    cmp_probs = g.tile("nsa_cmp_probs", [P, TT, R, NCP], F32, work)
    cmp_stats = g.tile("nsa_cmp_stats", [P, 3, TT, R], F32, work)
    g.ring_banks = 2
    units = [(n, a, z, t) for n in range(PAIRS) for a in range(2) for z in range(2) for t in range(TT)]
    exp_done, turned_ready, least_ready = {}, {}, {}
    prob_free, turn_free, low_free, total_free, part_free = [None] * 5, [None] * 3, {}, [None] * 2, [None] * 2
    state = {"cmp_free": None, "cmp_stats_free": None, "out": out_zeroed, "cmp_scores": None}

    def scores(i):
        n, a, z, t = units[i]
        b, s, keys, sq = 2 + i % 2, i % 5, P * (t + 1), n % 3
        rows = slice(64 * z, 64 * z + 64)
        low = stats[:, n % 2, 0, 8 * a + 2 * t + z:8 * a + 2 * t + z + 1]
        grp = 2 * n // R
        emits = [lambda e, x=x, k=k, j=j: e.matmul(g.bank[b][:, 0:keys], x[rows, sq, P * t:P * (t + 1)], k[rows, a, grp, 0:keys], start=(j == 0), stop=(j == 2))
                 for j, (x, k) in enumerate(((q_hi, k_hi), (q_hi, k_lo), (q_lo, k_hi)))]
        mm = g.pe.do_all(emits, g.bank_free[b], q_ready[n], keys_ready)
        pair_used[n] = mm
        g.bank_free[b] = m = g.dve.do(lambda e: e.tensor_tensor_reduce(
            probs[:, s, 0:keys], g.bank[b][:, 0:keys], bias[:, n % 3, z, T - keys:T], 1.0, 3.0e38, add, ALU.min, low),
            mm, bias_loaded[n], prob_free[s], low_free.get((n % 2, a, z, t)), free2)
        bias_used[n] = least_ready[i] = m

    def exponentials(i):
        n, a, z, t = units[i]
        s, keys = i % 5, P * (t + 1)
        low, total = (stats[:, n % 2, j, 8 * a + 2 * t + z:8 * a + 2 * t + z + 1] for j in (0, 1))
        exp_done[i] = g.act.do(lambda e: e.activation(probs[:, s, 0:keys], probs[:, s, 0:keys], ACT.Exp, bias=low, scale=-1.0, accum_out=total),
                               least_ready[i], total_free[n % 2])
        low_free[n % 2, a, z, t] = exp_done[i]

    def turn(i):
        _, _, _, t = units[i]
        s, b, keys = i % 5, 4 + i % 2, P * (t + 1)
        prob_free[s] = mm = transpose_tiles(g, probs[:, s, :], t + 1, b, exp_done[i])
        if i % 2:
            m = g.act.do(lambda e: e.activation(turned[:, i % 3, 0:keys], g.bank[b][:, 0:keys], ACT.Copy), mm, turn_free[i % 3])
        else:
            m = g.dve.do(lambda e: e.tensor_copy(turned[:, i % 3, 0:keys], g.bank[b][:, 0:keys]), mm, turn_free[i % 3])
        g.bank_free[b] = turned_ready[i] = m

    def values(i):
        n, a, z, t = units[i]
        grp = 2 * n // R
        ob = g.bank[6 + a]
        c = slice(P * t + NSA_HD * z, P * t + NSA_HD * (z + 1))
        vc = slice(KVW * a + NSA_HD * grp, KVW * a + NSA_HD * (grp + 1))
        emits = [lambda e, j=j: e.matmul(ob[:, c], turned[:, i % 3, P * j:P * (j + 1)], v[:, j, vc], start=(j == 0), stop=(j == t)) for j in range(t + 1)]
        turn_free[i % 3] = mm = g.pe.do_all(emits, turned_ready[i], v_ready, g.bank_free[6 + a] if (z, t) == (0, 0) else None)
        if (z, t) == (1, TT - 1):
            cols = slice(8 * a, 8 * a + 8)
            inv = stats[:, n % 2, 2, cols]
            m = g.dve.do(lambda e: e.reciprocal(inv, stats[:, n % 2, 1, cols]), exp_done[i])
            gate = gates[:, :, 6 * n + 1 + a:6 * n + 1 + a + 4:3]
            grid = inv.rearrange("p (t z) -> p t z", t=TT)
            m = g.dve.do(lambda e: e.tensor_tensor(grid, grid, gate, mul), m)
            total_free[n % 2] = m
            wide = inv.unsqueeze(2).broadcast_to([P, 8, NSA_HD])
            g.bank_free[6 + a] = part_ready = g.dve.do(lambda e: e.tensor_tensor(
                part[:, a, :].rearrange("p (h d) -> p h d", h=8), ob[:, :].rearrange("p (h d) -> p h d", h=8), wide, mul), m, mm, part_free[a])
            dst = out[:, :, P * n:P * (n + 1)]
            src = part[:, a, :].rearrange("p (t c) -> p t c", t=TT)
            part_free[a] = state["out"] = g.pool.do(lambda e: e.tensor_tensor(dst, dst, src, add), part_ready, state["out"])

    def compressed_scores(n):
        b, s, grp = g.take_bank(), n % 3, 2 * n // R
        emits = []
        for t in range(TT):
            for j, (x, k) in enumerate(((q_hi, kcmp_hi), (q_hi, kcmp_lo), (q_lo, kcmp_hi))):
                emits.append(lambda e, x=x, k=k, j=j, t=t: e.matmul(g.bank[b][:, 64 * t:64 * (t + 1)], x[:, s, P * t:P * (t + 1)],
                                                                   k[:, grp, :, :].rearrange("p z c -> p (z c)"), start=(j == 0), stop=(j == 2)))
        mm = g.pe.do_all(emits, q_ready[n], kcmp_ready, g.bank_free[b])
        first = 2 * n - R * grp
        g.bank_free[b] = state["cmp_scores"] = g.dve.do(lambda e: e.tensor_tensor(
            cmp_probs[:, :, first:first + 2, :].rearrange("p t z c -> p t (z c)"), g.bank[b][:, 0:4 * 64].rearrange("p (t c) -> p t c", t=TT),
            bias_c[:, :, 2 * n:2 * n + 2, :].rearrange("p t z c -> p t (z c)"), add), mm, cmp_bias_loaded, free2, state["cmp_free"])

    def compressed_attention(grp):
        low, total = (cmp_stats[:, j, :, :].rearrange("p t h -> p (t h)") for j in range(2))
        flat = cmp_probs[:, :, :, :].rearrange("p t h c -> p (t h) c")
        wide = lambda x: x.unsqueeze(2).broadcast_to([P, TT * R, NCP])
        m = g.dve.do(lambda e: e.tensor_reduce(low, flat, AX.X, ALU.min), state["cmp_scores"])
        yield
        m = g.dve.do(lambda e: e.tensor_tensor(flat, flat, wide(low), sub), m)
        m = g.act.do(lambda e: e.activation(flat, flat, ACT.Exp, scale=-1.0), m)
        yield
        m = g.dve.do(lambda e: e.tensor_reduce(total, flat, AX.X, add), m)
        m2 = g.dve.do(lambda e: e.reciprocal(total, total), m)
        gate = gates[:, :, 3 * R * grp:3 * R * (grp + 1):3]
        scale_ready = g.dve.do(lambda e: e.tensor_tensor(cmp_stats[:, 2, :, :], cmp_stats[:, 1, :, :], gate, mul), m2, state["cmp_stats_free"])
        masked = g.pool.do(lambda e: e.tensor_tensor(cmp_probs[:, :, :, :], cmp_probs[:, :, :, :],
                                                     valid_c[:, :, :].unsqueeze(2).broadcast_to([P, TT, R, NCP]), mul), m, cmp_bias_loaded)
        yield
        yield
        for t in range(TT):
            b, s = g.take_bank(), t % 2
            turn = transpose_tiles(g, cmp_probs[:, t, :, :].rearrange("p h c -> p (h c)"), 2, b, masked)
            state["cmp_free"] = turn
            x = g.square[:, s, 0:2 * P]
            g.bank_free[b] = m = g.act.do(lambda e, b=b, x=x: e.activation(x, g.bank[b][:, 0:2 * P], ACT.Copy), turn, g.square_free[s])
            yield
            b = g.take_bank()
            emits = [lambda e, b=b, r=r, x=x: e.matmul(g.bank[b][:, 256 * r:256 * (r + 1)], x[:, P * r:P * (r + 1)],
                                                       vcmp[:, grp, :, :].rearrange("p r d -> p (r d)"), start=True, stop=True) for r in range(2)]
            g.square_free[s] = mm = g.pe.do_all(emits, m, vcmp_ready, g.bank_free[b])
            cols = slice(512 * grp, 512 * (grp + 1))
            heads = lambda x: x.rearrange("p (h d) -> p h d", h=R)
            y = g.normed[:, s, :]
            g.bank_free[b] = m = g.dve.do(lambda e, b=b, y=y, t=t: e.tensor_tensor(
                heads(y), heads(g.bank[b][:, :]), cmp_stats[:, 2, t, :].unsqueeze(2).broadcast_to([P, R, NSA_HD]), mul), mm, scale_ready, g.normed_free[s])
            state["cmp_stats_free"] = m
            g.normed_free[s] = state["out"] = g.pool.do(lambda e, y=y, t=t, cols=cols: e.tensor_tensor(out[:, t, cols], out[:, t, cols], y, add),
                                                            m, state["out"])
            yield

    def attention():
        extra = iter(())
        for i in range(len(units) + 4):
            if i < len(units):
                n, a, z, t = units[i]
                while n not in q_ready:
                    yield False
                if (a, z, t) == (0, 0, 0):
                    load_bias(n + 2)
                    compressed_scores(n)
                    if n % (PAIRS // GROUPS) == PAIRS // GROUPS - 1:
                        extra = compressed_attention(2 * n // R)
                scores(i)
            if 3 <= i < len(units) + 3:
                turn(i - 3)
            if i < len(units):
                exponentials(i)
            if i >= 4:
                values(i - 4)
            next(extra, None)
            yield True

    run_together(front, attention(), 2)
    work.close()
    inner.close()
    g.ring_banks = RING_BANKS
    free = g.fence()
    o_hi = g.tile("odd_o_hi", [P, KT, T], F32R, outer)
    o_lo = g.tile("odd_o_lo", [P, KT, T], F32R, outer)
    o_ready = [to_features(g, lambda t, k=k: out[:, t, P * k:P * (k + 1)], k, o_hi, o_lo, state["out"], free, 1.0) for k in range(KT)]
    g.add_to_residual("odd_w_out", KT, o_hi, o_lo, o_ready)
    outer.close()


def rope_tables(g, cos, sin, work, free, state):
    mul, add = ALU.mult, ALU.add
    parts = (6.28125, 0.0019350051879882812, 2 * math.pi - 6.28125 - 0.0019350051879882812)
    pos_i, pos_f, angle, turns, whole = (work[:, i, :] for i in range(5))
    loaded = g.load("positions", g.pool, [(pos_i.bitcast(I32), g.dram["positions"])], free)
    for _ in range(KT):
        yield
    m = g.dve.do(lambda e: e.tensor_copy(pos_f, pos_i.bitcast(I32)), loaded)
    yield
    angled = g.dve.do(lambda e: e.tensor_scalar(angle, pos_f, g.inv_freq[:, 0:1], None, mul), m, g.const_ready)
    yield
    for i, (out, shift) in enumerate(((sin, 0.0), (cos, 0.25))):
        m = g.dve.do(lambda e, shift=shift: e.tensor_scalar(turns, angle, 1 / (2 * math.pi), shift, mul, add), angled)
        yield
        m = g.dve.do(lambda e: e.tensor_copy(whole.bitcast(I32), turns), m)
        yield
        m = g.dve.do(lambda e: e.tensor_copy(turns, whole.bitcast(I32)), m)
        yield
        m = g.dve.do(lambda e, out=out: e.scalar_tensor_tensor(out, turns, -parts[0], angle, mul, add), m)
        yield
        m = g.dve.do(lambda e, out=out: e.scalar_tensor_tensor(out, turns, -parts[1], out, mul, add), m)
        yield
        m = g.dve.do(lambda e, out=out: e.scalar_tensor_tensor(out, turns, -parts[2], out, mul, add), m)
        yield
        m = g.dve.do(lambda e, out=out, shift=shift: e.tensor_scalar(out, out, 2 * math.pi * shift, math.pi - 1e-6, add, ALU.min), m)
        yield
        m = g.dve.do(lambda e, out=out: e.tensor_scalar(out, out, -(math.pi - 1e-6), None, ALU.max), m)
        yield
        angled = m
        state["tables"] = g.act.do(lambda e, out=out: e.activation(out, out, ACT.Sin), m)


def diff_mixer(g):
    mul, add, sub = ALU.mult, ALU.add, ALU.subtract
    hd = 64
    outer = ExitStack()
    free = g.fence()
    out = g.tile("diff_out", [P, TT, D], F32, outer)
    rms = g.tile("diff_rms", [P, 3, DIFF_HEADS, TT], F32, outer)
    inner = ExitStack()
    qk_hi = g.tile("diff_qk_hi", [P, 2, 3, T], F32R, inner)
    qk_lo = g.tile("diff_qk_lo", [P, 2, 3, T], F32R, inner)
    v = g.tile("diff_v", [P, TT, D], F32, inner)
    rotate = g.tile("rope_rotate", [P, P], F32, inner)
    cos = g.tile("rope_cos", [P, T], F32, inner)
    sin = g.tile("rope_sin", [P, T], F32, inner)
    plain = g.tile("rope_plain", [P, 2, T], F32, inner)
    turned_part = g.tile("rope_turned", [P, 2, T], F32, inner)
    lam_in = g.tile("diff_lam_in", [P, 4, hd], F32, inner)
    lam = g.tile("diff_lam", [P, 8], F32, inner)
    probs = g.tile("diff_probs", [P, 3, 2, T], F32, inner)
    mixed = g.tile("diff_mixed", [P, 2, T], F32, inner)
    turned = g.tile("diff_turned", [P, 2, T], F32, inner)
    stats = g.tile("diff_stats", [P, 5, DIFF_HEADS, TT, 2], F32, inner)
    scale_row = g.begin_layer()
    small_loaded = g.load("diff_tables", g.pool, [(rotate[:, :], g.dram["rope_rotate"]), (lam_in[:, :, :], g.dram["diff_lam"])], free)
    state, v_ready = {}, []
    tables = rope_tables(g, cos[:, :], sin[:, :], probs[:, :, :, :].rearrange("p s c t -> p (s c) t"), free, state)
    plain_free, part_free = [None, None], [None, None]
    head_used, qk_ready = {}, {}

    def rope(h, which, plain_ready):
        s, b = which, g.take_bank()
        x = g.normed[:, s, :]
        mm = g.pe.do(lambda e: e.matmul(g.bank[b][:, :], rotate[:, :], plain[:, s, :], start=True, stop=True), plain_ready, g.bank_free[b], small_loaded)
        a = g.pool.do(lambda e: e.tensor_tensor(x, plain[:, s, :], cos[:, :], mul), plain_ready, state["tables"], g.normed_free[s])
        plain_free[s] = [mm, a]
        g.bank_free[b] = c = g.dve.do(lambda e: e.tensor_tensor(turned_part[:, s, :], g.bank[b][:, :], sin[:, :], mul), mm, state["tables"], part_free[s], free)
        part_free[s] = m = g.pool.do(lambda e: e.tensor_tensor(x, x, turned_part[:, s, :], add), a, c)

        def split():
            g.normed_free[s] = ready = g.split_into(x, qk_hi[:, which, h % 3, :], qk_lo[:, which, h % 3, :], m, head_used.get(h - 3), free)
            qk_ready.setdefault(h, []).append(ready)

        return split

    pending = []
    started = set()

    def heads(first, last):
        for h in range(first, last):
            for which in range(2):
                steps = g.feature_steps("diff_w_qkv_2", D * which + P * h, KT, g.x_hi, g.x_lo, g.x_ready)
                for _ in range(2):
                    yield next(steps)
                split = rope(*pending.pop()) if pending else None
                for _ in range(3):
                    yield next(steps)
                if split:
                    split()
                b, done = yield from steps
                if which == 0:
                    started.add(h)
                g.bank_free[b] = m = g.dve.do(lambda e, which=which, b=b: e.tensor_tensor(plain[:, which, :], g.bank[b][:, :], scale_row, mul),
                                              done, g.scale_ready, free, plain_free[which])
                pending.append((h, which, m))
                yield
        if last == DIFF_HEADS:
            rope(*pending.pop())()
            started.add(last)

    def first_projections():
        projected = []
        for which in range(2):
            projected.append((yield from g.feature_steps("diff_w_qkv_2", D * which, KT, g.x_hi, g.x_lo, g.x_ready)))
            yield
        for which, (b, done) in enumerate(projected):
            g.bank_free[b] = m = g.dve.do(lambda e, which=which, b=b: e.tensor_tensor(plain[:, which, :], g.bank[b][:, :], scale_row, mul),
                                          done, g.scale_ready, free)
            pending.append((0, which, m))
        for half in range(2):
            banks, done = yield from g.token_steps("diff_w_qkv_2", 2 * D + 512 * half, 512, g.x_hi, g.x_lo, g.x_ready)
            v_ready.append(g.tokens_out(banks, done, lambda t: v[:, t, 512 * half:512 * (half + 1)], free))
            while pending:
                rope(*pending.pop(0))()
            yield

    run_between(first_projections(), tables, 1)
    for i in range(2):
        m = g.dve.do(lambda e, i=i: e.tensor_tensor(lam_in[:, 2 * i, :], lam_in[:, 2 * i, :], lam_in[:, 2 * i + 1, :], mul), small_loaded)
        m = g.dve.do(lambda e, i=i: e.tensor_reduce(lam[:, i:i + 1], lam_in[:, 2 * i, :], AX.X, add), m)
    m = g.act.do(lambda e: e.activation(lam[:, 2:4], lam[:, 0:2], ACT.Exp), m)
    m = g.dve.do(lambda e: e.tensor_tensor(lam[:, 4:5], lam[:, 3:4], lam[:, 2:3], sub), m)
    lam_ready = g.dve.do(lambda e: e.tensor_scalar(lam[:, 5:6], lam[:, 4:5], LAM_INIT, None, sub), m)

    g.ring_banks = 2
    units = [(h, t) for h in range(DIFF_HEADS) for t in range(TT)]
    probs_free, mixed_free, turned_free = [None] * 3, [None] * 2, [None] * 2
    highest, summed, mixed_ready, turned_ready, squared = {}, {}, {}, {}, {}
    scaled = []
    scale = hd ** -0.5
    by_head = lambda x: x.rearrange("p h t -> p (h t)")

    def scores(n):
        h, t = units[n]
        for c in range(2):
            b = 2 + (2 * n + c) % 3
            rows = slice(hd * c, hd * (c + 1))
            emits = [lambda e, b=b, rows=rows, q=q, k=k, i=i: e.matmul(
                g.bank[b][:, :], q[rows, 0, h % 3, P * t:P * (t + 1)], k[rows, 1, h % 3, :], start=(i == 0), stop=(i == 2))
                for i, (q, k) in enumerate(((qk_hi, qk_hi), (qk_hi, qk_lo), (qk_lo, qk_hi)))]
            head_used[h] = mm = g.pe.do_all(emits, g.bank_free[b], qk_ready[h])
            m = g.dve.do(lambda e, b=b, c=c: e.tensor_reduce(stats[:, 0, h, t, c:c + 1], g.bank[b][:, :], AX.X, ALU.max), mm, free)
            highest[n, c] = g.dve.do(lambda e, c=c: e.tensor_scalar(stats[:, 1, h, t, c:c + 1], stats[:, 0, h, t, c:c + 1], -scale, None, mul), m)
            if c == 0:
                exponentials(n, c)

    def exponentials(n, c):
        h, t = units[n]
        b = 2 + (2 * n + c) % 3
        g.bank_free[b] = summed[n] = g.act.do(lambda e: e.activation(
            probs[:, n % 3, c, :], g.bank[b][:, :], ACT.Exp, bias=stats[:, 1, h, t, c:c + 1], scale=scale,
            accum_out=stats[:, 2, h, t, c:c + 1]), highest[n, c], probs_free[n % 3], state["tables"])

    def mix(n):
        h, t = units[n]
        st = lambda i, c: stats[:, i, h, t, c:c + 1]
        m = g.dve.do(lambda e: e.reciprocal(stats[:, 3, h, t, :], stats[:, 2, h, t, :]), summed[n])
        m = g.dve.do(lambda e: e.tensor_scalar(st(4, 0), st(3, 1), st(2, 0), lam[:, 5:6], mul, mul), m, lam_ready)
        probs_free[n % 3] = mixed_ready[n] = g.dve.do(lambda e: e.scalar_tensor_tensor(
            mixed[:, n % 2, :], probs[:, n % 3, 1, :], st(4, 0), probs[:, n % 3, 0, :], mul, add), m, mixed_free[n % 2])

    def turn(n):
        mixed_free[n % 2] = mm = transpose_tiles(g, mixed[:, n % 2, :], TT, 5, mixed_ready[n])
        g.bank_free[5] = turned_ready[n] = g.act.do(lambda e: e.activation(turned[:, n % 2, :], g.bank[5][:, :], ACT.Copy), mm, turned_free[n % 2], free)

    def values(n):
        h, t = units[n]
        ob = 6 + h % 2
        emits = [lambda e, j=j: e.matmul(g.bank[ob][:, P * t:P * (t + 1)], turned[:, n % 2, P * j:P * (j + 1)], v[:, j, P * h:P * (h + 1)],
                                         start=(j == 0), stop=(j == TT - 1)) for j in range(TT)]
        turned_free[n % 2] = mm = g.pe.do_all(emits, turned_ready[n], v_ready, g.bank_free[ob] if t == 0 else None)
        if t < TT - 1:
            return
        tiles = lambda x: x.rearrange("p (t d) -> p t d", d=P)
        o = out[:, :, P * h:P * (h + 1)]
        s = h % 2
        g.bank_free[ob] = m = g.dve.do(lambda e: e.tensor_tensor(o, tiles(g.bank[ob][:, :]), stats[:, 3, h, :, 0:1].broadcast_to([P, TT, P]), mul), mm)
        state["fence"] = g.fence()
        m = g.pool.do(lambda e: e.tensor_tensor(tiles(g.square[:, s, :]), o, o, mul), m, g.square_free[s])
        state["squares"] = lambda: g.dve.do(lambda e: e.tensor_reduce(rms[:, 0, h, :], tiles(g.square[:, s, :]), AX.X, add), m)

    def sum_of_squares(h):
        g.square_free[h % 2] = squared[h] = state["squares"]()

    def sub_norm(first, last):
        hs, n = slice(first, last), (last - first) * TT
        _, m = g.token_scales(by_head(rms[:, 0, hs, :]), n, P, SUBLN_EPS, squared[last - 1], *(by_head(rms[:, i, hs, :]) for i in (2, 0, 1)))
        for h in range(first, last):
            o = out[:, :, P * h:P * (h + 1)]
            lane = g.pool if h % 2 or last < DIFF_HEADS else g.dve
            scaled.append(lane.do(lambda e, o=o, h=h: e.tensor_tensor(o, o, rms[:, 2, h, :].unsqueeze(2).broadcast_to([P, TT, P]), mul), m))
            yield

    def attention():
        norming = iter(())
        for i in range(len(units) + 3):
            if i < len(units):
                while units[i][0] + 1 not in started:
                    yield False
                scores(i)
                yield True
            next(norming, None)
            if 2 <= i < len(units) + 2:
                turn(i - 2)
            if i < len(units):
                exponentials(i, 1)
            if 1 <= i < len(units) + 1:
                mix(i - 1)
            yield True
            if i >= 3:
                values(i - 3)
                h, t = units[i - 3]
                if h and t == 0:
                    sum_of_squares(h - 1)
                if (h, t) == (4, 0):
                    norming = sub_norm(0, 4)
            yield True
        sum_of_squares(DIFF_HEADS - 1)

    run_together(heads(1, DIFF_HEADS), attention(), 1)
    inner.close()
    g.ring_banks = RING_BANKS
    free = state["fence"]
    o_hi = g.tile("diff_o_hi", [P, KT, T], F32R, outer)
    o_lo = g.tile("diff_o_lo", [P, KT, T], F32R, outer)
    turned_head = lambda h: to_features(g, lambda t: out[:, t, P * h:P * (h + 1)], h, o_hi, o_lo, scaled[h], free, g.subln_gain[:, 0:1])
    o_ready = [turned_head(h) for h in range(4)]
    for _ in sub_norm(4, DIFF_HEADS):
        pass
    o_ready += [turned_head(h) for h in range(4, DIFF_HEADS)]
    g.add_to_residual("diff_w_o_2", KT, o_hi, o_lo, o_ready)
    outer.close()


def final_norm(g):
    scales = g.norm_scales()
    places = [g.raw[:, slot, T * half:T * (half + 1)] for slot in range(RAW_SLOTS) for half in range(2)] + [g.normed[:, s, :] for s in range(2)]
    weights_done = g.is_split[len(g.units) - 1]
    marks = []
    for k in range(KT):
        full = g.dve.do(lambda e, x=places[k], k=k: e.scalar_tensor_tensor(
            x, g.residual[:, k, :], g.norm_gain[:, NORM_OF["final"], k:k + 1], g.bank[6][:, :], ALU.mult, ALU.mult),
            scales, g.normed_free, weights_done)
        marks.append(g.load(f"store{k}", g.sp, [(g.dram["out"][P * k:P * (k + 1), :], places[k])], full))
    g.sp.wait(marks)


MIXERS = {"even": even_mixer, "odd": odd_mixer, "pool": pool_mixer, "diff": diff_mixer}


def build(nc, dram, stages):
    units = [unit for stage in stages for unit in stage_units(stage)]
    with ExitStack() as ctx:
        g = Program(nc, ctx, dram, units)
        consts = {}
        for name, shape, dtype in (("lower_bounds", [P, 2, HG_HEADS], F32), ("hgrn_gain", [P, 1], F32), ("ret_gain", [P, 1], F32),
                                   ("pool_scale", [P, KT], F32), ("conv_w", [P, 6, HT], F32),
                                   ("conv_b", [P, 2, HT], F32), ("subln_gain", [P, 1], F32), ("inv_freq", [P, 1], F32),
                                   ("head_rms", [P, 3, 2 * HG_HEADS * TT], F32)):
            consts[name] = g.tile(name, shape, dtype)
        (g.lower_bounds, g.hgrn_gain, g.ret_gain, g.pool_scale, g.conv_w, g.conv_b, g.subln_gain, g.inv_freq,
         g.head_rms) = consts.values()
        g.load_unit(0)
        g.gain_ready = g.load("norm_gain", g.sp, [(g.norm_gain[:, :, :], dram["norm_gain"])])
        x_loaded = [g.load(f"x{k}", g.sp, [(g.residual[:, k, :], dram["x"][P * k:P * (k + 1), :])]) for k in range(KT)]
        full = lambda t: t[tuple(slice(None) for _ in t.shape)]
        g.load_unit(1)
        consts.update(ident=g.ident, ones=g.ones, window_share=g.window_share)
        del consts["head_rms"]
        for name, t in consts.items():
            g.constants.start(g.sp, full(t), dram[name])
        g.const_ready = (g.constants.sem, g.constants.count)
        g.next_stage = stages[0]
        g.load_unit(2)
        g.split_unit(0)
        g.split_low()
        for k in range(KT):
            g.residual_done(k, x_loaded[k], None)
        g.split_unit(1)
        g.dve.do(lambda e: e.tensor_scalar(g.subln_gain[:, :], g.subln_gain[:, :], 1.0 - LAM_INIT, None, ALU.mult), g.const_ready)
        for i, stage in enumerate(stages):
            g.next_stage = stages[i + 1] if i + 1 < len(stages) else "final"
            if stage in MIXERS:
                MIXERS[stage](g)
            else:
                feed_forward(g, stage)
        assert g.unit_at == len(units)
        final_norm(g)

        block = ctx.enter_context(nc.Block())

        @block.sync
        def _(e):
            g.sp.run(e)

        @block.scalar
        def _(e):
            g.act.run(e)

        @block.vector
        def _(e):
            g.dve.run(e)

        @block.gpsimd
        def _(e):
            g.pool.run(e)

        @block.tensor
        def _(e):
            g.pe.run(e)


def shape_constants():
    p = np.arange(P)
    i = np.arange(T)
    gamma = 1.0 - 2.0 ** (-5.0 - np.arange(HG_HEADS))
    dist = i[None, :] - p[:, None]
    ret = np.where(dist[None] >= 0, gamma[:, None, None] ** np.maximum(dist, 0)[None], 0.0) * P ** -0.5
    mask = np.zeros((P, 7, 64), np.int32)
    for level, s in enumerate((64, 32, 16, 8, 4, 2, 1)):
        for c in range(64):
            start = (c // s) * 2 * s
            mask[start:start + s, level, c] = 1
    slopes = 2.0 ** (-8.0 * np.arange(1, NSA_HEADS + 1) / NSA_HEADS)
    slopes = slopes.astype(np.float32)
    back = (p[:, None] + T - P - i[None, :]).astype(np.float32)
    alibi = np.where(back[:, None, :] >= 0, slopes[None, :, None] * back[:, None, :], np.float32(MASKED))
    c_end = np.arange(NCP) * CMP_STRIDE + CMP_BLOCK - 1
    tok = (P * np.arange(TT)[None, :] + p[:, None]).astype(np.float32)
    far = tok[:, :, None] - c_end[None, None, :]
    valid = (far >= 0) & (np.arange(NCP) < NC)
    bias = np.where(valid[:, :, None, :], slopes[None, None, :, None] * far[:, :, None, :], MASKED)
    share = np.zeros((P, len(POOL_WINDOWS), 2, PAD), np.float32)
    for n, w in enumerate(POOL_WINDOWS):
        all_shares = 1.0 / (np.clip(i + w - w // 2, 0, T) - np.clip(i - w // 2, 0, T))
        share[:, n, 0, :], share[:, n, 1, :] = all_shares[:PAD], all_shares[T - PAD:]
    inv = np.float32(ROPE_THETA) ** (-np.arange(0, 64, 2, dtype=np.float32) / np.float32(64))
    rot = np.zeros((P, P), np.float32)
    for m in range(P):
        if m % 64 < 32:
            rot[m + 32, m] = -1.0
        else:
            rot[m - 32, m] = 1.0
    f = lambda a: np.ascontiguousarray(a, np.float32)
    return {"ret_decay": f(ret.transpose(1, 0, 2)), "level_mask": mask, "alibi": f(alibi), "cmp_bias": f(bias),
            "cmp_valid": f(valid), "window_share": share, "inv_freq": f(np.tile(inv, 4)[:, None]), "rope_rotate": rot,
            "ident": np.eye(P, dtype=np.float32), "ones": np.ones((P, 1), np.float32)}


def by_feature(v):
    v = np.asarray(v)
    return np.ascontiguousarray(np.moveaxis(v.reshape(v.shape[:-1] + (-1, P)), -1, 0))


def lay_out(inputs, stages):
    a = {k: np.asarray(v) for k, v in inputs.items()}
    units = [unit for stage in stages for unit in stage_units(stage)]
    weights = np.zeros((len(units), P, UNIT), np.float32)
    for n, (name, layer, k0, k, c0, c) in enumerate(units):
        w = a[name][layer if name != "pool_w_2" else 0]
        if name == "pool_w_2":
            w = w[layer]
        pieces = c0 if isinstance(c0, tuple) else ((c0, c),)
        rows = w[k0 * P:(k0 + k) * P]
        block = np.concatenate([rows[:, a:a + n_cols] for a, n_cols in pieces], axis=1).reshape(k, P, c).transpose(1, 0, 2)
        weights[n, :, 0:k * c] = block.reshape(P, k * c)
    w1 = np.zeros((2, P, CMP_BLOCK, P), np.float32)
    w2 = np.zeros((P, 2, P), np.float32)
    pos = np.zeros((P, 2, CMP_BLOCK), np.float32)
    for i, kind in enumerate("kv"):
        m1 = a[f"cmp_w1_{kind}"][0].reshape(CMP_BLOCK, NSA_HD, NSA_HD).transpose(1, 0, 2)
        for grp in range(GROUPS):
            rows = slice(64 * grp, 64 * grp + 64)
            w1[i, rows, :, rows] = m1
            w2[rows, i, rows] = a[f"cmp_w2_{kind}"][0]
            pos[rows, i, :] = a[f"cmp_pos_{kind}"][0].T
    norms = np.stack([a["mix_norm"][0], a["ffn_norm"][0], a["mix_norm"][1], a["ffn_norm"][1],
                      a["mix_norm_2"][0], a["ffn_norm_2"][0], a["mix_norm_2"][1], a["ffn_norm_2"][1], a["final_norm"], a["final_norm_2"]])
    arrays = {
        "x": np.ascontiguousarray(a["x"][0].T), "weights": weights, "norm_gain": by_feature(norms),
        "lower_bounds": by_feature(a["hgrn_lower_bounds"]),
        "hgrn_gain": np.ascontiguousarray(a["hgrn_out_norm"][0][:, None]), "ret_gain": np.ascontiguousarray(a["ret_out_norm"][0][:, None]),
        "pool_scale": by_feature(a["pool_scale_2"][0]),
        "conv_w": by_feature(a["ffn_conv_w_2"].reshape(6, FFN2)), "conv_b": by_feature(a["ffn_conv_b_2"]),
        "subln_gain": np.ascontiguousarray(a["diff_subln_2"][0][:, None]),
        "diff_lam": np.ascontiguousarray(np.broadcast_to(np.stack([a[f"diff_lam_{n}_2"][0] for n in ("q1", "k1", "q2", "k2")]), (P, 4, 64))),
        "positions": np.ascontiguousarray(np.broadcast_to(a["positions_2"], (P, T))),
        "cmp_w1": w1, "cmp_w2": w2, "cmp_pos": pos,
    }
    arrays.update(shape_constants())
    return arrays


def kernel(**inputs):
    import concourse.bacc as _bacc
    from concourse.bass_utils import run_bass_kernel_spmd as _run

    arrays = lay_out(inputs, STAGES)
    nc = _bacc.Bacc("TRN2", target_bir_lowering=False, num_devices=1)
    dram = {name: nc.dram_tensor("in_" + name, a.shape, mybir.dt.from_np(a.dtype), kind="ExternalInput").ap() for name, a in arrays.items()}
    dram["out"] = nc.dram_tensor("out", (D, T), F32, kind="ExternalOutput").ap()
    build(nc, dram, STAGES)
    results = _run(nc, [{"in_" + name: a for name, a in arrays.items()}], core_ids=[0])
    return np.ascontiguousarray(results.results[0]["out"].T)[None]
```
